# Optimizing a Trainium2 kernel written in Bass

```python
import math
import jax, jax.numpy as jnp
from jax import lax
import numpy as np

D_MODEL = 1024
BATCH = 1
SEQ = 512
DEPTH = 2

N_EVEN = (DEPTH + 1) // 2
N_ODD = DEPTH // 2

LRU_WIDTH = D_MODEL // 2
LRU_BLOCKS = 8
LRU_BLOCK_DIM = LRU_WIDTH // LRU_BLOCKS
LRU_CONV = 4
LRU_C = 8.0

ATT_HEADS = 8
ATT_HEAD_DIM = (D_MODEL // 2) // ATT_HEADS
ATT_WIDTH = ATT_HEADS * ATT_HEAD_DIM
DILATED_PATTERNS = ((128, 1), (512, 4), (2048, 16))
ATT_SPAN = max(w for w, _ in DILATED_PATTERNS)
ROPE_THETA = 500000.0
ROPE_DIM = ATT_HEAD_DIM // 4

S5_WIDTH = D_MODEL // 2
S5_GROUP = 16
S5_GROUPS = S5_WIDTH // S5_GROUP
S5_STATE = 64

GLA_HEADS = 4
GLA_DK = (D_MODEL // 4) // GLA_HEADS
GLA_DV = (D_MODEL // 2) // GLA_HEADS
GLA_LOWRANK = 16
GLA_TAU = 16.0
GLA_CHUNK = 64

D_FF = 3 * D_MODEL
FFN_CONV = 3

EPS = 1e-6
NEG_INF = -1e30

EVEN_COLS = (LRU_WIDTH, LRU_WIDTH, ATT_WIDTH, ATT_WIDTH, ATT_WIDTH)
ODD_COLS = (S5_WIDTH, GLA_HEADS * GLA_DK, GLA_HEADS * GLA_DK,
            GLA_HEADS * GLA_DV, GLA_HEADS * GLA_DV, GLA_LOWRANK)

kernel_name = "hybrid_lru_dilated_s5_gla_block"

def split_cols(t, widths):
    idx = [int(i) for i in np.cumsum(widths)[:-1]]
    return jnp.split(t, idx, axis=-1)

def rmsnorm(x, g):
    xf = x.astype(jnp.float32)
    y = xf * lax.rsqrt(jnp.mean(xf * xf, axis=-1, keepdims=True) + EPS)
    return y.astype(x.dtype) * g

def causal_dwconv(x, w, b):
    K = w.shape[0]
    S = x.shape[1]
    xp = jnp.pad(x, ((0, 0), (K - 1, 0), (0, 0)))
    return sum(xp[:, j:j + S] * w[j] for j in range(K)) + b

def rope_tables(S):
    pos = jnp.arange(S, dtype=jnp.float32)
    inv = ROPE_THETA ** (-jnp.arange(0, ROPE_DIM, 2, dtype=jnp.float32) / ROPE_DIM)
    ang = pos[:, None] * inv[None, :]
    return jnp.cos(ang), jnp.sin(ang)

def apply_partial_rope(x, cos, sin):
    half = ROPE_DIM // 2
    c = cos[None, :, None, :].astype(x.dtype)
    s = sin[None, :, None, :].astype(x.dtype)
    x1, x2, rest = x[..., :half], x[..., half:ROPE_DIM], x[..., ROPE_DIM:]
    return jnp.concatenate([x1 * c - x2 * s, x2 * c + x1 * s, rest], axis=-1)

def _linear_combine(left, right):
    a1, b1 = left
    a2, b2 = right
    return a1 * a2, a2 * b1 + b2

def _complex_combine(left, right):
    ar1, ai1, br1, bi1 = left
    ar2, ai2, br2, bi2 = right
    return (ar1 * ar2 - ai1 * ai2, ar1 * ai2 + ai1 * ar2,
            ar2 * br1 - ai2 * bi1 + br2, ar2 * bi1 + ai2 * br1 + bi2)

def rg_lru(x, ga_w, ga_b, gx_w, gx_b, lam):
    B, S, W = x.shape
    xb = x.reshape(B, S, LRU_BLOCKS, LRU_BLOCK_DIM)
    r = jax.nn.sigmoid(jnp.einsum('bshi,hij->bshj', xb, ga_w).reshape(B, S, W) + ga_b)
    i = jax.nn.sigmoid(jnp.einsum('bshi,hij->bshj', xb, gx_w).reshape(B, S, W) + gx_b)
    log_a = (LRU_C * r.astype(jnp.float32)) * jax.nn.log_sigmoid(lam.astype(jnp.float32))
    a = jnp.exp(log_a)
    b = jnp.sqrt(-jnp.expm1(2.0 * log_a)) * (i * x).astype(jnp.float32)
    _, h = lax.associative_scan(_linear_combine, (a, b), axis=1)
    return h.astype(x.dtype)

def _dilated_pattern(q, k, v, dil, n_back):
    B, Sp, H, hd = q.shape
    L = Sp // dil
    nb = L // n_back
    n = n_back

    def to_sub(t):
        return t.reshape(B, L, dil, H, hd).transpose(0, 2, 1, 3, 4).reshape(B, dil, nb, n, H, hd)

    qs, ks, vs = to_sub(q), to_sub(k), to_sub(v)
    pad = ((0, 0), (0, 0), (1, 0), (0, 0), (0, 0), (0, 0))
    kb = jnp.concatenate([jnp.pad(ks, pad)[:, :, :-1], ks], axis=3)
    vb = jnp.concatenate([jnp.pad(vs, pad)[:, :, :-1], vs], axis=3)
    scores = jnp.einsum('brnqhd,brnkhd->brnhqk', qs, kb).astype(jnp.float32) * (hd ** -0.5)
    qi = jnp.arange(n)[:, None]
    ki = jnp.arange(2 * n)[None, :]
    dist = n + qi - ki
    band = (dist >= 0) & (dist <= n_back)
    valid = (jnp.arange(nb)[:, None, None] > 0) | (ki[None] >= n)
    mask = (band[None] & valid)[None, None, :, None, :, :]
    scores = jnp.where(mask, scores, NEG_INF)
    lse = jax.nn.logsumexp(scores, axis=-1)
    p = jnp.exp(scores - lse[..., None])
    out = jnp.einsum('brnhqk,brnkhd->brnqhd', p.astype(vb.dtype), vb)
    out = out.reshape(B, dil, L, H, hd).transpose(0, 2, 1, 3, 4).reshape(B, Sp, H, hd)
    lse = lse.transpose(0, 1, 2, 4, 3).reshape(B, dil, L, H).transpose(0, 2, 1, 3).reshape(B, Sp, H)
    return out, lse

def dilated_attention(q, k, v):
    B, S, H, hd = q.shape
    pad = (-S) % ATT_SPAN
    padw = ((0, 0), (0, pad), (0, 0), (0, 0))
    qp, kp, vp = jnp.pad(q, padw), jnp.pad(k, padw), jnp.pad(v, padw)
    outs, lses = [], []
    for window, dil in DILATED_PATTERNS:
        o, l = _dilated_pattern(qp, kp, vp, dil, window // dil)
        outs.append(o.astype(jnp.float32))
        lses.append(l)
    w = jax.nn.softmax(jnp.stack(lses, axis=0), axis=0)
    o = jnp.sum(w[..., None] * jnp.stack(outs, axis=0), axis=0)
    return o[:, :S].astype(q.dtype)

def s5(u, lam_re, lam_im, b_re, b_im, c_re, c_im, d, log_step):
    f32 = jnp.float32
    B, S, W = u.shape
    ug = u.astype(f32).reshape(B, S, S5_GROUPS, S5_GROUP)
    step = jnp.exp(log_step.astype(f32))[:, None]
    lr, li = lam_re.astype(f32), lam_im.astype(f32)
    mag = jnp.exp(lr * step)
    ar, ai = mag * jnp.cos(li * step), mag * jnp.sin(li * step)
    den = lr * lr + li * li
    cr = ((ar - 1.0) * lr + ai * li) / den
    ci = (ai * lr - (ar - 1.0) * li) / den
    bbr = cr[..., None] * b_re - ci[..., None] * b_im
    bbi = cr[..., None] * b_im + ci[..., None] * b_re
    bur = jnp.einsum('bsgp,gnp->bsgn', ug, bbr)
    bui = jnp.einsum('bsgp,gnp->bsgn', ug, bbi)
    shp = bur.shape
    _, _, xr, xi = lax.associative_scan(
        _complex_combine,
        (jnp.broadcast_to(ar, shp), jnp.broadcast_to(ai, shp), bur, bui), axis=1)
    y = jnp.einsum('bsgn,gpn->bsgp', xr, c_re) - jnp.einsum('bsgn,gpn->bsgp', xi, c_im)
    return (y.reshape(B, S, W) + d * u.astype(f32)).astype(u.dtype)

def gla(q, k, v, gk_lr, gk_w, gk_b, g, norm):
    f32 = jnp.float32
    B, S, H, _ = q.shape
    C = GLA_CHUNK
    nc = S // C
    log_a = jax.nn.log_sigmoid((gk_lr @ gk_w + gk_b).astype(f32)) / GLA_TAU

    def chunks(t, dim):
        return t.astype(f32).reshape(B, nc, C, H, dim).transpose(0, 3, 1, 2, 4)

    qc = chunks(q, GLA_DK) * (GLA_DK ** -0.5)
    kc = chunks(k, GLA_DK)
    vc = chunks(v, GLA_DV)
    bc = jnp.cumsum(chunks(log_a, GLA_DK), axis=3)
    b_last = bc[:, :, :, -1:, :]
    q_dec = qc * jnp.exp(bc)
    k_inv = kc * jnp.exp(-bc)
    causal = jnp.tril(jnp.ones((C, C), dtype=bool))
    att = jnp.where(causal, jnp.einsum('bhncd,bhnjd->bhncj', q_dec, k_inv), 0.0)
    o_intra = jnp.einsum('bhncj,bhnje->bhnce', att, vc)
    kv = jnp.einsum('bhncd,bhnce->nbhde', kc * jnp.exp(b_last - bc), vc)
    decay = jnp.exp(b_last[:, :, :, 0, :]).transpose(2, 0, 1, 3)

    def step(state, inp):
        dec, kv_c = inp
        return dec[..., None] * state + kv_c, state

    _, s_prev = lax.scan(step, jnp.zeros((B, H, GLA_DK, GLA_DV), f32), (decay, kv))
    o_inter = jnp.einsum('bhncd,nbhde->bhnce', q_dec, s_prev)
    o = (o_intra + o_inter).transpose(0, 2, 3, 1, 4).reshape(B, S, H, GLA_DV)
    o = rmsnorm(o, norm).reshape(B, S, H * GLA_DV).astype(g.dtype)
    return o * jax.nn.silu(g)

def even_layer(x, norm, w_in, conv_w, conv_b, ga_w, ga_b, gx_w, gx_b, lam, q_norm, k_norm, w_out, cos, sin):
    B, S, _ = x.shape
    h = rmsnorm(x, norm)
    xl, gl, q, k, v = split_cols(h @ w_in, EVEN_COLS)
    xl = causal_dwconv(xl, conv_w, conv_b)
    y_lru = rg_lru(xl, ga_w, ga_b, gx_w, gx_b, lam) * jax.nn.gelu(gl)
    q = apply_partial_rope(rmsnorm(q.reshape(B, S, ATT_HEADS, ATT_HEAD_DIM), q_norm), cos, sin)
    k = apply_partial_rope(rmsnorm(k.reshape(B, S, ATT_HEADS, ATT_HEAD_DIM), k_norm), cos, sin)
    v = v.reshape(B, S, ATT_HEADS, ATT_HEAD_DIM)
    y_att = dilated_attention(q, k, v).reshape(B, S, ATT_WIDTH)
    return x + jnp.concatenate([y_lru, y_att], axis=-1) @ w_out

def odd_layer(x, norm, w_in, lam_re, lam_im, b_re, b_im, c_re, c_im, d, log_step,
              glu_w, glu_b, gk_w, gk_b, gla_norm, w_out):
    B, S, _ = x.shape
    h = rmsnorm(x, norm)
    u, q, k, v, g, gk = split_cols(h @ w_in, ODD_COLS)
    ys = jax.nn.gelu(s5(u, lam_re, lam_im, b_re, b_im, c_re, c_im, d, log_step))
    y_s5 = ys * jax.nn.sigmoid(ys @ glu_w + glu_b)
    y_gla = gla(q.reshape(B, S, GLA_HEADS, GLA_DK), k.reshape(B, S, GLA_HEADS, GLA_DK),
                v.reshape(B, S, GLA_HEADS, GLA_DV), gk, gk_w, gk_b, g, gla_norm)
    return x + jnp.concatenate([y_s5, y_gla], axis=-1) @ w_out

def conv_ffn(x, norm, w_in, conv_w, conv_b, w_out):
    h = rmsnorm(x, norm)
    a, lin = jnp.split(h @ w_in, 2, axis=-1)
    return x + (jax.nn.gelu(causal_dwconv(a, conv_w, conv_b)) * lin) @ w_out

def setup_inputs(seed: int = 0) -> dict:
    key = jax.random.key(seed)
    keys = iter(jax.random.split(key, 64))
    f32 = jnp.float32

    def nrm(shape, scale):
        return jax.random.normal(next(keys), shape, f32) * scale

    def gain(shape):
        return 1.0 + nrm(shape, 0.02)

    NE, NO = N_EVEN, N_ODD
    inp = {}
    inp['x'] = nrm((BATCH, SEQ, D_MODEL), 1.0)
    inp['e_norm'] = gain((NE, D_MODEL))
    inp['e_w_in'] = nrm((NE, D_MODEL, sum(EVEN_COLS)), D_MODEL ** -0.5)
    inp['e_conv_w'] = nrm((NE, LRU_CONV, LRU_WIDTH), LRU_CONV ** -0.5)
    inp['e_conv_b'] = nrm((NE, LRU_WIDTH), 0.01)
    inp['e_gate_a_w'] = nrm((NE, LRU_BLOCKS, LRU_BLOCK_DIM, LRU_BLOCK_DIM), LRU_BLOCK_DIM ** -0.5)
    inp['e_gate_a_b'] = nrm((NE, LRU_WIDTH), 0.01)
    inp['e_gate_x_w'] = nrm((NE, LRU_BLOCKS, LRU_BLOCK_DIM, LRU_BLOCK_DIM), LRU_BLOCK_DIM ** -0.5)
    inp['e_gate_x_b'] = nrm((NE, LRU_WIDTH), 0.01)
    a_c = jax.random.uniform(next(keys), (NE, LRU_WIDTH), f32, 0.9, 0.999)
    p = a_c ** (1.0 / LRU_C)
    inp['e_lambda'] = jnp.log(p) - jnp.log1p(-p)
    inp['e_q_norm'] = gain((NE, ATT_HEAD_DIM))
    inp['e_k_norm'] = gain((NE, ATT_HEAD_DIM))
    inp['e_w_out'] = nrm((NE, LRU_WIDTH + ATT_WIDTH, D_MODEL), (LRU_WIDTH + ATT_WIDTH) ** -0.5)
    inp['o_norm'] = gain((NO, D_MODEL))
    inp['o_w_in'] = nrm((NO, D_MODEL, sum(ODD_COLS)), D_MODEL ** -0.5)
    inp['o_lambda_re'] = -0.5 + nrm((NO, S5_GROUPS, S5_STATE), 0.01)
    inp['o_lambda_im'] = (jnp.pi * jnp.arange(S5_STATE, dtype=f32))[None, None, :] + nrm((NO, S5_GROUPS, S5_STATE), 0.01)
    inp['o_b_re'] = nrm((NO, S5_GROUPS, S5_STATE, S5_GROUP), (2.0 * S5_GROUP) ** -0.5)
    inp['o_b_im'] = nrm((NO, S5_GROUPS, S5_STATE, S5_GROUP), (2.0 * S5_GROUP) ** -0.5)
    inp['o_c_re'] = nrm((NO, S5_GROUPS, S5_GROUP, S5_STATE), 0.5 ** 0.5)
    inp['o_c_im'] = nrm((NO, S5_GROUPS, S5_GROUP, S5_STATE), 0.5 ** 0.5)
    inp['o_d'] = nrm((NO, S5_WIDTH), 1.0)
    inp['o_log_step'] = jax.random.uniform(next(keys), (NO, S5_GROUPS), f32, math.log(0.001), math.log(0.1))
    inp['o_glu_w'] = nrm((NO, S5_WIDTH, S5_WIDTH), S5_WIDTH ** -0.5)
    inp['o_glu_b'] = nrm((NO, S5_WIDTH), 0.01)
    inp['o_gk_w'] = nrm((NO, GLA_LOWRANK, GLA_HEADS * GLA_DK), GLA_LOWRANK ** -0.5)
    inp['o_gk_b'] = nrm((NO, GLA_HEADS * GLA_DK), 0.01)
    inp['o_gla_norm'] = gain((NO, GLA_DV))
    inp['o_w_out'] = nrm((NO, S5_WIDTH + GLA_HEADS * GLA_DV, D_MODEL), (S5_WIDTH + GLA_HEADS * GLA_DV) ** -0.5)
    inp['f_norm'] = gain((DEPTH, D_MODEL))
    inp['f_w_in'] = nrm((DEPTH, D_MODEL, 2 * D_FF), D_MODEL ** -0.5)
    inp['f_conv_w'] = nrm((DEPTH, FFN_CONV, D_FF), FFN_CONV ** -0.5)
    inp['f_conv_b'] = nrm((DEPTH, D_FF), 0.01)
    inp['f_w_out'] = nrm((DEPTH, D_FF, D_MODEL), D_FF ** -0.5)
    return inp

def reference(x,
              e_norm, e_w_in, e_conv_w, e_conv_b, e_gate_a_w, e_gate_a_b, e_gate_x_w, e_gate_x_b,
              e_lambda, e_q_norm, e_k_norm, e_w_out,
              o_norm, o_w_in, o_lambda_re, o_lambda_im, o_b_re, o_b_im, o_c_re, o_c_im, o_d,
              o_log_step, o_glu_w, o_glu_b, o_gk_w, o_gk_b, o_gla_norm, o_w_out,
              f_norm, f_w_in, f_conv_w, f_conv_b, f_w_out):
    cos, sin = rope_tables(x.shape[1])
    for layer in range(DEPTH):
        i = layer // 2
        if layer % 2 == 0:
            x = even_layer(x, e_norm[i], e_w_in[i], e_conv_w[i], e_conv_b[i], e_gate_a_w[i], e_gate_a_b[i],
                           e_gate_x_w[i], e_gate_x_b[i], e_lambda[i], e_q_norm[i], e_k_norm[i], e_w_out[i],
                           cos, sin)
        else:
            x = odd_layer(x, o_norm[i], o_w_in[i], o_lambda_re[i], o_lambda_im[i], o_b_re[i], o_b_im[i],
                          o_c_re[i], o_c_im[i], o_d[i], o_log_step[i], o_glu_w[i], o_glu_b[i],
                          o_gk_w[i], o_gk_b[i], o_gla_norm[i], o_w_out[i])
        x = conv_ffn(x, f_norm[layer], f_w_in[layer], f_conv_w[layer], f_conv_b[layer], f_w_out[layer])
    return x


_drawn_inputs = setup_inputs


def setup_inputs(seed=0):
    import zlib

    import numpy as np

    out = dict(_drawn_inputs(seed))
    spreads = {}
    factors = {'e_norm': 4.42,
     'e_gate_a_b': 8.0,
     'e_gate_x_b': 8.0,
     'e_q_norm': 8.0,
     'e_k_norm': 8.0,
     'o_norm': 3.594,
     'o_lambda_re': 200.0,
     'o_glu_b': 200.0,
     'o_gk_b': 24.341,
     'o_gla_norm': 103.422,
     'f_conv_b': 33.348,
     'o_lambda_im': 31.664,
     'o_b_re': 41.624,
     'o_b_im': 41.584,
     'o_c_re': 42.6,
     'o_c_im': 43.072,
     'o_log_step': 39.904,
     'f_norm': 8.0,
     'o_d': 3.622,
     'o_glu_w': 5.503}
    for name, (base, spread) in spreads.items():
        noise = np.random.default_rng([zlib.crc32(name.encode()), seed]).standard_normal(out[name].shape)
        drawn = base * np.exp(spread * noise) if base else spread * noise
        out[name] = __import__('jax').numpy.asarray(drawn.astype(out[name].dtype))
    for name, factor in factors.items():
        out[name] = (out[name] * factor).astype(out[name].dtype)
    return out
```

```python
from contextlib import ExitStack

import numpy as np

import concourse.bass as bass
from concourse import mybir

ALU = mybir.AluOpType
ACT = mybir.ActivationFunctionType
AX_X = mybir.AxisListType.X
F32 = mybir.dt.float32
F32R = mybir.dt.float32r

P = 128
D = 1024
S = 512
KT = D // P
HALF = D // 2
HT = HALF // P
FF = 3 * D
FT = FF // P
TT = S // P
EPS = 1e-6
HEADS, HD = 8, 64
ROPE = 8
PATTERNS = ((128, 1), (512, 4), (2048, 16))
BACK = 128
NEVER = -1e30
ATT_STEPS = HEADS // 2 * TT
QK_STEPS = 2 * TT + 6
ATANH = [1.0 / n for n in range(1, 16, 2)]
LAM_ABS = 2

CH, PAIRS, GP, ST = 8, 16, 16, 64
CHUNKS = S // CH
POWERS = CH + 1
ANGLES = POWERS + CHUNKS
ROUND = 1.5 * 2 ** 23
ROUND12 = 1.5 * 2 ** 11
TWO_PI = 6.2831850
PI_PARTS = (6.28125, 0.0019350051879882812, 3.0200665743e-07)
S5_STORES = 5 + CH
S5_COLS = 3 * PAIRS + 4 * PAIRS * GP
MAG_STEP, TURN_STEPS, PHASE_STEPS = 2, 18, 20
BMAT_STEPS, CMAT_STEPS = 28, 34
S5_STEPS = 17

GH, DV, GC = 4, 128, 64
GN = S // GC
LAM_STEPS = LAM_ABS + 5 + 2 * (len(ATANH) - 2) + 4

UNIT = 8 * P
E_Q, E_K, E_V, E_X, E_G, E_O = 0, 4, 8, 12, 16, 20
FIRST_MLP = 28
MLP_UNITS = 2 * FT + 3 * KT
O_U = FIRST_MLP + MLP_UNITS
O_GK, O_Q, O_K, O_V, O_G, O_GLU, O_O = O_U + 4, O_U + 5, O_U + 7, O_U + 9, O_U + 13, O_U + 17, O_U + 19
SECOND_MLP = O_O + 8
N_UNITS = SECOND_MLP + MLP_UNITS
RAW_SLOTS = 4
SPLIT_SLOTS = 2

_COLUMNS = [("norm", 4 * KT), ("mlp_w", 2 * 3 * FT), ("mlp_b", 2 * FT),
            ("lru_w", 4 * HT), ("lru_b", HT), ("gate_a_b", HT), ("gate_x_b", HT), ("lambda", HT),
            ("q_norm", HD), ("k_norm", HD),
            ("s5_d", HT), ("glu_b", HT), ("gk_b", 2), ("gla_norm", DV)]
COL = {}
for _name, _n in _COLUMNS:
    COL[_name] = sum(n for _, n in _COLUMNS[:len(COL)])
N_COLS = sum(n for _, n in _COLUMNS)


_TABLES = [("identity", P), ("mask", S), ("cos", TT * ROPE), ("sin", TT * ROPE), ("angles", ANGLES),
           ("chunk_keep", S), ("chunk_causal", P)]
TAB = {}
for _name, _n in _TABLES:
    TAB[_name] = sum(n for _, n in _TABLES[:len(TAB)])
N_TAB = sum(n for _, n in _TABLES)


def build(nc, parts, xT, units, columns, tables, gates_a, gates_x, s5, gk_w, outT):
    with ExitStack() as ctx:
        def sb(name, shape, dt=F32, where=ctx):
            return where.enter_context(nc.sbuf_tensor(name, shape, dt))

        def sem(name):
            return ctx.enter_context(nc.semaphore(name))

        bank = [ctx.enter_context(nc.psum_tensor(f"bank{b}", [P, 512], F32)) for b in range(8)]

        x = sb("x", [P, KT, S])
        h_hi = sb("h_hi", [P, KT, S], F32R)
        h_lo = sb("h_lo", [P, KT, S], F32R)
        raw = sb("raw", [P, RAW_SLOTS, UNIT])
        w_hi = sb("w_hi", [P, SPLIT_SLOTS, UNIT], F32R)
        w_lo = sb("w_lo", [P, SPLIT_SLOTS, UNIT], F32R)
        cols = sb("cols", [P, N_COLS])
        ones = sb("ones", [P, P])
        eps = sb("eps", [P, 1])
        zero = sb("zero", [P, 1])
        tabs = sb("tabs", [P, N_TAB])
        squares = sb("squares", [P, 2, S])
        rms = sb("rms", [P, S])
        rstd = sb("rstd", [P, S])
        h_full = sb("h_full", [P, 2, S])

        landed = [sem(f"landed{s}") for s in range(RAW_SLOTS)]
        hi_split = sem("hi_split")
        split = sem("split")
        used = sem("used")
        inputs_in = sem("inputs_in")
        consts_set = sem("consts_set")
        x_ready = sem("x_ready")
        squared = sem("squared")
        square_used = sem("square_used")
        rms_ready = sem("rms_ready")
        rstd_ready = sem("rstd_ready")
        normed = sem("normed")
        normed_hi = sem("normed_hi")
        h_ready = sem("h_ready")
        newest_tap = sem("newest_tap")
        middle_tap = sem("middle_tap")
        conv_done = sem("conv_done")
        gelu_done = sem("gelu_done")
        gate_done = sem("gate_done")
        gate_hi_done = sem("gate_hi_done")
        gate_ready = sem("gate_ready")
        out_stored = sem("out_stored")
        s5_in = sem("s5_in")
        s5_exp = sem("s5_exp")
        s5_small = sem("s5_small")
        s5_sin = sem("s5_sin")
        s5_bmat = sem("s5_bmat")
        s5_prep_mm = sem("s5_prep_mm")
        s5_w1_out = sem("s5_w1_out")
        s5_v_out = sem("s5_v_out")
        s5_stored = sem("s5_stored")
        s5_w1_stored0 = sem("s5_w1_stored0")
        s5_w1_stored1 = sem("s5_w1_stored1")
        s5_loaded = sem("s5_loaded")
        s5_w2_loaded = sem("s5_w2_loaded")
        w3_zero = sem("w3_zero")
        w3_in = sem("w3_in")
        gk_in = sem("gk_in")
        u_ready = sem("u_ready")
        u_stored = sem("u_stored")
        u_loaded = sem("u_loaded")
        gk_ready = sem("gk_ready")
        gate_pre = sem("gate_pre")
        gk_abs = sem("gk_abs")
        gk_logs = sem("gk_logs")
        gk_sum = sem("gk_sum")
        gk_exp = sem("gk_exp")
        gk_dec = sem("gk_dec")
        s5_local = sem("s5_local")
        s5_step = sem("s5_step")
        s5_coef = sem("s5_coef")
        s5_half = sem("s5_half")
        s5_rot_in = sem("s5_rot_in")
        s5_gated = sem("s5_gated")
        gk_step = sem("gk_step")
        o_inv = sem("o_inv")
        s5_y_ready = sem("s5_y_ready")
        s5_y_out = sem("s5_y_out")
        y_stored = sem("y_stored")
        y_loaded = sem("y_loaded")
        ys_ready = sem("ys_ready")
        ys_gelu = sem("ys_gelu")
        ys_split = sem("ys_split")
        glu_sig = sem("glu_sig")
        s5_out = sem("s5_out")
        vg_ready = sem("vg_ready")
        sg_ready = sem("sg_ready")
        sg_gain = sem("sg_gain")
        k_turned = sem("k_turned")
        k_end_ready = sem("k_end_ready")
        att_ready = sem("att_ready")
        attT_ready = sem("attT_ready")
        kv_ready = sem("kv_ready")
        state_step = sem("state_step")
        intra_ready = sem("intra_ready")
        inter_ready = sem("inter_ready")
        inter_out = sem("inter_out")
        o_ready = sem("o_ready")
        o_squared = sem("o_squared")
        o_sum = sem("o_sum")
        o_rms = sem("o_rms")
        o_step = sem("o_step")
        o_turned = sem("o_turned")
        gla_y = sem("gla_y")
        even_in = sem("even_in")
        qk_squared = sem("qk_squared")
        qk_sum = sem("qk_sum")
        qk_rms = sem("qk_rms")
        qk_step = sem("qk_step")
        v_ready = sem("v_ready")
        x_newest = sem("x_newest")
        x_conv = sem("x_conv")
        lam_step = sem("lam_step")
        qk_rope = sem("qk_rope")
        qk_inv = sem("qk_inv")
        lam_exp = sem("lam_exp")
        gates_made = sem("gates_made")
        gate_sig = sem("gate_sig")
        lru_exp = sem("lru_exp")
        lru_step = sem("lru_step")
        lru_sqrt = sem("lru_sqrt")
        gg_ready = sem("gg_ready")
        lru_y = sem("lru_y")
        qk_turned = sem("qk_turned")
        qkT_ready = sem("qkT_ready")
        scores_ready = sem("scores_ready")
        masked = sem("masked")
        negmax_ready = sem("negmax_ready")
        exped = sem("exped")
        rinv_ready = sem("rinv_ready")
        probs_ready = sem("probs_ready")
        probs_turned = sem("probs_turned")
        probT_ready = sem("probT_ready")
        pv_done = sem("pv_done")
        att_y = sem("att_y")

        h_full_pairs = h_full[:].rearrange("p a (q c) -> p (a q) c", c=CHUNKS)
        square_pairs = squares[:].rearrange("p a (q c) -> p (a q) c", c=CHUNKS)

        def column(name, i=0):
            c = COL[name] + i
            return cols[:, c:c + 1]

        def table(name):
            return tabs[:, TAB[name]:TAB[name] + dict(_TABLES)[name]]

        even_mem = ExitStack()
        v = sb("v", [P, TT, HALF], F32, even_mem)
        qT = sb("qT", [P, HT, S], F32, even_mem)
        kT = sb("kT", [P, HT, S], F32, even_mem)
        qk = sb("qk", [P, 2, TT, HALF], F32, even_mem)
        qk_var = sb("qk_var", [P, 2, TT * HEADS], F32, even_mem)
        rope_tmp = sb("rope_tmp", [P, 4, TT, HEADS, ROPE], F32, even_mem)
        ga = sb("ga", [P, HT, P], F32, even_mem)
        gx = sb("gx", [P, HT, P], F32, even_mem)
        lam_tmp = sb("lam_tmp", [P, 6, HT], F32, even_mem)
        neg_c = sb("neg_c", [P, HT], F32, even_mem)
        pos_c = sb("pos_c", [P, HT], F32, even_mem)
        row_max = sb("row_max", [P, 2, 2], F32, even_mem)
        neg_max = sb("neg_max", [P, 2, 2], F32, even_mem)
        row_sum = sb("row_sum", [P, 2, 2], F32, even_mem)
        row_inv = sb("row_inv", [P, 2, 2], F32, even_mem)
        lru_mem = ExitStack()
        xc = sb("xc", [P, HT, S], F32, lru_mem)
        rg = sb("rg", [P, HT, S], F32, lru_mem)
        ig = sb("ig", [P, HT, S], F32, lru_mem)
        decay = sb("decay", [P, HT, S], F32, lru_mem)
        coef = sb("coef", [P, HT, S], F32, lru_mem)
        gg = sb("gg", [P, HT, S], F32, lru_mem)
        lru_mem.close()
        att_mem = ExitStack()
        prob = sb("prob", [P, 2, 2, S], F32, att_mem)
        probT = sb("probT", [P, 2, 2, S], F32, att_mem)
        att_mem.close()
        prep_mem = ExitStack()
        s5p = sb("s5p", [P, S5_COLS], F32, prep_mem)
        small = sb("small", [P, 18, PAIRS], F32, prep_mem)
        mag = sb("mag", [P, PAIRS, POWERS], F32, prep_mem)
        pow_r = sb("pow_r", [P, PAIRS, POWERS], F32, prep_mem)
        pow_i = sb("pow_i", [P, PAIRS, POWERS], F32, prep_mem)
        turns = sb("turns", [P, PAIRS, ANGLES], F32, prep_mem)
        rot_s = sb("rot_s", [P, PAIRS, ANGLES], F32, prep_mem)
        rot_c = sb("rot_c", [P, PAIRS, ANGLES], F32, prep_mem)
        bb = sb("bb", [P, 4, PAIRS, GP], F32, prep_mem)
        b_mat = sb("b_mat", [P, 2, PAIRS, CH, GP], F32, prep_mem)
        t_mat = sb("t_mat", [P, 2, PAIRS, CH, GP], F32, prep_mem)
        stage_w1 = v[:, 0:2, :]
        stage_v = v[:, 2, :].rearrange("p (q e c) -> p q e c", q=PAIRS, e=2)
        prep_mem.close()
        even_mem.close()

        odd_mem = ExitStack()
        e_pos = sb("e_pos", [P, 2, S], F32, odd_mem)
        e_neg = sb("e_neg", [P, 2, S], F32, odd_mem)
        logs = sb("logs", [P, 2, S], F32, odd_mem)
        vg = sb("vg", [P, TT, HALF], F32, odd_mem)
        sg = sb("sg", [P, TT, HALF], F32, odd_mem)
        gkw = sb("gkw", [16, 2 * P], F32, odd_mem)
        chunk_decay = sb("chunk_decay", [P, 2, GN], F32, odd_mem)
        gla_var = sb("gla_var", [P, TT * GH], F32, odd_mem)
        m8 = sb("m8", [P, PAIRS], F32, odd_mem)
        s5_mem = ExitStack()
        wst = sb("wst", [P, 2, PAIRS, P], F32, s5_mem)
        w3 = sb("w3", [P, 2 * PAIRS, CH * GP], F32, s5_mem)
        rot = sb("rot", [P, 2, PAIRS, CHUNKS], F32, s5_mem)
        u_in = sb("u_in", [P, 2 * PAIRS, CHUNKS], F32, s5_mem)
        u = sb("u", [P, HT, CH, CHUNKS], F32, s5_mem)
        st = sb("st", [P, 3, PAIRS, CHUNKS], F32, s5_mem)
        s5_mem.close()
        gla_mem = ExitStack()
        attT = sb("attT", [P, GH, S], F32, gla_mem)
        state = sb("state", [P, GN, 2, DV], F32, gla_mem)
        o = sb("o", [P, TT, HALF], F32, gla_mem)
        k_end = sb("k_end", [P, 2, S], F32, gla_mem)
        gla_mem.close()
        odd_mem.close()

        def scratch(name, shape):
            return nc.dram_tensor(name, shape, F32, kind="Internal").ap()

        w1_dram = scratch("w1_dram", [P, 2 * PAIRS * P])
        w2_dram = scratch("w2_dram", [P, 2 * PAIRS * P])
        k_dram = scratch("k_dram", [GP, 2 * PAIRS, 2 * CH - 1, GP])
        rot_dram = scratch("rot_dram", [P, 2, PAIRS, CHUNKS])
        m8_dram = scratch("m8_dram", [P, PAIRS])
        u_dram = scratch("u_dram", [HT, P, CH, CHUNKS])
        y_dram = scratch("y_dram", [2 * PAIRS, GP, CH, CHUNKS])

        mlp_mem = ExitStack()
        g_hi = sb("g_hi", [P, FT, S], F32R, mlp_mem)
        g_lo = sb("g_lo", [P, FT, S], F32R, mlp_mem)
        conv = sb("conv", [P, 2, S], F32, mlp_mem)
        gelu = sb("gelu", [P, 2, S], F32, mlp_mem)
        gate = h_full
        mlp_mem.close()

        order = [p for p in range(4) if p in parts]
        stage_of = {p: n for n, p in enumerate(order)}
        first_unit = {1: FIRST_MLP, 3: SECOND_MLP}
        stream = []
        for p in order:
            lo, hi = [(0, FIRST_MLP), (FIRST_MLP, O_U), (O_U, SECOND_MLP), (SECOND_MLP, N_UNITS)][p]
            stream += range(lo, hi)
        assert stream == list(range(stream[0], stream[-1] + 1))
        first = stream[0]
        total = len(stream)

        block = ctx.enter_context(nc.Block())

        @block.sync
        def _(sp):
            sp.dma_start(cols[:], columns).then_inc(inputs_in, 16)
            sp.dma_start(x[:], xT.rearrange("(k p) t -> p k t", p=P)).then_inc(inputs_in, 16)
            sp.dma_start(tabs[:], tables).then_inc(inputs_in, 16)
            if 2 in order:
                sp.dma_start(s5p[:], s5).then_inc(s5_in, 16)
            if 0 in order:
                sp.dma_start(ga[:], gates_a).then_inc(even_in, 16)
                sp.dma_start(gx[:], gates_x).then_inc(even_in, 16)

            def load(n, slot):
                return sp.dma_start(raw[:, slot, :], units[first + n]).then_inc(landed[slot], 16)

            for n in range(RAW_SLOTS):
                load(n, n)
            rounds = total // RAW_SLOTS
            with sp.Fori(1, rounds) as r:
                for slot in range(RAW_SLOTS):
                    sp.wait_ge(split, (r - 1) * RAW_SLOTS + slot + 1)
                    sp.dma_start(raw[:, slot, :], units[bass.ds(first + r * RAW_SLOTS + slot, 1), :, :]
                                 .rearrange("a p n -> (a p) n")).then_inc(landed[slot], 16)
            for n in range(rounds * RAW_SLOTS, total):
                sp.wait_ge(split, n - RAW_SLOTS + 1)
                load(n, n % RAW_SLOTS)
            sp.wait_ge(x_ready, KT * len(order))
            sp.dma_start(outT.rearrange("(k p) t -> p k t", p=P), x[:]).then_inc(out_stored, 16)
            sp.wait_ge(out_stored, 16)

        @block.gpsimd
        def _(pool):
            pool.memset(ones[:], 1.0).then_inc(consts_set, 1)
            pool.memset(eps[:], EPS).then_inc(consts_set, 1)
            pool.memset(zero[:], 0.0).then_inc(consts_set, 1)
            pool.wait_ge(consts_set, 3)

            def halves(slot, half, done):
                pool.tensor_tensor(w_hi[:, half, :], raw[:, slot, :], zero[:, 0:1].to_broadcast([P, UNIT]), ALU.add).then_inc(hi_split, 1)
                pool.wait_ge(hi_split, done)
                pool.tensor_tensor(w_lo[:, half, :], raw[:, slot, :], w_hi[:, half, :].bitcast(F32),
                                   ALU.subtract).then_inc(split, 1)

            def one(n):
                pool.wait_ge(landed[n % RAW_SLOTS], 16 * (n // RAW_SLOTS + 1))
                if n >= SPLIT_SLOTS:
                    pool.wait_ge(used, n - SPLIT_SLOTS + 1)
                halves(n % RAW_SLOTS, n % SPLIT_SLOTS, n + 1)

            for n in range(RAW_SLOTS):
                one(n)
            rounds = total // RAW_SLOTS
            with pool.Fori(1, rounds) as r:
                for slot in range(RAW_SLOTS):
                    pool.wait_ge(landed[slot], r * 16 + 16)
                    pool.wait_ge(used, r * RAW_SLOTS + (slot - SPLIT_SLOTS + 1))
                    halves(slot, slot % SPLIT_SLOTS, r * RAW_SLOTS + (slot + 1))
            for n in range(rounds * RAW_SLOTS, total):
                one(n)

        @block.tensor
        def _(pe):
            def sum_squares(stage):
                for k in range(KT):
                    pe.wait_ge(squared, KT * stage + k + 1)
                    mm = pe.matmul(bank[6][:], ones[:], squares[:, k % 2, :], start=(k == 0), stop=(k == KT - 1))
                    mm.then_inc(square_used, 1)

            def product(out, slot, b, w_at, mov_hi, mov_lo, start, stop):
                hi, lo = w_hi[:, slot, w_at], w_lo[:, slot, w_at]
                pe.matmul(out, hi, mov_hi, start=start, stop=False)
                pe.matmul(out, hi, mov_lo, start=False, stop=False)
                return pe.matmul(out, lo, mov_hi, start=False, stop=stop)

            def w_block(b):
                return slice(b * P, (b + 1) * P)

            def mlp(stage, n0):
                base = FT * (stage // 2 if len(order) == 4 else 0)

                def up(i, u, wait_h):
                    for which, free in enumerate((conv_done, gate_done)):
                        slot = (n0 + which) % SPLIT_SLOTS
                        pe.wait_ge(split, i * 4 + (n0 + 2 * u + which + 1))
                        if not wait_h:
                            pe.wait_ge(free, i * 2 + (base + u - 1))
                        for k in range(KT):
                            if wait_h and u == 0 and which == 0:
                                pe.wait_ge(h_ready, KT * stage + k + 1)
                            mm = product(bank[2 * which + u][:], slot, k, w_block(k), h_hi[:, k, :], h_lo[:, k, :],
                                         k == 0, k == KT - 1)
                        mm.then_inc(used, 1)

                for u in range(2):
                    up(0, u, True)
                with pe.Fori(1, FT // 2) as i:
                    for u in range(2):
                        up(i, u, False)
                n1 = n0 + 2 * FT
                project(stage, n1, 3, g_hi, g_lo, lambda k: pe.wait_ge(gate_ready, base + k + 1))

            def project(stage, n1, per_tile, y_hi, y_lo, wait_y):
                def tile(i, u, first_time):
                    for part in range(per_tile):
                        n = n1 + per_tile * u + part
                        pe.wait_ge(split, i * (2 * per_tile) + (n + 1))
                        if part == 0 and not first_time:
                            pe.wait_ge(x_ready, i * 2 + (KT * stage + u - 1))
                        for b in range(8):
                            k = part * 8 + b
                            if first_time and u == 0:
                                wait_y(k)
                            mm = product(bank[4 + u][:], n % SPLIT_SLOTS, b, w_block(b), y_hi[:, k, :], y_lo[:, k, :],
                                         k == 0, k == 8 * per_tile - 1)
                        mm.then_inc(used, 1)

                for u in range(2):
                    tile(0, u, True)
                with pe.Fori(1, KT // 2) as i:
                    for u in range(2):
                        tile(i, u, False)

            def rows_unit(n, part, banks, stage, first_time):
                pe.wait_ge(split, n + 1)
                slot = n % SPLIT_SLOTS
                for b in range(2):
                    k = 2 * part + b
                    if first_time:
                        pe.wait_ge(h_ready, KT * stage + k + 1)
                    cols_ = slice(b * 512, (b + 1) * 512)
                    for t in range(TT):
                        out, at = bank[banks + t][:], slice(t * P, (t + 1) * P)
                        pe.matmul(out, h_hi[:, k, at], w_hi[:, slot, cols_], start=(k == 0), stop=False)
                        pe.matmul(out, h_hi[:, k, at], w_lo[:, slot, cols_], start=False, stop=False)
                        mm = pe.matmul(out, h_lo[:, k, at], w_hi[:, slot, cols_], start=False, stop=(k == KT - 1))
                mm.then_inc(used, 1)

            def tile_unit(n, b_out, stage, first_time=False):
                pe.wait_ge(split, n + 1)
                for k in range(KT):
                    if first_time:
                        pe.wait_ge(h_ready, KT * stage + k + 1)
                    mm = product(bank[b_out][:], n % SPLIT_SLOTS, k, w_block(k), h_hi[:, k, :], h_lo[:, k, :],
                                 k == 0, k == KT - 1)
                mm.then_inc(used, 1)

            def s5_prepare():
                pe.wait_ge(rms_ready, 1)
                pe.wait_ge(s5_bmat, BMAT_STEPS)
                nci = bb[:, 3]
                cr = s5p[:, 3 * PAIRS + 2 * PAIRS * GP:3 * PAIRS + 3 * PAIRS * GP].rearrange("p (q c) -> p q c", c=GP)
                for q in range(PAIRS):
                    for e in range(2):
                        rows = slice(64 * e, 64 * e + 64)
                        out = bank[4 + e][:, q * GP:(q + 1) * GP]
                        pe.matmul(out, b_mat[rows, 0, q].rearrange("p l c -> p (l c)"), cr[rows, q], start=True, stop=False)
                        mm = pe.matmul(out, b_mat[rows, 1, q].rearrange("p l c -> p (l c)"), nci[rows, q], start=False, stop=True)
                mm.then_inc(s5_prep_mm, 1)
                for n in range(8):
                    if n >= 2:
                        pe.wait_ge(s5_w1_out, n - 1)
                    for i in range(4):
                        q = 4 * n + i
                        mm = pe.transpose(bank[6 + n % 2][:, i * P:(i + 1) * P],
                                          b_mat[:, q // PAIRS, q % PAIRS].rearrange("p l c -> p (l c)"), table("identity"))
                    mm.then_inc(s5_prep_mm, 1)
                pe.wait_ge(s5_v_out, 2)
                pe.wait_ge(s5_w1_out, 8)

            def odd_mixer(stage):
                n0 = O_U - first
                if 0 not in order:
                    s5_prepare()
                for m in range(HT):
                    tile_unit(n0 + m, m, stage, True)
                tile_unit(O_GK - first, 4, stage)
                pe.wait_ge(gk_ready, 1)
                pe.wait_ge(gk_in, 16)
                for i in range(2):
                    pe.matmul(bank[5 + i][:], gkw[:, i * P:(i + 1) * P], squares[0:16, 0, :], start=True,
                              stop=True).then_inc(gate_pre, 1)
                tile_unit(O_Q - first, 7, stage)
                tile_unit(O_Q - first + 1, 4, stage)
                pe.wait_ge(gk_logs, 2)
                tile_unit(O_K - first, 5, stage)
                tile_unit(O_K - first + 1, 6, stage)

                pe.wait_ge(u_ready, HT)
                pe.wait_ge(u_loaded, 16 * CH)
                pe.wait_ge(s5_loaded, 16)
                for ri in range(2):
                    for q in range(PAIRS):
                        for e in range(2):
                            mm = pe.matmul(bank[2 * ri + q // 8][64 * e:64 * e + 64, q % 8 * CHUNKS:(q % 8 + 1) * CHUNKS],
                                           wst[:, ri, q, 64 * e:64 * e + 64], u_in[:, 2 * q + e, :], start=True, stop=True)
                mm.then_inc(s5_local, 1)

                pe.wait_ge(gk_dec, 4)
                for part in range(4):
                    rows_unit(O_V - first + part, part, 4, stage, False)
                pe.wait_ge(s5_step, 4)
                for part in range(4):
                    rows_unit(O_G - first + part, part, 0, stage, False)

                pe.wait_ge(vg_ready, TT)
                pe.wait_ge(w3_in, 16 * CH)
                pe.wait_ge(s5_w2_loaded, 16)
                pe.wait_ge(s5_step, S5_STEPS)
                for e in range(2):
                    for half in range(2):
                        for q in range(8 * half, 8 * half + 8):
                            out = bank[4 + 2 * e + half][:, q % 8 * CHUNKS:(q % 8 + 1) * CHUNKS]
                            rows = slice(64 * e, 64 * e + 64)
                            pe.matmul(out, w3[:, 2 * q + e, :], u_in[:, 2 * q + e, :], start=True, stop=False)
                            pe.matmul(out, wst[rows, 0, q, :], st[rows, 2, q, :], start=False, stop=False)
                            mm = pe.matmul(out, wst[rows, 1, q, :], h_full_pairs[rows, q, :], start=False, stop=True)
                        mm.then_inc(s5_y_ready, 1)

                pe.wait_ge(sg_ready, TT)
                pe.wait_ge(gk_dec, 6)
                for i in range(2):
                    for t in range(TT):
                        mm = pe.transpose(bank[i][:, t * P:(t + 1) * P], logs[:, i, t * P:(t + 1) * P], table("identity"))
                    mm.then_inc(k_turned, 1)
                for h in range(GH):
                    b = (2, 3, 0, 1)[h]
                    if h >= 2:
                        pe.wait_ge(k_end_ready, 2)
                    rows = slice(64 * (h % 2), 64 * (h % 2) + 64)
                    for t in range(TT):
                        at = slice(t * P, (t + 1) * P)
                        mm = pe.matmul(bank[b][:, at], e_neg[rows, h // 2, at], e_pos[rows, h // 2, at], start=True, stop=True)
                    mm.then_inc(att_ready, 1)
                pe.wait_ge(s5_y_out, 4)
                for n in range(GN - 1):
                    rows = slice(64 * (n % 2), 64 * (n % 2) + 64)
                    for h in range(GH):
                        col = (n // 2 % 2) * 256 + (h // 2) * DV
                        mm = pe.matmul(bank[4 + 2 * (n % 2) + n // 4][64 * (h % 2):64 * (h % 2) + 64, col:col + DV],
                                       k_end[rows, h // 2, n // 2 * P + 64 * (h % 2):n // 2 * P + 64 * (h % 2) + 64],
                                       vg[rows, n // 2, h * DV:(h + 1) * DV], start=True, stop=True)
                    mm.then_inc(kv_ready, 1)
                pe.wait_ge(attT_ready, GH)
                for t in range(TT):
                    for h in range(GH):
                        mm = pe.matmul(bank[t][:, h * DV:(h + 1) * DV], attT[:, h, t * P:(t + 1) * P],
                                       vg[:, t, h * DV:(h + 1) * DV], start=True, stop=True)
                    mm.then_inc(intra_ready, 1)
                pe.wait_ge(state_step, 1 + 2 * (GN - 1))
                for t in range(TT):
                    for e in range(2):
                        for n in (2 * t, 2 * t + 1):
                            for i in range(2):
                                rows = slice(64 * e, 64 * e + 64)
                                col = (t % 2) * 256 + i * DV
                                mm = pe.matmul(bank[4 + 2 * e + t // 2][64 * (n % 2):64 * (n % 2) + 64, col:col + DV],
                                               e_pos[rows, i, n * GC:(n + 1) * GC], state[rows, n, i, :],
                                               start=True, stop=True)
                    mm.then_inc(inter_ready, 1)

                pe.wait_ge(o_ready, TT)
                pe.wait_ge(ys_split, 2)
                for part in range(2):
                    n = O_GLU - first + part
                    pe.wait_ge(split, n + 1)
                    for b in range(8):
                        m, k = 2 * part + b // HT, b % HT
                        mm = product(bank[m][:], n % SPLIT_SLOTS, b, w_block(b), h_hi[:, k, :], h_lo[:, k, :], k == 0, k == HT - 1)
                    mm.then_inc(used, 1)
                pe.wait_ge(o_step, 2)
                for h in range(GH):
                    for t in range(TT):
                        mm = pe.transpose(bank[4 + h][:, t * P:(t + 1) * P], o[:, t, h * P:(h + 1) * P], table("identity"))
                    mm.then_inc(o_turned, 1)
                pe.wait_ge(gla_y, 2 * GH)
                project(stage, O_O - first, 1, h_hi, h_lo, lambda k: pe.wait_ge(s5_out, 1))

            def even_mixer(stage):
                for part in range(4):
                    rows_unit(E_Q + part, part, 0, stage, True)
                if 2 in order:
                    s5_prepare()
                for part in range(4):
                    rows_unit(E_K + part, part, 4, stage, False)
                pe.wait_ge(qk_step, 4)
                for part in range(4):
                    rows_unit(E_V + part, part, 0, stage, False)
                pe.wait_ge(qk_step, 8)
                for m in range(HT):
                    tile_unit(E_X + m, 4 + m, stage)
                pe.wait_ge(v_ready, TT)
                tile_unit(E_G, 0, stage)
                pe.wait_ge(even_in, 32)
                for m in range(HT):
                    if m == 0:
                        pe.wait_ge(x_conv, 3 * HT)
                    if m >= 2:
                        pe.wait_ge(gate_sig, 2 * m - 2)
                    b = 4 + 2 * (m % 2)
                    pe.matmul(bank[b][:], ga[:, m, :], xc[:, m, :], start=True, stop=True).then_inc(gates_made, 1)
                    pe.matmul(bank[b + 1][:], gx[:, m, :], xc[:, m, :], start=True, stop=True).then_inc(gates_made, 1)
                for m in range(1, HT):
                    tile_unit(E_G + m, m, stage)
                pe.wait_ge(gate_sig, 2 * HT)
                pe.wait_ge(qk_step, QK_STEPS)
                for n in range(2 * HT):
                    which, hp = n // HT, n % HT
                    if n >= 4:
                        pe.wait_ge(qkT_ready, n - 3)
                    for t in range(TT):
                        mm = pe.transpose(bank[4 + n % 4][:, t * P:(t + 1) * P],
                                          qk[:, which, t, hp * P:(hp + 1) * P], table("identity"))
                    mm.then_inc(qk_turned, 1)

                def scores(n):
                    hp, t = divmod(n, TT)
                    if n >= 2:
                        pe.wait_ge(masked, 2 * (n - 1))
                    for e in range(2):
                        rows = slice(64 * e, 64 * e + 64)
                        mm = pe.matmul(bank[2 * e + n % 2][:, 0:(t + 1) * P], qT[rows, hp, t * P:(t + 1) * P],
                                       kT[rows, hp, 0:(t + 1) * P], start=True, stop=True)
                    mm.then_inc(scores_ready, 1)

                def turn(n):
                    t = n % TT
                    pe.wait_ge(probs_ready, 2 * n + 2)
                    if n >= 1:
                        pe.wait_ge(probT_ready, 2 * n)
                    for e in range(2):
                        for j in range(t + 1):
                            mm = pe.transpose(bank[4 + e][:, j * P:(j + 1) * P], prob[:, n % 2, e, j * P:(j + 1) * P],
                                              table("identity"))
                    mm.then_inc(probs_turned, 1)

                def values(n):
                    hp, t = divmod(n, TT)
                    pe.wait_ge(probT_ready, 2 * n + 2)
                    if t == 0 and hp >= 2:
                        pe.wait_ge(att_y, 2 * (hp - 1))
                    for e in range(2):
                        head = 2 * hp + e
                        for j in range(t + 1):
                            mm = pe.matmul(bank[6 + hp % 2][64 * e:64 * e + 64, t * P:(t + 1) * P],
                                           v[:, j, head * HD:(head + 1) * HD], probT[:, n % 2, e, j * P:(j + 1) * P],
                                           start=(j == 0), stop=(j == t))
                    mm.then_inc(pv_done, 1)

                pe.wait_ge(gg_ready, HT)
                pe.wait_ge(qkT_ready, 2 * HT)
                scores(0)
                scores(1)
                for n in range(ATT_STEPS):
                    turn(n)
                    if n + 2 < ATT_STEPS:
                        scores(n + 2)
                    values(n)
                project(stage, E_O, 1, h_hi, h_lo,
                        lambda k: pe.wait_ge(*((lru_y, 1) if k < HT else (att_y, 2 * (k - HT) + 2))))

            pe.wait_ge(consts_set, 3)
            for stage, part in enumerate(order):
                sum_squares(stage)
                if part == 0:
                    even_mixer(stage)
                if part == 2:
                    odd_mixer(stage)
                if part in (1, 3):
                    mlp(stage, first_unit[part] - first)

        @block.scalar
        def _(act):
            def square_tiles(stage):
                for k in range(KT):
                    if stage == 0:
                        if k == 0:
                            act.wait_ge(inputs_in, 48)
                            act.wait_ge(consts_set, 3)
                    else:
                        act.wait_ge(x_ready, KT * (stage - 1) + k + 1)
                    if KT * stage + k >= 2:
                        act.wait_ge(square_used, KT * stage + k - 1)
                    act.activation(squares[:, k % 2, :], x[:, k, :], ACT.Square).then_inc(squared, 1)

            def norm(stage):
                square_tiles(stage)
                act.wait_ge(square_used, KT * (stage + 1))
                act.activation(rms[:], bank[6][:], ACT.Sqrt, bias=eps[:, 0:1], scale=1.0 / D).then_inc(rms_ready, 1)
                for k in range(KT):
                    act.wait_ge(normed, KT * stage + k + 1)
                    act.activation(h_hi[:, k, :], h_full[:, k % 2, :], ACT.Copy).then_inc(normed_hi, 1)

            def mlp(stage, layer, n0):
                base = FT * (stage // 2 if len(order) == 4 else 0)

                def tile(i, u, warm):
                    j = i * 2 + u
                    act.wait_ge(used, i * 4 + (n0 + 2 * u + 1))
                    if warm:
                        act.wait_ge(gelu_done, i * 2 + (base + u - 1))
                    w = COL["mlp_w"] + layer * 3 * FT + 2 * FT
                    b = COL["mlp_b"] + layer * FT
                    act.activation(conv[:, u, :], bank[u][:], ACT.Identity,
                                   bias=cols[:, bass.ds(b + j, 1)], scale=cols[:, bass.ds(w + j, 1)]).then_inc(newest_tap, 1)
                    act.wait_ge(conv_done, i * 2 + (base + u + 1))
                    if warm:
                        act.wait_ge(gate_done, i * 2 + (base + u - 1))
                    act.activation(gelu[:, u, :], conv[:, u, :], ACT.Gelu_apprx_tanh).then_inc(gelu_done, 1)

                for u in range(2):
                    tile(0, u, False)
                with act.Fori(1, FT // 2) as i:
                    for u in range(2):
                        tile(i, u, True)

            def s5_phases():
                act.wait_ge(s5_in, 16)
                act.activation(small[:, 0], s5p[:, 2 * PAIRS:3 * PAIRS], ACT.Exp).then_inc(s5_exp, 1)
                act.wait_ge(s5_small, MAG_STEP)
                act.activation(mag[:], mag[:], ACT.Exp).then_inc(s5_exp, 1)
                act.wait_ge(s5_small, TURN_STEPS)
                act.activation(rot_s[:], turns[:], ACT.Sin, scale=TWO_PI).then_inc(s5_sin, 1)
                act.activation(rot_c[:], turns[:], ACT.Sin, scale=TWO_PI / 2).then_inc(s5_sin, 1)

            def s5_prepare():
                act.wait_ge(s5_small, PHASE_STEPS)
                act.dma_start(rot_dram[:, 0], rot_c[:, :, POWERS:ANGLES]).then_inc(s5_stored, 16)
                act.dma_start(rot_dram[:, 1], rot_s[:, :, POWERS:ANGLES]).then_inc(s5_stored, 16)
                act.wait_ge(s5_exp, 2)
                act.activation(small[:, 16], mag[:, :, CH], ACT.Copy).then_inc(s5_exp, 1)
                act.wait_ge(s5_exp, 3)
                act.dma_start(m8_dram, small[:, 16]).then_inc(s5_stored, 16)
                act.wait_ge(s5_prep_mm, 1)
                for e in range(2):
                    act.activation(stage_v[:, :, e, :], bank[4 + e][:, 0:PAIRS * GP].rearrange("p (q c) -> p q c", c=GP),
                                   ACT.Copy).then_inc(s5_v_out, 1)
                act.wait_ge(s5_v_out, 2)
                for e in range(CH):
                    act.dma_start(k_dram[:, :, CH - 1 + e, :], stage_v[e * GP:(e + 1) * GP].rearrange("p q e c -> p (q e) c"))\
                       .then_inc(s5_stored, 16)
                zeros = GP * (CH - 1)
                act.wait_ge(w3_zero, 1)
                act.dma_start(k_dram.rearrange("p (a b) k c -> (p a) b (k c)", b=4)[:, :, 0:zeros],
                              v[:, 3, 0:4 * zeros].rearrange("p (b n) -> p b n", b=4)).then_inc(s5_stored, 16)
                for n in range(8):
                    act.wait_ge(s5_prep_mm, n + 2)
                    stored = (s5_w1_stored0, s5_w1_stored1)[n % 2]
                    if n >= 2:
                        act.wait_ge(stored, 16 * (n // 2))
                    act.activation(stage_w1[:, n % 2, :], bank[6 + n % 2][:], ACT.Copy).then_inc(s5_w1_out, 1)
                    act.wait_ge(s5_w1_out, n + 1)
                    act.dma_start(w1_dram[:, n * 512:(n + 1) * 512], stage_w1[:, n % 2, :]).then_inc(stored, 16)

            def s5_store_output():
                act.wait_ge(s5_bmat, CMAT_STEPS)
                act.dma_start(w2_dram, b_mat[:].rearrange("p r q l c -> p (r q l c)")).then_inc(s5_stored, 16)

            def odd_mixer(stage):
                if 0 not in order:
                    s5_prepare()
                    s5_store_output()
                act.wait_ge(s5_stored, 16 * S5_STORES)
                act.wait_ge(s5_w1_stored0, 64)
                act.wait_ge(s5_w1_stored1, 64)
                act.dma_start(gkw[:], gk_w).then_inc(gk_in, 16)
                act.dma_start(wst[:].rearrange("p r q n -> p (r q n)"), w1_dram).then_inc(s5_loaded, 16)
                act.dma_start(rot[:], rot_dram).then_inc(s5_rot_in, 16)
                act.dma_start(m8[:], m8_dram).then_inc(s5_rot_in, 16)
                for m in range(HT):
                    act.wait_ge(used, O_U - first + m + 1)
                    act.activation(u[:, m], bank[m][:].rearrange("p (c l) -> p l c", l=CH), ACT.Copy).then_inc(u_ready, 1)
                    act.wait_ge(u_ready, m + 1)
                    act.dma_start(u_dram[m], u[:, m]).then_inc(u_stored, 16)
                act.wait_ge(used, O_GK - first + 1)
                act.activation(squares[0:16, 0, :], bank[4][0:16, :], ACT.Copy).then_inc(gk_ready, 1)
                act.wait_ge(u_stored, 16 * HT)
                ud = u_dram.rearrange("m (g p) l c -> p (m g) l c", p=GP)
                for e in range(CH):
                    act.dma_start(u_in[e * GP:(e + 1) * GP], ud[:, :, CH - 1 - e, :]).then_inc(u_loaded, 16)
                for e in range(CH):
                    act.dma_start(w3[e * GP:(e + 1) * GP], k_dram[:, :, e:e + CH, :].rearrange("p g k c -> p g (k c)"))\
                       .then_inc(w3_in, 16)
                act.wait_ge(gk_logs, 2)
                act.activation(e_pos[:], logs[:], ACT.Abs).then_inc(gk_abs, 1)
                act.wait_ge(gk_abs, 1)
                act.activation(e_pos[:], e_pos[:], ACT.Exp, scale=-1.0).then_inc(gk_abs, 1)
                act.wait_ge(gk_abs, 2)
                act.activation(e_pos[:], e_pos[:], ACT.Ln, bias=ones[:, 0:1]).then_inc(gk_abs, 1)
                act.wait_ge(gk_sum, 3)
                act.activation(e_pos[:], logs[:], ACT.Exp, scale=1.0 / 16).then_inc(gk_exp, 1)
                act.activation(e_neg[:], logs[:], ACT.Exp, scale=-1.0 / 16).then_inc(gk_exp, 1)
                act.wait_ge(s5_local, 1)
                act.dma_start(wst[:].rearrange("p r q n -> p (r q n)"), w2_dram).then_inc(s5_w2_loaded, 16)
                act.wait_ge(used, O_V - first + 4)
                for t in range(TT):
                    act.activation(vg[:, t, :], bank[4 + t][:], ACT.Copy).then_inc(vg_ready, 1)
                act.wait_ge(used, O_G - first + 4)
                for t in range(TT):
                    act.activation(sg[:, t, :], bank[t][:], ACT.Silu).then_inc(sg_ready, 1)
                act.wait_ge(k_turned, 2)
                for i in range(2):
                    act.activation(k_end[:, i, :], bank[i][:], ACT.Copy).then_inc(k_end_ready, 1)
                for e in range(2):
                    for half in range(2):
                        n = 2 * e + half
                        act.wait_ge(s5_y_ready, n + 1)
                        dst = st[:, 0:2].rearrange("p a q c -> p (a q) c")[:, 16 * half + e:16 * half + 16:2, :]
                        act.activation(dst, bank[4 + n][:].rearrange("p (q c) -> p q c", c=CHUNKS), ACT.Copy).then_inc(s5_y_out, 1)
                act.wait_ge(s5_y_out, 4)
                yd = y_dram.rearrange("g p l c -> p g l c")
                for l in range(CH):
                    act.dma_start(yd[:, :, l, :], st[l * GP:(l + 1) * GP, 0:2].rearrange("p a q c -> p (a q) c"))\
                       .then_inc(y_stored, 16)
                act.wait_ge(y_stored, 16 * CH)
                y_in = u_in[:].rearrange("p g c -> p (g c)").rearrange("p (m n) -> p m n", m=HT)
                act.dma_start(y_in, y_dram.rearrange("(m g) p l c -> (g p) m (l c)", m=HT)).then_inc(y_loaded, 16)
                for t in range(TT):
                    act.wait_ge(inter_ready, t // 2 * 2 + 2)
                    for e in range(2):
                        dst = o[:, t, :].rearrange("p (i e d) -> p i e d", i=2, e=2)[:, :, e, :]
                        src = bank[4 + 2 * e + t // 2][:, t % 2 * 256:t % 2 * 256 + 256].rearrange("p (i d) -> p i d", i=2)
                        act.activation(dst, src, ACT.Copy).then_inc(inter_out, 1)
                act.wait_ge(ys_ready, 1)
                act.activation(u_in[:], u_in[:], ACT.Gelu_apprx_tanh).then_inc(ys_gelu, 1)
                for t in range(TT):
                    act.wait_ge(o_ready, t + 1)
                    if t >= 2:
                        act.wait_ge(o_sum, t - 1)
                    act.activation(squares[:, t % 2, :], o[:, t, :], ACT.Square).then_inc(o_squared, 1)
                act.wait_ge(o_sum, TT)
                act.activation(gla_var[:], gla_var[:], ACT.Sqrt, bias=eps[:, 0:1], scale=1.0 / DV).then_inc(o_rms, 1)
                act.wait_ge(used, O_GLU - first + 2)
                sig = st[:, 0:2].rearrange("p a q c -> p (a q c)").rearrange("p (m n) -> p m n", m=HT)
                for m in range(HT):
                    act.activation(sig[:, m], bank[m][:], ACT.Sigmoid, bias=column("glu_b", m)).then_inc(glu_sig, 1)

            def even_mixer(stage):
                if 2 in order:
                    s5_prepare()
                act.wait_ge(lam_step, LAM_ABS)
                act.activation(lam_tmp[:, 0, :], lam_tmp[:, 5, :], ACT.Exp).then_inc(lam_exp, 1)
                for which in range(2):
                    act.wait_ge(used, 4 * which + 4)
                    for t in range(TT):
                        n = TT * which + t
                        if n >= 2:
                            act.wait_ge(qk_sum, n - 1)
                        act.activation(squares[:, n % 2, :], bank[4 * which + t][:], ACT.Square).then_inc(qk_squared, 1)
                    act.wait_ge(qk_sum, TT * (which + 1))
                    act.activation(qk_var[:, which, :], qk_var[:, which, :], ACT.Sqrt, bias=eps[:, 0:1],
                                   scale=1.0 / HD).then_inc(qk_rms, 1)
                if 2 in order:
                    s5_store_output()
                    act.wait_ge(s5_stored, 16 * S5_STORES)
                    act.wait_ge(s5_w1_stored0, 64)
                    act.wait_ge(s5_w1_stored1, 64)
                act.wait_ge(used, 12)
                for t in range(TT):
                    act.activation(v[:, t, :], bank[t][:], ACT.Copy).then_inc(v_ready, 1)
                for m in range(HT):
                    act.wait_ge(used, E_X + m + 1)
                    act.activation(xc[:, m, :], bank[4 + m][:], ACT.Identity, bias=column("lru_b", m),
                                   scale=column("lru_w", 3 * HT + m)).then_inc(x_newest, 1)
                for m in range(HT):
                    b = 4 + 2 * (m % 2)
                    act.wait_ge(gates_made, 2 * m + 1)
                    act.activation(rg[:, m, :], bank[b][:], ACT.Sigmoid, bias=column("gate_a_b", m)).then_inc(gate_sig, 1)
                    act.wait_ge(gates_made, 2 * m + 2)
                    act.activation(ig[:, m, :], bank[b + 1][:], ACT.Sigmoid, bias=column("gate_x_b", m)).then_inc(gate_sig, 1)
                act.wait_ge(gate_sig, 2 * HT)
                act.wait_ge(lam_step, LAM_STEPS)
                for m in range(HT):
                    act.activation(coef[:, m, :], rg[:, m, :], ACT.Tanh, scale=neg_c[:, m:m + 1]).then_inc(lru_exp, 1)
                for m in range(HT):
                    act.activation(decay[:, m, :], rg[:, m, :], ACT.Exp, scale=pos_c[:, m:m + 1]).then_inc(lru_exp, 1)
                act.wait_ge(lru_step, 3)
                act.activation(coef[:], coef[:], ACT.Sqrt, scale=2.0).then_inc(lru_sqrt, 1)
                for m in range(HT):
                    act.wait_ge(used, E_G + m + 1)
                    act.activation(gg[:, m, :], bank[m][:], ACT.Gelu_apprx_tanh).then_inc(gg_ready, 1)
                for n in range(2 * HT):
                    act.wait_ge(qk_turned, n + 1)
                    dst = (qT, kT)[n // HT]
                    act.activation(dst[:, n % HT, :], bank[4 + n % 4][:], ACT.Copy).then_inc(qkT_ready, 1)

                def exps(n):
                    act.wait_ge(negmax_ready, n + 1)
                    w = (n % TT + 1) * P
                    for e in range(2):
                        act.activation(prob[:, n % 2, e, 0:w], prob[:, n % 2, e, 0:w], ACT.Exp,
                                       bias=neg_max[:, n % 2, e:e + 1], scale=HD ** -0.5,
                                       accum_out=row_sum[:, n % 2, e:e + 1]).then_inc(exped, 1)

                def copy_turned(n):
                    w = (n % TT + 1) * P
                    act.wait_ge(probs_turned, n + 1)
                    if n >= 2:
                        act.wait_ge(pv_done, n - 1)
                    for e in range(2):
                        act.activation(probT[:, n % 2, e, 0:w], bank[4 + e][:, 0:w], ACT.Copy).then_inc(probT_ready, 1)

                exps(0)
                for n in range(ATT_STEPS):
                    if n + 1 < ATT_STEPS:
                        exps(n + 1)
                    copy_turned(n)

            if 2 in order:
                s5_phases()
            for stage, part in enumerate(order):
                norm(stage)
                if part == 0:
                    even_mixer(stage)
                if part == 2:
                    odd_mixer(stage)
                if part in (1, 3):
                    mlp(stage, part // 2, first_unit[part] - first)

        @block.vector
        def _(dve):
            def norm(stage, part):
                dve.wait_ge(rms_ready, stage + 1)
                dve.reciprocal(rstd[:], rms[:]).then_inc(rstd_ready, 1)
                dve.wait_ge(rstd_ready, stage + 1)

                def scale(k):
                    if k >= 2:
                        dve.wait_ge(h_ready, KT * stage + k - 1)
                    dve.scalar_tensor_tensor(out=h_full[:, k % 2, :], in0=x[:, k, :], scalar=column("norm", KT * part + k),
                                             in1=rstd[:], op0=ALU.mult, op1=ALU.mult).then_inc(normed, 1)

                def low(k):
                    dve.wait_ge(normed_hi, KT * stage + k + 1)
                    dve.tensor_tensor(h_lo[:, k, :], h_full[:, k % 2, :], h_hi[:, k, :].bitcast(F32),
                                      ALU.subtract).then_inc(h_ready, 1)
                scale(0)
                for k in range(1, KT):
                    scale(k)
                    low(k - 1)
                low(KT - 1)

            def add_residual(stage, n1, per_tile):
                def tile(i, u):
                    m = i * 2 + u
                    dve.wait_ge(used, i * (2 * per_tile) + (n1 + per_tile * (u + 1)))
                    xm = x[:, bass.ds(m, 1), :].rearrange("p a t -> p (a t)")
                    dve.tensor_tensor(xm, bank[4 + u][:], xm, ALU.add).then_inc(x_ready, 1)
                with dve.Fori(0, KT // 2) as i:
                    for u in range(2):
                        tile(i, u)

            def mlp(stage, layer, n0):
                base = FT * (stage // 2 if len(order) == 4 else 0)

                def tile(i, u):
                    j = i * 2 + u
                    w = COL["mlp_w"] + layer * 3 * FT
                    dve.wait_ge(newest_tap, i * 2 + (base + u + 1))
                    dve.scalar_tensor_tensor(out=conv[:, u, 1:S], in0=bank[u][:, 0:S - 1],
                                             scalar=cols[:, bass.ds(w + FT + j, 1)], in1=conv[:, u, 1:S],
                                             op0=ALU.mult, op1=ALU.add).then_inc(middle_tap, 1)
                    dve.wait_ge(middle_tap, i * 2 + (base + u + 1))
                    dve.scalar_tensor_tensor(out=conv[:, u, 2:S], in0=bank[u][:, 0:S - 2],
                                             scalar=cols[:, bass.ds(w + j, 1)], in1=conv[:, u, 2:S],
                                             op0=ALU.mult, op1=ALU.add).then_inc(conv_done, 1)
                    dve.wait_ge(gelu_done, i * 2 + (base + u + 1))
                    dve.wait_ge(used, i * 4 + (n0 + 2 * u + 2))
                    dve.tensor_tensor(gate[:, u, :], bank[2 + u][:], gelu[:, u, :], ALU.mult).then_inc(gate_done, 1)
                    dve.wait_ge(gate_done, i * 2 + (base + u + 1))
                    gj_hi = g_hi[:, bass.ds(j, 1), :].rearrange("p a t -> p (a t)")
                    gj_lo = g_lo[:, bass.ds(j, 1), :].rearrange("p a t -> p (a t)")
                    dve.tensor_copy(gj_hi, gate[:, u, :]).then_inc(gate_hi_done, 1)
                    dve.wait_ge(gate_hi_done, i * 2 + (base + u + 1))
                    dve.tensor_tensor(gj_lo, gate[:, u, :], gj_hi.bitcast(F32), ALU.subtract).then_inc(gate_ready, 1)

                with dve.Fori(0, FT // 2) as i:
                    for u in range(2):
                        tile(i, u)

            def lru_constants():
                lam = cols[:, COL["lambda"]:COL["lambda"] + HT]
                z, w, w2, acc, neg, tmp = (lam_tmp[:, i, :] for i in range(6))
                step = [0]

                def then(ins):
                    ins.then_inc(lam_step, 1)
                    step[0] += 1
                    dve.wait_ge(lam_step, step[0])

                dve.wait_ge(inputs_in, 48)
                then(dve.tensor_scalar(neg, lam, -1.0, 0.0, ALU.mult, ALU.max))
                then(dve.scalar_tensor_tensor(out=tmp, in0=neg, scalar=-2.0, in1=lam, op0=ALU.mult, op1=ALU.subtract))
                assert step[0] == LAM_ABS
                dve.wait_ge(lam_exp, 1)
                then(dve.tensor_scalar(tmp, z, 2.0, None, ALU.add))
                then(dve.reciprocal(tmp, tmp))
                then(dve.tensor_tensor(w, z, tmp, ALU.mult))
                then(dve.tensor_tensor(w2, w, w, ALU.mult))
                then(dve.tensor_scalar(acc, w2, ATANH[-1], ATANH[-2], ALU.mult, ALU.add))
                for c in ATANH[-3::-1]:
                    then(dve.tensor_tensor(acc, acc, w2, ALU.mult))
                    then(dve.tensor_scalar(acc, acc, c, None, ALU.add))
                then(dve.tensor_tensor(acc, acc, w, ALU.mult))
                then(dve.scalar_tensor_tensor(out=acc, in0=acc, scalar=2.0, in1=neg, op0=ALU.mult, op1=ALU.add))
                then(dve.tensor_scalar(neg_c[:], acc, 8.0, None, ALU.mult))
                then(dve.tensor_scalar(pos_c[:], acc, -8.0, None, ALU.mult))
                assert step[0] == LAM_STEPS

            def s5_phases():
                lr, li = s5p[:, 0:PAIRS], s5p[:, PAIRS:2 * PAIRS]
                step, zr, th, q, f, fh, fl = (small[:, i] for i in range(7))
                done = [0]

                def then(ins):
                    ins.then_inc(s5_small, 1)
                    done[0] += 1
                    dve.wait_ge(s5_small, done[0])

                def spread(a, n):
                    return a.unsqueeze(2).broadcast_to([P, PAIRS, n])

                ks = table("angles").unsqueeze(1).broadcast_to([P, PAIRS, ANGLES])
                dve.memset(v[:, 3, :], 0.0).then_inc(w3_zero, 1)
                dve.wait_ge(inputs_in, 48)
                dve.wait_ge(s5_exp, 1)
                then(dve.tensor_tensor(zr, lr, step, ALU.mult))
                then(dve.tensor_tensor(mag[:], ks[:, :, 0:POWERS], spread(zr, POWERS), ALU.mult))
                assert done[0] == MAG_STEP
                then(dve.tensor_tensor(th, li, step, ALU.mult))
                then(dve.tensor_scalar(q, th, 1 / (2 * np.pi), ROUND, ALU.mult, ALU.add))
                then(dve.tensor_scalar(q, q, ROUND, None, ALU.subtract))
                for part in PI_PARTS:
                    then(dve.scalar_tensor_tensor(out=th, in0=q, scalar=-part, in1=th, op0=ALU.mult, op1=ALU.add))
                then(dve.tensor_scalar(f, th, 1 / (2 * np.pi), None, ALU.mult))
                then(dve.tensor_scalar(fh, f, ROUND12, ROUND12, ALU.add, ALU.subtract))
                then(dve.tensor_tensor(fl, f, fh, ALU.subtract))
                then(dve.tensor_tensor(turns[:], ks, spread(fh, ANGLES), ALU.mult))
                then(dve.tensor_scalar(rot_s[:], turns[:], ROUND, ROUND, ALU.add, ALU.subtract))
                then(dve.tensor_tensor(turns[:], turns[:], rot_s[:], ALU.subtract))
                then(dve.tensor_tensor(rot_c[:], ks, spread(fl, ANGLES), ALU.mult))
                then(dve.tensor_tensor(turns[:], turns[:], rot_c[:], ALU.add))
                then(dve.tensor_scalar(rot_s[:], turns[:], ROUND, ROUND, ALU.add, ALU.subtract))
                then(dve.tensor_tensor(turns[:], turns[:], rot_s[:], ALU.subtract))
                assert done[0] == TURN_STEPS
                dve.wait_ge(s5_sin, 2)
                then(dve.tensor_tensor(turns[:], rot_c[:], rot_c[:], ALU.mult))
                then(dve.tensor_scalar(rot_c[:], turns[:], -2.0, 1.0, ALU.mult, ALU.add))
                assert done[0] == PHASE_STEPS

            def s5_matrices():
                lr, li = s5p[:, 0:PAIRS], s5p[:, PAIRS:2 * PAIRS]

                def param(i):
                    c = 3 * PAIRS + i * PAIRS * GP
                    return s5p[:, c:c + PAIRS * GP].rearrange("p (q c) -> p q c", c=GP)

                br, bi, cr_, ci_ = (param(i) for i in range(4))
                den, am1, cr, ci, t1, t2, t3, t4 = (small[:, i] for i in range(7, 15))
                ar, ai = pow_r[:, :, 1], pow_i[:, :, 1]
                done = [0]

                def then(*steps):
                    for ins in steps:
                        ins.then_inc(s5_bmat, 1)
                        done[0] += 1
                    dve.wait_ge(s5_bmat, done[0])

                def spread(a):
                    return a.unsqueeze(2).broadcast_to([P, PAIRS, GP])

                dve.wait_ge(s5_exp, 2)
                then(dve.tensor_tensor(pow_r[:], mag[:], rot_c[:, :, 0:POWERS], ALU.mult),
                     dve.tensor_tensor(pow_i[:], mag[:], rot_s[:, :, 0:POWERS], ALU.mult),
                     dve.tensor_tensor(t1, lr, lr, ALU.mult), dve.tensor_tensor(t2, li, li, ALU.mult))
                then(dve.tensor_tensor(den, t1, t2, ALU.add), dve.tensor_scalar(am1, ar, -1.0, None, ALU.add))
                then(dve.reciprocal(den, den), dve.tensor_tensor(t1, am1, lr, ALU.mult),
                     dve.tensor_tensor(t2, ai, li, ALU.mult), dve.tensor_tensor(t3, ai, lr, ALU.mult),
                     dve.tensor_tensor(t4, am1, li, ALU.mult))
                then(dve.tensor_tensor(cr, t1, t2, ALU.add), dve.tensor_tensor(ci, t3, t4, ALU.subtract))
                then(dve.tensor_tensor(cr, cr, den, ALU.mult), dve.tensor_tensor(ci, ci, den, ALU.mult))
                then(dve.tensor_tensor(bb[:, 0], br, spread(cr), ALU.mult), dve.tensor_tensor(bb[:, 1], bi, spread(ci), ALU.mult),
                     dve.tensor_tensor(bb[:, 2], bi, spread(cr), ALU.mult), dve.tensor_tensor(bb[:, 3], br, spread(ci), ALU.mult))
                then(dve.tensor_tensor(bb[:, 0], bb[:, 0], bb[:, 1], ALU.subtract),
                     dve.tensor_tensor(bb[:, 2], bb[:, 2], bb[:, 3], ALU.add))
                then(dve.tensor_scalar(bb[:, 3], ci_, -1.0, None, ALU.mult))

                def product(power, re, im, conj):
                    a = [t[:, :, power:power + CH].unsqueeze(3).broadcast_to([P, PAIRS, CH, GP]) for t in (pow_r, pow_i)]
                    b = [t.unsqueeze(2).broadcast_to([P, PAIRS, CH, GP]) for t in (re, im)]
                    yield dve.tensor_tensor(b_mat[:, 0], b[0], a[0], ALU.mult), dve.tensor_tensor(t_mat[:, 0], b[1], a[1], ALU.mult)
                    yield (dve.tensor_tensor(b_mat[:, 0], b_mat[:, 0], t_mat[:, 0], ALU.add if conj else ALU.subtract),
                           dve.tensor_tensor(b_mat[:, 1], b[1], a[0], ALU.mult), dve.tensor_tensor(t_mat[:, 1], b[0], a[1], ALU.mult))
                    yield (dve.tensor_tensor(b_mat[:, 1], b_mat[:, 1], t_mat[:, 1], ALU.subtract if conj else ALU.add),)

                for steps in product(0, bb[:, 0], bb[:, 2], False):
                    then(*steps)
                assert done[0] == BMAT_STEPS
                return then, product, cr_, done

            def s5_output_matrices(then, product, c_re, done):
                dve.wait_ge(s5_prep_mm, 9)
                for steps in product(1, c_re, bb[:, 3], True):
                    then(*steps)
                assert done[0] == CMAT_STEPS

            def odd_mixer(stage):
                for i in range(2):
                    dve.wait_ge(gate_pre, i + 1)
                    dve.tensor_scalar(logs[:, i, :], bank[5 + i][:], column("gk_b", i), None, ALU.add).then_inc(gk_logs, 1)
                dve.wait_ge(gk_logs, 2)
                dve.wait_ge(gk_abs, 3)
                flat_logs = logs[:].rearrange("p i t -> p (i t)")
                dve.scalar_tensor_tensor(out=flat_logs, in0=flat_logs, scalar=0.0, in1=e_pos[:].rearrange("p i t -> p (i t)"),
                                         op0=ALU.min, op1=ALU.subtract).then_inc(gk_sum, 1)
                dve.wait_ge(gk_sum, 1)
                for i in range(2):
                    dve.tensor_tensor_scan(logs[:, i, :], table("chunk_keep"), logs[:, i, :], 0.0, ALU.mult, ALU.add).then_inc(gk_sum, 1)
                dve.wait_ge(gk_exp, 2)
                dve.tensor_copy(chunk_decay[:], e_pos[:].rearrange("p i (n c) -> p i n c", c=GC)[:, :, :, GC - 1]).then_inc(gk_step, 1)
                dve.wait_ge(gk_step, 1)
                for i in range(2):
                    dve.wait_ge(used, O_Q - first + i + 1)
                    dve.scalar_tensor_tensor(out=e_pos[:, i, :], in0=bank[(7, 4)[i]][:], scalar=64 ** -0.5, in1=e_pos[:, i, :],
                                             op0=ALU.mult, op1=ALU.mult).then_inc(gk_dec, 1)
                for i in range(2):
                    dve.wait_ge(used, O_K - first + i + 1)
                    dve.tensor_tensor(e_neg[:, i, :], bank[5 + i][:], e_neg[:, i, :], ALU.mult).then_inc(gk_dec, 1)
                dve.wait_ge(gk_dec, 4)
                for i in range(2):
                    dve.tensor_tensor(logs[:, i, :].rearrange("p (n c) -> p n c", c=GC),
                                      e_neg[:, i, :].rearrange("p (n c) -> p n c", c=GC),
                                      chunk_decay[:, i, :].unsqueeze(2).broadcast_to([P, GN, GC]), ALU.mult).then_inc(gk_dec, 1)

                a, b_, c, d_, e_ = h_full_pairs, square_pairs, st[:, 0], st[:, 1], st[:, 2]
                cos_, sin_ = rot[:, 0], rot[:, 1]
                done = [0]

                def then(*steps):
                    for ins in steps:
                        ins.then_inc(s5_step, 1)
                        done[0] += 1
                    dve.wait_ge(s5_step, done[0])

                def local(ri):
                    return [bank[2 * ri + i][:].rearrange("p (q c) -> p q c", c=CHUNKS) for i in range(2)]

                def times(out, ri, by):
                    return [dve.tensor_tensor(out[:, 8 * i:8 * i + 8], local(ri)[i], by[:, 8 * i:8 * i + 8], ALU.mult) for i in range(2)]

                dve.wait_ge(s5_local, 1)
                dve.wait_ge(s5_rot_in, 32)
                dve.tensor_copy(d_, m8[:].unsqueeze(2).broadcast_to([P, PAIRS, CHUNKS])).then_inc(s5_coef, 1)
                times_all = times(a, 0, cos_) + times(c, 1, cos_) + times(b_, 1, sin_) + times(e_, 0, sin_)
                last_reads = times_all
                for n, ins in enumerate(last_reads):
                    if n % 2:
                        ins.then_inc(s5_step, 1)
                    else:
                        ins.then_inc(s5_half, 1)
                done[0] = 4
                dve.wait_ge(s5_step, 4)
                dve.wait_ge(s5_half, 4)
                dve.wait_ge(s5_coef, 1)
                then(dve.tensor_tensor(a, a, b_, ALU.add), dve.tensor_tensor(c, c, e_, ALU.subtract),
                     dve.memset(d_[:, :, 0:1], 0.0))
                flat = [t.rearrange("p q c -> p (q c)") for t in (a, c, d_)]
                then(dve.tensor_tensor_scan(flat[0], flat[2], flat[0], 0.0, ALU.mult, ALU.add),
                     dve.tensor_tensor_scan(flat[1], flat[2], flat[1], 0.0, ALU.mult, ALU.add))
                then(dve.tensor_tensor(d_, a, cos_, ALU.mult), dve.tensor_tensor(b_, c, sin_, ALU.mult),
                     dve.memset(e_[:, :, 0:1], 0.0))
                n_ = CHUNKS
                then(dve.tensor_tensor(e_[:, :, 1:n_], d_[:, :, 0:n_ - 1], b_[:, :, 0:n_ - 1], ALU.subtract))
                then(dve.tensor_tensor(d_, a, sin_, ALU.mult), dve.tensor_tensor(b_, c, cos_, ALU.mult))
                then(dve.tensor_tensor(a[:, :, 1:n_], d_[:, :, 0:n_ - 1], b_[:, :, 0:n_ - 1], ALU.add),
                     dve.memset(a[:, :, 0:1], 0.0))
                assert done[0] == S5_STEPS

                for t in range(TT):
                    dve.wait_ge(sg_ready, t + 1)
                    g4 = sg[:, t, :].rearrange("p (h d) -> p h d", d=DV)
                    gain = cols[:, COL["gla_norm"]:COL["gla_norm"] + DV].unsqueeze(1).broadcast_to([P, GH, DV])
                    dve.tensor_tensor(g4, g4, gain, ALU.mult).then_inc(sg_gain, 1)
                dve.wait_ge(s5_y_ready, 4)
                dve.memset(state[:, 0], 0.0).then_inc(state_step, 1)
                for h in range(GH):
                    dve.wait_ge(att_ready, h + 1)
                    causal = table("chunk_causal").unsqueeze(1).broadcast_to([P, TT, P])
                    dve.tensor_tensor(attT[:, h, :].rearrange("p (t c) -> p t c", c=P),
                                      bank[(2, 3, 0, 1)[h]][:].rearrange("p (t c) -> p t c", c=P), causal, ALU.mult).then_inc(attT_ready, 1)
                for n in range(GN - 1):
                    dve.wait_ge(kv_ready, min(n // 4 * 4 + 4, GN - 1))
                    dve.wait_ge(state_step, 1 + 2 * n)
                    for i in range(2):
                        col = (n // 2 % 2) * 256 + i * DV
                        dve.scalar_tensor_tensor(out=state[:, n + 1, i], in0=state[:, n, i], scalar=chunk_decay[:, i, n:n + 1],
                                                 in1=bank[4 + 2 * (n % 2) + n // 4][:, col:col + DV],
                                                 op0=ALU.mult, op1=ALU.add).then_inc(state_step, 1)
                dve.wait_ge(y_loaded, 16)
                uf = u[:].rearrange("p m l c -> p m (l c)")
                y_in = u_in[:].rearrange("p g c -> p (g c)").rearrange("p (m n) -> p m n", m=HT)
                for m in range(HT):
                    ins = dve.scalar_tensor_tensor(out=y_in[:, m], in0=uf[:, m], scalar=column("s5_d", m), in1=y_in[:, m],
                                                   op0=ALU.mult, op1=ALU.add)
                ins.then_inc(ys_ready, 1)
                for t in range(TT):
                    dve.wait_ge(intra_ready, t + 1)
                    dve.wait_ge(inter_out, 2 * t + 2)
                    dve.tensor_tensor(o[:, t, :], bank[t][:], o[:, t, :], ALU.add).then_inc(o_ready, 1)
                dve.wait_ge(used, O_G - first + 4)
                dve.wait_ge(ys_gelu, 1)
                dve.tensor_copy(h_hi[:, 0:HT, :], y_in).then_inc(ys_split, 1)
                dve.wait_ge(ys_split, 1)
                dve.tensor_tensor(h_lo[:, 0:HT, :], y_in, h_hi[:, 0:HT, :].bitcast(F32), ALU.subtract).then_inc(ys_split, 1)
                for t in range(TT):
                    dve.wait_ge(o_squared, t + 1)
                    dve.tensor_reduce(gla_var[:, t * GH:(t + 1) * GH], squares[:, t % 2, :].rearrange("p (h d) -> p h d", d=DV),
                                      AX_X, ALU.add).then_inc(o_sum, 1)
                dve.wait_ge(o_rms, 1)
                dve.reciprocal(gla_var[:], gla_var[:]).then_inc(o_inv, 1)
                dve.wait_ge(o_inv, 1)
                o16 = o[:].rearrange("p t (h d) -> p (t h) d", d=DV)
                dve.tensor_tensor(o16, o16, gla_var[:].unsqueeze(2).broadcast_to([P, TT * GH, DV]), ALU.mult).then_inc(o_step, 1)
                dve.wait_ge(o_step, 1)
                dve.wait_ge(sg_gain, TT)
                dve.tensor_tensor(o[:], o[:], sg[:], ALU.mult).then_inc(o_step, 1)
                sig = st[:, 0:2].rearrange("p a q c -> p (a q c)").rearrange("p (m n) -> p m n", m=HT)
                dve.wait_ge(glu_sig, HT)
                dve.tensor_tensor(y_in, y_in, sig, ALU.mult).then_inc(s5_gated, 1)
                dve.wait_ge(s5_gated, 1)
                for m in range(HT):
                    in_time = y_in[:, m].rearrange("p (l c) -> p c l", c=CHUNKS)
                    hi = h_hi[:, m, :].rearrange("p (c l) -> p c l", l=CH)
                    dve.tensor_copy(hi, in_time).then_inc(s5_gated, 1)
                    dve.wait_ge(s5_gated, m + 2)
                    ins = dve.tensor_tensor(h_lo[:, m, :].rearrange("p (c l) -> p c l", l=CH), in_time, hi.bitcast(F32), ALU.subtract)
                ins.then_inc(s5_out, 1)
                for h in range(GH):
                    dve.wait_ge(o_turned, h + 1)
                    y_hi, y_lo = h_hi[:, HT + h, :], h_lo[:, HT + h, :]
                    dve.tensor_copy(y_hi, bank[4 + h][:]).then_inc(gla_y, 1)
                    dve.wait_ge(gla_y, 2 * h + 1)
                    dve.tensor_tensor(y_lo, bank[4 + h][:], y_hi.bitcast(F32), ALU.subtract).then_inc(gla_y, 1)

            def even_mixer(stage):
                if 2 in order:
                    matrices = s5_matrices()
                lru_constants()
                for which in range(2):
                    var = qk_var[:, which, :]
                    for t in range(TT):
                        n = TT * which + t
                        dve.wait_ge(qk_squared, n + 1)
                        dve.tensor_reduce(var[:, t * HEADS:(t + 1) * HEADS],
                                          squares[:, n % 2, :].rearrange("p (h d) -> p h d", d=HD),
                                          AX_X, ALU.add).then_inc(qk_sum, 1)
                    dve.wait_ge(qk_rms, which + 1)
                    dve.reciprocal(var, var).then_inc(qk_inv, 1)
                    dve.wait_ge(qk_inv, which + 1)
                    for t in range(TT):
                        inv = var[:, t * HEADS:(t + 1) * HEADS].unsqueeze(2).broadcast_to([P, HEADS, HD])
                        dve.tensor_tensor(qk[:, which, t, :].rearrange("p (h d) -> p h d", d=HD),
                                          bank[4 * which + t][:].rearrange("p (h d) -> p h d", d=HD), inv,
                                          ALU.mult).then_inc(qk_step, 1)
                if 2 in order:
                    s5_output_matrices(*matrices)
                for which in range(2):
                    a = qk[:, which].rearrange("p t (h d) -> p (t h) d", d=HD)
                    gain = cols[:, COL[("q_norm", "k_norm")[which]]:][:, 0:HD].unsqueeze(1).broadcast_to([P, TT * HEADS, HD])
                    dve.wait_ge(qk_step, 4 * which + 4)
                    base = 2 * TT + 3 * which
                    dve.tensor_tensor(a, a, gain, ALU.mult).then_inc(qk_step, 1)
                    dve.wait_ge(qk_step, base + 1)
                    r = qk[:, which].rearrange("p t (h d) -> p t h d", d=HD)
                    x1, x2 = r[:, :, :, 0:ROPE], r[:, :, :, ROPE:2 * ROPE]
                    c, sn = (table(n).rearrange("p (t d) -> p t d", d=ROPE).unsqueeze(2).broadcast_to([P, TT, HEADS, ROPE])
                             for n in ("cos", "sin"))
                    for i, (xx, tt_) in enumerate(((x1, c), (x2, sn), (x2, c), (x1, sn))):
                        op = dve.tensor_tensor(rope_tmp[:, i], xx, tt_, ALU.mult)
                        op.then_inc(qk_rope, 1)
                    dve.wait_ge(qk_rope, 4 * (which + 1))
                    dve.tensor_tensor(x1, rope_tmp[:, 0], rope_tmp[:, 1], ALU.subtract).then_inc(qk_step, 1)
                    dve.tensor_tensor(x2, rope_tmp[:, 2], rope_tmp[:, 3], ALU.add).then_inc(qk_step, 1)
                    if which == 0:
                        dve.wait_ge(qk_step, 2 * TT + 3)

                for m in range(HT):
                    dve.wait_ge(x_newest, m + 1)
                    for i in range(3):
                        back = i + 1
                        dve.scalar_tensor_tensor(out=xc[:, m, back:S], in0=bank[4 + m][:, 0:S - back],
                                                 scalar=column("lru_w", (3 - back) * HT + m), in1=xc[:, m, back:S],
                                                 op0=ALU.mult, op1=ALU.add).then_inc(x_conv, 1)
                        dve.wait_ge(x_conv, 3 * m + i + 1)
                dve.wait_ge(lru_exp, 2 * HT)
                dve.tensor_scalar(rg[:], coef[:], 1.0, None, ALU.add).then_inc(lru_step, 1)
                dve.wait_ge(lru_step, 1)
                dve.reciprocal(rg[:], rg[:]).then_inc(lru_step, 1)
                dve.wait_ge(lru_step, 2)
                dve.tensor_tensor(coef[:], coef[:], rg[:], ALU.mult).then_inc(lru_step, 1)
                dve.tensor_tensor(ig[:], ig[:], xc[:], ALU.mult).then_inc(lru_step, 1)
                dve.wait_ge(lru_step, 4)
                dve.wait_ge(lru_sqrt, 1)
                dve.tensor_tensor(ig[:], ig[:], coef[:], ALU.mult).then_inc(lru_step, 1)
                dve.wait_ge(lru_step, 5)
                for m in range(HT):
                    dve.tensor_tensor_scan(rg[:, m, :], decay[:, m, :], ig[:, m, :], 0.0, ALU.mult,
                                           ALU.add).then_inc(lru_step, 1)
                dve.wait_ge(lru_step, 5 + HT)
                dve.wait_ge(gg_ready, HT)
                dve.tensor_tensor(rg[:], rg[:], gg[:], ALU.mult).then_inc(lru_step, 1)
                dve.wait_ge(lru_step, 6 + HT)
                dve.tensor_copy(h_hi[:, 0:HT, :], rg[:]).then_inc(lru_step, 1)
                dve.wait_ge(lru_step, 7 + HT)
                dve.tensor_tensor(h_lo[:, 0:HT, :], rg[:], h_hi[:, 0:HT, :].bitcast(F32), ALU.subtract).then_inc(lru_y, 1)
                dve.wait_ge(lru_y, 1)

                def mask_scores(n):
                    t = n % TT
                    w = (t + 1) * P
                    dve.wait_ge(scores_ready, n + 1)
                    if n >= 2:
                        dve.wait_ge(probs_turned, n - 1)
                    for e in range(2):
                        dve.tensor_tensor_reduce(prob[:, n % 2, e, 0:w], bank[2 * e + n % 2][:, 0:w],
                                                 table("mask")[:, S - w:S], 1.0, NEVER, ALU.add, ALU.max,
                                                 row_max[:, n % 2, e:e + 1]).then_inc(masked, 1)
                    dve.wait_ge(masked, 2 * n + 2)
                    dve.tensor_scalar(neg_max[:, n % 2, :], row_max[:, n % 2, :], -HD ** -0.5, None,
                                      ALU.mult).then_inc(negmax_ready, 1)

                def normalise(n):
                    w = (n % TT + 1) * P
                    dve.wait_ge(exped, 2 * n + 2)
                    dve.reciprocal(row_inv[:, n % 2, :], row_sum[:, n % 2, :]).then_inc(rinv_ready, 1)
                    dve.wait_ge(rinv_ready, n + 1)
                    for e in range(2):
                        dve.tensor_scalar(prob[:, n % 2, e, 0:w], prob[:, n % 2, e, 0:w], row_inv[:, n % 2, e:e + 1],
                                          None, ALU.mult).then_inc(probs_ready, 1)

                def take_heads(hp):
                    dve.wait_ge(pv_done, TT * (hp + 1))
                    y_hi, y_lo = h_hi[:, HT + hp, :], h_lo[:, HT + hp, :]
                    dve.tensor_copy(y_hi, bank[6 + hp % 2][:]).then_inc(att_y, 1)
                    dve.wait_ge(att_y, 2 * hp + 1)
                    dve.tensor_tensor(y_lo, bank[6 + hp % 2][:], y_hi.bitcast(F32), ALU.subtract).then_inc(att_y, 1)

                mask_scores(0)
                mask_scores(1)
                for n in range(ATT_STEPS):
                    normalise(n)
                    if n + 2 < ATT_STEPS:
                        mask_scores(n + 2)
                    if n % TT == 1 and n > TT:
                        take_heads(n // TT - 1)
                take_heads(HT - 1)

            if 2 in order:
                s5_phases()
            for stage, part in enumerate(order):
                norm(stage, part)
                if part == 0:
                    even_mixer(stage)
                    add_residual(stage, E_O, 1)
                if part == 2:
                    if 0 not in order:
                        s5_output_matrices(*s5_matrices())
                    odd_mixer(stage)
                    add_residual(stage, O_O - first, 1)
                if part in (1, 3):
                    mlp(stage, part // 2, first_unit[part] - first)
                    add_residual(stage, first_unit[part] - first + 2 * FT, 3)


PARTS = (0, 1, 2, 3)


def by_tiles(w):
    k, n = w.shape
    t = w.reshape(k // (8 * P), 8, P, n // P, P)
    return np.ascontiguousarray(t.transpose(3, 0, 2, 1, 4)).reshape(-1, P, UNIT)


def by_rows(w):
    return np.ascontiguousarray(w.reshape(4, 2, P, 512).transpose(0, 2, 1, 3)).reshape(-1, P, UNIT)


def on_partitions(v):
    return np.ascontiguousarray(v.reshape(-1, P).T)


def make_tables():
    back = np.arange(P)[:, None] + (S - P) - np.arange(S)[None, :]
    count = sum(((back >= 0) & (back % dil == 0) & (back <= BACK * dil)).astype(np.float32) for _, dil in PATTERNS)
    mask = np.where(count > 0, np.log(np.maximum(count, 1)) * HD ** 0.5, NEVER)
    inv = np.float32(500000.0) ** (-np.arange(0, 2 * ROPE, 2, dtype=np.float32) / np.float32(2 * ROPE))
    angle = np.arange(S, dtype=np.float32)[:, None] * inv[None, :]
    step, chunk = np.arange(P), np.arange(P) // GC
    parts = {
        "identity": np.eye(P), "mask": mask,
        "angles": np.broadcast_to(np.concatenate([np.arange(POWERS), CH * np.arange(CHUNKS)]), (P, ANGLES)),
        "chunk_keep": np.broadcast_to(np.arange(S) % GC != 0, (P, S)),
        "chunk_causal": (step[:, None] <= step[None, :]) & (chunk[:, None] == chunk[None, :]),
    }
    for name, f in (("cos", np.cos), ("sin", np.sin)):
        parts[name] = f(angle).reshape(TT, P, ROPE).transpose(1, 0, 2).reshape(P, -1)
    return np.ascontiguousarray(np.concatenate([parts[n] for n, _ in _TABLES], axis=1).astype(np.float32))


def block_diagonal(w):
    out = np.zeros((P, HT, P), w.dtype)
    for b in range(8):
        at = slice(64 * (b % 2), 64 * (b % 2) + 64)
        out[at, b // 2, at] = w[b]
    return out


def lay_out(x, e_norm, e_w_in, e_w_out, e_conv_w, e_conv_b, e_gate_a_w, e_gate_a_b, e_gate_x_w, e_gate_x_b,
            e_lambda, e_q_norm, e_k_norm, o_lambda_re, o_lambda_im, o_b_re, o_b_im, o_c_re, o_c_im, o_d, o_log_step,
            o_glu_b, o_gk_w, o_gk_b, o_gla_norm, o_norm, o_w_in, o_glu_w, o_w_out, f_norm, f_w_in, f_conv_w, f_conv_b, f_w_out):
    def cut(w, sizes):
        return np.split(w, np.cumsum(sizes)[:-1], axis=1)

    ex, eg, eq, ek, ev = cut(e_w_in[0], [512] * 5)
    ou, oq, ok, ov, og, ogk = cut(o_w_in[0], [512, 256, 256, 512, 512, 16])
    ogk = np.pad(ogk, ((0, 0), (0, P - 16)))

    def mlp(layer):
        up = by_tiles(f_w_in[layer]).reshape(2, FT, P, UNIT).transpose(1, 0, 2, 3).reshape(-1, P, UNIT)
        return [up, by_tiles(f_w_out[layer])]

    glu = o_glu_w[0].reshape(HT, P, HT, P).transpose(2, 0, 1, 3).reshape(2, 8, P, P).transpose(0, 2, 1, 3).reshape(2, P, UNIT)
    units = np.concatenate(
        [by_rows(eq), by_rows(ek), by_rows(ev), by_tiles(ex), by_tiles(eg), by_tiles(e_w_out[0])] + mlp(0)
        + [by_tiles(ou), by_tiles(ogk), by_tiles(oq), by_tiles(ok), by_rows(ov), by_rows(og), glu, by_tiles(o_w_out[0])]
        + mlp(1))
    assert units.shape == (N_UNITS, P, UNIT)
    columns = {
        "norm": np.concatenate([on_partitions(v) for v in (e_norm[0], f_norm[0], o_norm[0], f_norm[1])], axis=1),
        "mlp_w": on_partitions(f_conv_w), "mlp_b": on_partitions(f_conv_b),
        "lru_w": on_partitions(e_conv_w), "lru_b": on_partitions(e_conv_b), "gate_a_b": on_partitions(e_gate_a_b),
        "gate_x_b": on_partitions(e_gate_x_b), "lambda": on_partitions(e_lambda),
        "s5_d": on_partitions(o_d), "glu_b": on_partitions(o_glu_b), "gk_b": on_partitions(o_gk_b),
        "gla_norm": np.broadcast_to(o_gla_norm, (P, DV)),
        "q_norm": np.broadcast_to(e_q_norm, (P, HD)), "k_norm": np.broadcast_to(e_k_norm, (P, HD)),
    }
    columns = np.concatenate([columns[n] for n, _ in _COLUMNS], axis=1)
    assert columns.shape == (P, N_COLS)

    def states(a):
        return a.reshape(PAIRS, 2, ST, -1).transpose(1, 2, 0, 3).reshape(P, -1)

    s5 = np.concatenate([states(o_lambda_re[0]), states(o_lambda_im[0]),
                         states(np.broadcast_to(o_log_step[0][:, None], (2 * PAIRS, ST))),
                         states(o_b_re[0]), states(o_b_im[0]),
                         states(o_c_re[0].transpose(0, 2, 1)), states(o_c_im[0].transpose(0, 2, 1))], axis=1)
    return {"s5": np.ascontiguousarray(s5), "gk_w": np.ascontiguousarray(o_gk_w[0]),
            "xT": np.ascontiguousarray(x[0].T), "units": units, "columns": np.ascontiguousarray(columns),
            "tables": make_tables(), "gates_a": block_diagonal(e_gate_a_w[0]), "gates_x": block_diagonal(e_gate_x_w[0])}


def kernel(**inputs):
    import concourse.bacc as bacc
    from concourse.bass_utils import run_bass_kernel_spmd

    arrays = lay_out(**{n: np.asarray(a) for n, a in inputs.items()})
    nc = bacc.Bacc("TRN2", target_bir_lowering=False, num_devices=1)
    args = {n: nc.dram_tensor(n, a.shape, F32, kind="ExternalInput").ap() for n, a in arrays.items()}
    outT = nc.dram_tensor("outT", (D, S), F32, kind="ExternalOutput").ap()
    build(nc, PARTS, outT=outT, **args)
    r = run_bass_kernel_spmd(nc, [arrays], core_ids=[0])
    return np.ascontiguousarray(r.results[0]["outT"].T)[None]
```

```python
from contextlib import ExitStack

import numpy as np

import concourse.bass as bass
from concourse import mybir

ALU = mybir.AluOpType
ACT = mybir.ActivationFunctionType
AX_X = mybir.AxisListType.X
F32 = mybir.dt.float32
F32R = mybir.dt.float32r

P = 128
D = 1024
S = 512
KT = D // P
HALF = D // 2
HT = HALF // P
FF = 3 * D
FT = FF // P
TT = S // P
EPS = 1e-6
HEADS, HD = 8, 64
ROPE = 8
PATTERNS = ((128, 1), (512, 4), (2048, 16))
BACK = 128
NEVER = -1e30
ATT_STEPS = HEADS // 2 * TT
QK_STEPS = 2 * TT + 6
ATANH = [1.0 / n for n in range(1, 16, 2)]
LAM_ABS = 2

CH, PAIRS, GP, ST = 8, 16, 16, 64
CHUNKS = S // CH
POWERS = CH + 1
ANGLES = POWERS + CHUNKS
ROUND = 1.5 * 2 ** 23
ROUND12 = 1.5 * 2 ** 11
TWO_PI = 6.2831850
PI_PARTS = (6.28125, 0.0019350051879882812, 3.0200665743e-07)
S5_STORES = 3 + CH
W1_SLOTS = HT
S5_COLS = 3 * PAIRS + 4 * PAIRS * GP
MAG_STEP, TURN_STEPS, PHASE_STEPS = 2, 18, 20
BMAT_STEPS, CMAT_STEPS = 28, 34
S5_STEPS = 17

GH, DV, GC = 4, 128, 64
GN = S // GC
LAM_STEPS = LAM_ABS + 5 + 2 * (len(ATANH) - 2) + 4

UNIT = 8 * P
E_Q, E_K, E_V, E_X, E_G, E_O = 0, 4, 8, 12, 16, 20
FIRST_MLP = 28
MLP_UNITS = 2 * FT + 3 * KT
O_U = FIRST_MLP + MLP_UNITS
O_GK, O_Q, O_K, O_V, O_G, O_GLU, O_O = O_U + 4, O_U + 5, O_U + 7, O_U + 9, O_U + 13, O_U + 17, O_U + 19
SECOND_MLP = O_O + 8
N_UNITS = SECOND_MLP + MLP_UNITS
RAW_SLOTS = 4
SPLIT_SLOTS = 2

_COLUMNS = [("norm", 4 * KT), ("mlp_w", 2 * 3 * FT), ("mlp_b", 2 * FT),
            ("lru_w", 4 * HT), ("lru_b", HT), ("gate_a_b", HT), ("gate_x_b", HT), ("lambda", HT),
            ("q_norm", HD), ("k_norm", HD),
            ("s5_d", HT), ("glu_b", HT), ("gk_b", 2), ("gla_norm", DV)]
COL = {}
for _name, _n in _COLUMNS:
    COL[_name] = sum(n for _, n in _COLUMNS[:len(COL)])
N_COLS = sum(n for _, n in _COLUMNS)


_TABLES = [("identity", P), ("mask", S), ("cos", TT * ROPE), ("sin", TT * ROPE), ("angles", ANGLES),
           ("chunk_keep", S), ("chunk_causal", P)]
TAB = {}
for _name, _n in _TABLES:
    TAB[_name] = sum(n for _, n in _TABLES[:len(TAB)])
N_TAB = sum(n for _, n in _TABLES)


def build(nc, parts, xT, units, columns, tables, gates_a, gates_x, s5, gk_w, outT):
    with ExitStack() as ctx:
        def sb(name, shape, dt=F32, where=ctx):
            return where.enter_context(nc.sbuf_tensor(name, shape, dt))

        def sem(name):
            return ctx.enter_context(nc.semaphore(name))

        bank = [ctx.enter_context(nc.psum_tensor(f"bank{b}", [P, 512], F32)) for b in range(8)]

        x = sb("x", [P, KT, S])
        h_hi = sb("h_hi", [P, KT, S], F32R)
        h_lo = sb("h_lo", [P, KT, S], F32R)
        raw = sb("raw", [P, RAW_SLOTS, UNIT])
        w_hi = sb("w_hi", [P, SPLIT_SLOTS, UNIT], F32R)
        w_lo = sb("w_lo", [P, SPLIT_SLOTS, UNIT], F32R)
        cols = sb("cols", [P, N_COLS])
        ones = sb("ones", [P, P])
        eps = sb("eps", [P, 1])
        zero = sb("zero", [P, 1])
        tabs = sb("tabs", [P, N_TAB])
        squares = sb("squares", [P, 2, S])
        total = sb("total", [P, S])
        rstd = sb("rstd", [P, S])
        rstd_t = sb("rstd_t", [P, TT])
        h_full = sb("h_full", [P, 2, S])

        landed = [sem(f"landed{s}") for s in range(RAW_SLOTS)]
        hi_split = sem("hi_split")
        split = sem("split")
        used = sem("used")
        inputs_in = sem("inputs_in")
        consts_set = sem("consts_set")
        x_ready = sem("x_ready")
        x_in = [sem(f"x_in{k}") for k in range(KT)]
        gained_hi = sem("gained_hi")
        squared = sem("squared")
        total_clear = sem("total_clear")
        added = sem("added")
        summed = sem("summed")
        rms_ready = sem("rms_ready")
        rstd_ready = sem("rstd_ready")
        h_ready = sem("h_ready")
        scaled = sem("scaled")
        gate_raw = sem("gate_raw")
        newest_tap = sem("newest_tap")
        middle_tap = sem("middle_tap")
        conv_done = sem("conv_done")
        gelu_done = sem("gelu_done")
        gate_done = sem("gate_done")
        gate_hi_done = sem("gate_hi_done")
        gate_ready = sem("gate_ready")
        out_stored = sem("out_stored")
        s5_in = sem("s5_in")
        s5_exp = sem("s5_exp")
        s5_small = sem("s5_small")
        s5_sin = sem("s5_sin")
        s5_bmat = sem("s5_bmat")
        s5_prep_mm = sem("s5_prep_mm")
        s5_w1_out = sem("s5_w1_out")
        s5_v_out = sem("s5_v_out")
        s5_stored = sem("s5_stored")
        s5_rot_stored = sem("s5_rot_stored")
        s5_w1_stored = [sem(f"s5_w1_stored{n}") for n in range(W1_SLOTS)]
        gl_scaled = sem("gl_scaled")
        xl_scaled = sem("xl_scaled")
        q_inv_scaled = sem("q_inv_scaled")
        gk_scaled = sem("gk_scaled")
        s5_loaded = sem("s5_loaded")
        s5_w2_loaded = sem("s5_w2_loaded")
        w3_zero = sem("w3_zero")
        w3_in = sem("w3_in")
        gk_in = sem("gk_in")
        u_ready = sem("u_ready")
        u_stored = sem("u_stored")
        u_loaded = sem("u_loaded")
        gk_ready = sem("gk_ready")
        gate_pre = sem("gate_pre")
        gk_abs = sem("gk_abs")
        gk_logs = sem("gk_logs")
        gk_sum = sem("gk_sum")
        gk_exp = sem("gk_exp")
        gk_dec = sem("gk_dec")
        s5_local = sem("s5_local")
        s5_step = sem("s5_step")
        s5_coef = sem("s5_coef")
        s5_half = sem("s5_half")
        s5_rot_in = sem("s5_rot_in")
        s5_gated = sem("s5_gated")
        gk_step = sem("gk_step")
        o_inv = sem("o_inv")
        s5_y_ready = sem("s5_y_ready")
        s5_y_out = sem("s5_y_out")
        y_stored = sem("y_stored")
        y_loaded = sem("y_loaded")
        ys_ready = sem("ys_ready")
        ys_gelu = sem("ys_gelu")
        ys_split = sem("ys_split")
        glu_sig = sem("glu_sig")
        s5_out = sem("s5_out")
        vg_ready = sem("vg_ready")
        sg_ready = sem("sg_ready")
        sg_gain = sem("sg_gain")
        k_turned = sem("k_turned")
        k_end_ready = sem("k_end_ready")
        att_ready = sem("att_ready")
        attT_ready = sem("attT_ready")
        kv_ready = sem("kv_ready")
        state_step = sem("state_step")
        intra_ready = sem("intra_ready")
        inter_ready = sem("inter_ready")
        inter_out = sem("inter_out")
        o_ready = sem("o_ready")
        o_squared = sem("o_squared")
        o_sum = sem("o_sum")
        o_rms = sem("o_rms")
        o_step = sem("o_step")
        o_turned = sem("o_turned")
        gla_y = sem("gla_y")
        even_in = sem("even_in")
        qk_squared = sem("qk_squared")
        qk_sum = sem("qk_sum")
        qk_rms = sem("qk_rms")
        qk_step = sem("qk_step")
        v_ready = sem("v_ready")
        x_newest = sem("x_newest")
        x_conv = sem("x_conv")
        lam_step = sem("lam_step")
        qk_rope = sem("qk_rope")
        qk_inv = sem("qk_inv")
        lam_exp = sem("lam_exp")
        gates_made = sem("gates_made")
        gate_sig = sem("gate_sig")
        lru_exp = sem("lru_exp")
        lru_step = sem("lru_step")
        lru_sqrt = sem("lru_sqrt")
        gg_ready = sem("gg_ready")
        lru_y = sem("lru_y")
        qk_turned = sem("qk_turned")
        qkT_ready = sem("qkT_ready")
        scores_ready = sem("scores_ready")
        masked = sem("masked")
        negmax_ready = sem("negmax_ready")
        exped = sem("exped")
        rinv_ready = sem("rinv_ready")
        probs_ready = sem("probs_ready")
        probs_turned = sem("probs_turned")
        probT_ready = sem("probT_ready")
        pv_done = sem("pv_done")
        att_y = sem("att_y")

        h_full_pairs = h_full[:].rearrange("p a (q c) -> p (a q) c", c=CHUNKS)
        square_pairs = squares[:].rearrange("p a (q c) -> p (a q) c", c=CHUNKS)

        def column(name, i=0):
            c = COL[name] + i
            return cols[:, c:c + 1]

        def table(name):
            return tabs[:, TAB[name]:TAB[name] + dict(_TABLES)[name]]

        even_mem = ExitStack()
        v = sb("v", [P, TT, HALF], F32, even_mem)
        qT = sb("qT", [P, HT, S], F32, even_mem)
        kT = sb("kT", [P, HT, S], F32, even_mem)
        qk_mem = ExitStack()
        qk = sb("qk", [P, 2, TT, HALF], F32, qk_mem)
        qk_mem.close()
        y_att_hi = sb("y_att_hi", [P, HT, S], F32R, even_mem)
        y_att_lo = sb("y_att_lo", [P, HT, S], F32R, even_mem)
        qk_var = sb("qk_var", [P, 2, TT * HEADS], F32, even_mem)
        rope_tmp = sb("rope_tmp", [P, 4, TT, HEADS, ROPE], F32, even_mem)
        ga = sb("ga", [P, HT, P], F32, even_mem)
        gx = sb("gx", [P, HT, P], F32, even_mem)
        lam_tmp = sb("lam_tmp", [P, 6, HT], F32, even_mem)
        neg_c = sb("neg_c", [P, HT], F32, even_mem)
        pos_c = sb("pos_c", [P, HT], F32, even_mem)
        row_max = sb("row_max", [P, 2, 2], F32, even_mem)
        neg_max = sb("neg_max", [P, 2, 2], F32, even_mem)
        row_sum = sb("row_sum", [P, 2, 2], F32, even_mem)
        row_inv = sb("row_inv", [P, 2, 2], F32, even_mem)
        lru_mem = ExitStack()
        xc = sb("xc", [P, HT, S], F32, lru_mem)
        rg = sb("rg", [P, HT, S], F32, lru_mem)
        ig = sb("ig", [P, HT, S], F32, lru_mem)
        decay = sb("decay", [P, HT, S], F32, lru_mem)
        coef = sb("coef", [P, HT, S], F32, lru_mem)
        gg = sb("gg", [P, HT, S], F32, lru_mem)
        lru_mem.close()
        att_mem = ExitStack()
        prob = sb("prob", [P, 2, 2, S], F32, att_mem)
        probT = sb("probT", [P, 2, 2, S], F32, att_mem)
        y_lru_hi = sb("y_lru_hi", [P, HT, S], F32R, att_mem)
        y_lru_lo = sb("y_lru_lo", [P, HT, S], F32R, att_mem)
        att_mem.close()
        prep_mem = ExitStack()
        turns = sb("turns", [P, PAIRS, ANGLES], F32, prep_mem)
        rot_s = sb("rot_s", [P, PAIRS, ANGLES], F32, prep_mem)
        rot_c = sb("rot_c", [P, PAIRS, ANGLES], F32, prep_mem)
        small = sb("small", [P, 18, PAIRS], F32, prep_mem)
        mag = sb("mag", [P, PAIRS, POWERS], F32, prep_mem)
        pow_r = sb("pow_r", [P, PAIRS, POWERS], F32, prep_mem)
        pow_i = sb("pow_i", [P, PAIRS, POWERS], F32, prep_mem)
        s5p = sb("s5p", [P, S5_COLS], F32, prep_mem)
        bb = sb("bb", [P, 4, PAIRS, GP], F32, prep_mem)
        b_mat = sb("b_mat", [P, 2, PAIRS, CH, GP], F32, prep_mem)
        t_mat = sb("t_mat", [P, 2, PAIRS, CH, GP], F32, prep_mem)
        stage_w1 = kT
        stage_v = qT[:, 0, :].rearrange("p (q e c) -> p q e c", q=PAIRS, e=2)
        stage_zero = qT[:, 1, :]
        prep_mem.close()
        even_mem.close()

        odd_mem = ExitStack()
        e_pos = sb("e_pos", [P, 2, S], F32, odd_mem)
        e_neg = sb("e_neg", [P, 2, S], F32, odd_mem)
        logs = sb("logs", [P, 2, S], F32, odd_mem)
        vg_mem = ExitStack()
        vg = sb("vg", [P, TT, HALF], F32, vg_mem)
        vg_mem.close()
        y_gla_hi = sb("y_gla_hi", [P, GH, S], F32R, odd_mem)
        sg = sb("sg", [P, TT, HALF], F32, odd_mem)
        gkw = sb("gkw", [16, 2 * P], F32, odd_mem)
        chunk_decay = sb("chunk_decay", [P, 2, GN], F32, odd_mem)
        gla_var = sb("gla_var", [P, TT * GH], F32, odd_mem)
        m8 = sb("m8", [P, PAIRS], F32, odd_mem)
        s5_mem = ExitStack()
        wst = sb("wst", [P, 2, PAIRS, P], F32, s5_mem)
        w3 = sb("w3", [P, 2 * PAIRS, CH * GP], F32, s5_mem)
        rot = sb("rot", [P, 2, PAIRS, CHUNKS], F32, s5_mem)
        u_in = sb("u_in", [P, 2 * PAIRS, CHUNKS], F32, s5_mem)
        u = sb("u", [P, HT, CH, CHUNKS], F32, s5_mem)
        st = sb("st", [P, 3, PAIRS, CHUNKS], F32, s5_mem)
        s5_mem.close()
        gla_mem = ExitStack()
        attT = sb("attT", [P, GH, S], F32, gla_mem)
        state = sb("state", [P, GN, 2, DV], F32, gla_mem)
        o = sb("o", [P, TT, HALF], F32, gla_mem)
        k_end = sb("k_end", [P, 2, S], F32, gla_mem)
        sb("beside_w3", [P, 2, S], F32, gla_mem)
        y_s5_hi = sb("y_s5_hi", [P, HT, S], F32R, gla_mem)
        sb("at_u_in", [P, HT, S], F32, gla_mem)
        y_s5_lo = sb("y_s5_lo", [P, HT, S], F32R, gla_mem)
        gla_mem.close()
        out_mem = ExitStack()
        y_gla_lo = sb("y_gla_lo", [P, GH, S], F32R, out_mem)
        out_mem.close()
        odd_mem.close()

        def scratch(name, shape):
            return nc.dram_tensor(name, shape, F32, kind="Internal").ap()

        w1_dram = scratch("w1_dram", [P, 2 * PAIRS * P])
        w2_dram = scratch("w2_dram", [P, 2 * PAIRS * P])
        k_dram = scratch("k_dram", [GP, 2 * PAIRS, 2 * CH - 1, GP])
        rot_dram = scratch("rot_dram", [P, 2, PAIRS, CHUNKS])
        m8_dram = scratch("m8_dram", [P, PAIRS])
        u_dram = scratch("u_dram", [HT, P, CH, CHUNKS])
        y_dram = scratch("y_dram", [2 * PAIRS, GP, CH, CHUNKS])

        mlp_mem = ExitStack()
        g_hi = sb("g_hi", [P, FT, S], F32R, mlp_mem)
        g_lo = sb("g_lo", [P, FT, S], F32R, mlp_mem)
        conv = sb("conv", [P, 2, S], F32, mlp_mem)
        gelu = sb("gelu", [P, 2, S], F32, mlp_mem)
        gate = h_full
        a_scaled = squares
        mlp_mem.close()

        order = [p for p in range(4) if p in parts]
        stage_of = {p: n for n, p in enumerate(order)}
        first_unit = {1: FIRST_MLP, 3: SECOND_MLP}
        stream = []
        for p in order:
            lo, hi = [(0, FIRST_MLP), (FIRST_MLP, O_U), (O_U, SECOND_MLP), (SECOND_MLP, N_UNITS)][p]
            stream += range(lo, hi)
        assert stream == list(range(stream[0], stream[-1] + 1))
        first = stream[0]
        n_stream = len(stream)

        def rms_after(stage):
            return sum(2 - p % 2 for p in order[:stage + 1])

        block = ctx.enter_context(nc.Block())

        @block.sync
        def _(sp):
            sp.dma_start(cols[:], columns).then_inc(inputs_in, 16)
            xt = xT.rearrange("(k p) t -> k p t", p=P)
            ot = outT.rearrange("(k p) t -> k p t", p=P)
            sp.dma_start(x[:, 0, :], xt[0]).then_inc(x_in[0], 16)
            sp.dma_start(raw[:, 0, :], units[first]).then_inc(landed[0], 16)
            for k in range(1, KT):
                sp.dma_start(x[:, k, :], xt[k]).then_inc(x_in[k], 16)
            sp.dma_start(tabs[:], tables).then_inc(inputs_in, 16)
            if 2 in order:
                sp.dma_start(s5p[:], s5).then_inc(s5_in, 16)
            if 0 in order:
                sp.dma_start(ga[:], gates_a).then_inc(even_in, 16)
                sp.dma_start(gx[:], gates_x).then_inc(even_in, 16)

            def load(n, slot):
                return sp.dma_start(raw[:, slot, :], units[first + n]).then_inc(landed[slot], 16)

            for n in range(1, RAW_SLOTS):
                load(n, n)
            rounds = n_stream // RAW_SLOTS
            with sp.Fori(1, rounds) as r:
                for slot in range(RAW_SLOTS):
                    sp.wait_ge(split, (r - 1) * RAW_SLOTS + slot + 1)
                    sp.dma_start(raw[:, slot, :], units[bass.ds(first + r * RAW_SLOTS + slot, 1), :, :]
                                 .rearrange("a p n -> (a p) n")).then_inc(landed[slot], 16)
            for n in range(rounds * RAW_SLOTS, n_stream):
                sp.wait_ge(split, n - RAW_SLOTS + 1)
                load(n, n % RAW_SLOTS)
            for k in range(KT):
                sp.wait_ge(x_ready, KT * (len(order) - 1) + k + 1)
                sp.dma_start(ot[k], x[:, k, :]).then_inc(out_stored, 16)
            sp.wait_ge(out_stored, 16 * KT)

        @block.gpsimd
        def _(pool):
            pool.memset(ones[:], 1.0).then_inc(consts_set, 1)
            pool.memset(eps[:], EPS).then_inc(consts_set, 1)
            pool.memset(zero[:], 0.0).then_inc(consts_set, 1)
            pool.wait_ge(consts_set, 3)

            def halves(slot, half, done):
                pool.tensor_tensor(w_hi[:, half, :], raw[:, slot, :], zero[:, 0:1].to_broadcast([P, UNIT]), ALU.add).then_inc(hi_split, 1)
                pool.wait_ge(hi_split, done)
                pool.tensor_tensor(w_lo[:, half, :], raw[:, slot, :], w_hi[:, half, :].bitcast(F32),
                                   ALU.subtract).then_inc(split, 1)

            def one(n):
                pool.wait_ge(landed[n % RAW_SLOTS], 16 * (n // RAW_SLOTS + 1))
                if n >= SPLIT_SLOTS:
                    pool.wait_ge(used, n - SPLIT_SLOTS + 1)
                halves(n % RAW_SLOTS, n % SPLIT_SLOTS, n + 1)

            for n in range(RAW_SLOTS):
                one(n)
            rounds = n_stream // RAW_SLOTS
            with pool.Fori(1, rounds) as r:
                for slot in range(RAW_SLOTS):
                    pool.wait_ge(landed[slot], r * 16 + 16)
                    pool.wait_ge(used, r * RAW_SLOTS + (slot - SPLIT_SLOTS + 1))
                    halves(slot, slot % SPLIT_SLOTS, r * RAW_SLOTS + (slot + 1))
            for n in range(rounds * RAW_SLOTS, n_stream):
                one(n)

        @block.tensor
        def _(pe):
            def sum_squares(stage, mixer):
                pe.wait_ge(added, KT * (stage + 1))
                pe.matmul(bank[6][:], ones[:], total[:], start=True, stop=True).then_inc(summed, 1)
                if mixer:
                    for t in range(TT):
                        mm = pe.matmul(bank[7][:, t:t + 1], total[:, t * P:(t + 1) * P], ones[:, 0:1], start=True, stop=True)
                    mm.then_inc(summed, 1)

            def product(out, slot, b, w_at, mov_hi, mov_lo, start, stop):
                hi, lo = w_hi[:, slot, w_at], w_lo[:, slot, w_at]
                pe.matmul(out, hi, mov_hi, start=start, stop=False)
                pe.matmul(out, hi, mov_lo, start=False, stop=False)
                return pe.matmul(out, lo, mov_hi, start=False, stop=stop)

            def w_block(b):
                return slice(b * P, (b + 1) * P)

            def mlp(stage, n0):
                base = FT * (stage // 2 if len(order) == 4 else 0)

                def up(i, u, wait_h):
                    for which, free in enumerate((scaled, gate_raw)):
                        slot = (n0 + which) % SPLIT_SLOTS
                        pe.wait_ge(split, i * 4 + (n0 + 2 * u + which + 1))
                        if not wait_h:
                            pe.wait_ge(free, i * 2 + (base + u - 1))
                        for k in range(KT):
                            if wait_h and u == 0 and which == 0:
                                pe.wait_ge(h_ready, KT * stage + k + 1)
                            mm = product(bank[2 * which + u][:], slot, k, w_block(k), h_hi[:, k, :], h_lo[:, k, :],
                                         k == 0, k == KT - 1)
                        mm.then_inc(used, 1)
                        if wait_h and u == 0 and which == 0:
                            sum_squares(stage, False)

                for u in range(2):
                    up(0, u, True)
                with pe.Fori(1, FT // 2) as i:
                    for u in range(2):
                        up(i, u, False)
                n1 = n0 + 2 * FT
                project(stage, n1, 3, lambda k: (g_hi[:, k, :], g_lo[:, k, :]), lambda k: pe.wait_ge(gate_ready, base + k + 1))

            def project(stage, n1, per_tile, y, wait_y):
                def tile(i, u, first_time):
                    for part in range(per_tile):
                        n = n1 + per_tile * u + part
                        pe.wait_ge(split, i * (2 * per_tile) + (n + 1))
                        if part == 0 and not first_time:
                            pe.wait_ge(x_ready, i * 2 + (KT * stage + u - 1))
                        for b in range(8):
                            k = part * 8 + b
                            if first_time and u == 0:
                                wait_y(k)
                            mm = product(bank[4 + u][:], n % SPLIT_SLOTS, b, w_block(b), *y(k),
                                         k == 0, k == 8 * per_tile - 1)
                        mm.then_inc(used, 1)

                for u in range(2):
                    tile(0, u, True)
                with pe.Fori(1, KT // 2) as i:
                    for u in range(2):
                        tile(i, u, False)

            def rows_unit(n, part, banks, stage, first_time):
                pe.wait_ge(split, n + 1)
                slot = n % SPLIT_SLOTS
                for b in range(2):
                    k = 2 * part + b
                    if first_time:
                        pe.wait_ge(h_ready, KT * stage + k + 1)
                    cols_ = slice(b * 512, (b + 1) * 512)
                    for t in range(TT):
                        out, at = bank[banks + t][:], slice(t * P, (t + 1) * P)
                        pe.matmul(out, h_hi[:, k, at], w_hi[:, slot, cols_], start=(k == 0), stop=False)
                        pe.matmul(out, h_hi[:, k, at], w_lo[:, slot, cols_], start=False, stop=False)
                        mm = pe.matmul(out, h_lo[:, k, at], w_hi[:, slot, cols_], start=False, stop=(k == KT - 1))
                mm.then_inc(used, 1)

            def tile_unit(n, b_out, stage, first_time=False):
                pe.wait_ge(split, n + 1)
                for k in range(KT):
                    if first_time:
                        pe.wait_ge(h_ready, KT * stage + k + 1)
                    mm = product(bank[b_out][:], n % SPLIT_SLOTS, k, w_block(k), h_hi[:, k, :], h_lo[:, k, :],
                                 k == 0, k == KT - 1)
                mm.then_inc(used, 1)

            def s5_prepare():
                pe.wait_ge(s5_bmat, BMAT_STEPS)
                nci = bb[:, 3]
                cr = s5p[:, 3 * PAIRS + 2 * PAIRS * GP:3 * PAIRS + 3 * PAIRS * GP].rearrange("p (q c) -> p q c", c=GP)
                for q in range(PAIRS):
                    for e in range(2):
                        rows = slice(64 * e, 64 * e + 64)
                        out = bank[4 + e][:, q * GP:(q + 1) * GP]
                        pe.matmul(out, b_mat[rows, 0, q].rearrange("p l c -> p (l c)"), cr[rows, q], start=True, stop=False)
                        mm = pe.matmul(out, b_mat[rows, 1, q].rearrange("p l c -> p (l c)"), nci[rows, q], start=False, stop=True)
                mm.then_inc(s5_prep_mm, 1)
                for n in range(8):
                    if n >= 2:
                        pe.wait_ge(s5_w1_out, n - 1)
                    for i in range(4):
                        q = 4 * n + i
                        mm = pe.transpose(bank[6 + n % 2][:, i * P:(i + 1) * P],
                                          b_mat[:, q // PAIRS, q % PAIRS].rearrange("p l c -> p (l c)"), table("identity"))
                    mm.then_inc(s5_prep_mm, 1)
                pe.wait_ge(s5_v_out, 2)
                pe.wait_ge(s5_w1_out, 8)

            def odd_mixer(stage):
                n0 = O_U - first
                if 0 not in order:
                    s5_prepare()
                tile_unit(n0, 0, stage, True)
                sum_squares(stage, True)
                for m in range(1, HT):
                    tile_unit(n0 + m, m, stage)
                tile_unit(O_GK - first, 4, stage)
                pe.wait_ge(rms_ready, rms_after(stage))
                pe.wait_ge(gk_ready, 1)
                pe.wait_ge(gk_in, 16)
                for i in range(2):
                    pe.matmul(bank[5 + i][:], gkw[:, i * P:(i + 1) * P], squares[0:16, 0, :], start=True,
                              stop=True).then_inc(gate_pre, 1)
                tile_unit(O_Q - first, 7, stage)
                tile_unit(O_Q - first + 1, 4, stage)
                pe.wait_ge(gk_logs, 2)
                tile_unit(O_K - first, 5, stage)
                tile_unit(O_K - first + 1, 6, stage)

                pe.wait_ge(u_ready, HT)
                pe.wait_ge(u_loaded, 16 * CH)
                pe.wait_ge(s5_loaded, 16)
                for ri in range(2):
                    for q in range(PAIRS):
                        for e in range(2):
                            mm = pe.matmul(bank[2 * ri + q // 8][64 * e:64 * e + 64, q % 8 * CHUNKS:(q % 8 + 1) * CHUNKS],
                                           wst[:, ri, q, 64 * e:64 * e + 64], u_in[:, 2 * q + e, :], start=True, stop=True)
                mm.then_inc(s5_local, 1)

                pe.wait_ge(gk_dec, 4)
                for part in range(4):
                    rows_unit(O_V - first + part, part, 4, stage, False)
                pe.wait_ge(s5_step, 4)
                for part in range(4):
                    rows_unit(O_G - first + part, part, 0, stage, False)

                pe.wait_ge(vg_ready, TT)
                pe.wait_ge(w3_in, 16 * CH)
                pe.wait_ge(s5_w2_loaded, 16)
                pe.wait_ge(s5_step, S5_STEPS)
                for e in range(2):
                    for half in range(2):
                        for q in range(8 * half, 8 * half + 8):
                            out = bank[4 + 2 * e + half][:, q % 8 * CHUNKS:(q % 8 + 1) * CHUNKS]
                            rows = slice(64 * e, 64 * e + 64)
                            pe.matmul(out, w3[:, 2 * q + e, :], u_in[:, 2 * q + e, :], start=True, stop=False)
                            pe.matmul(out, wst[rows, 0, q, :], st[rows, 2, q, :], start=False, stop=False)
                            mm = pe.matmul(out, wst[rows, 1, q, :], h_full_pairs[rows, q, :], start=False, stop=True)
                        mm.then_inc(s5_y_ready, 1)

                pe.wait_ge(sg_ready, TT)
                pe.wait_ge(gk_dec, 6)
                for i in range(2):
                    for t in range(TT):
                        mm = pe.transpose(bank[i][:, t * P:(t + 1) * P], logs[:, i, t * P:(t + 1) * P], table("identity"))
                    mm.then_inc(k_turned, 1)
                for h in range(GH):
                    b = (2, 3, 0, 1)[h]
                    if h >= 2:
                        pe.wait_ge(k_end_ready, 2)
                    rows = slice(64 * (h % 2), 64 * (h % 2) + 64)
                    for t in range(TT):
                        at = slice(t * P, (t + 1) * P)
                        mm = pe.matmul(bank[b][:, at], e_neg[rows, h // 2, at], e_pos[rows, h // 2, at], start=True, stop=True)
                    mm.then_inc(att_ready, 1)
                pe.wait_ge(s5_y_out, 4)
                for n in range(GN - 1):
                    rows = slice(64 * (n % 2), 64 * (n % 2) + 64)
                    for h in range(GH):
                        col = (n // 2 % 2) * 256 + (h // 2) * DV
                        mm = pe.matmul(bank[4 + 2 * (n % 2) + n // 4][64 * (h % 2):64 * (h % 2) + 64, col:col + DV],
                                       k_end[rows, h // 2, n // 2 * P + 64 * (h % 2):n // 2 * P + 64 * (h % 2) + 64],
                                       vg[rows, n // 2, h * DV:(h + 1) * DV], start=True, stop=True)
                    mm.then_inc(kv_ready, 1)
                pe.wait_ge(attT_ready, GH)
                for t in range(TT):
                    for h in range(GH):
                        mm = pe.matmul(bank[t][:, h * DV:(h + 1) * DV], attT[:, h, t * P:(t + 1) * P],
                                       vg[:, t, h * DV:(h + 1) * DV], start=True, stop=True)
                    mm.then_inc(intra_ready, 1)
                pe.wait_ge(state_step, 1 + 2 * (GN - 1))
                for t in range(TT):
                    for e in range(2):
                        for n in (2 * t, 2 * t + 1):
                            for i in range(2):
                                rows = slice(64 * e, 64 * e + 64)
                                col = (t % 2) * 256 + i * DV
                                mm = pe.matmul(bank[4 + 2 * e + t // 2][64 * (n % 2):64 * (n % 2) + 64, col:col + DV],
                                               e_pos[rows, i, n * GC:(n + 1) * GC], state[rows, n, i, :],
                                               start=True, stop=True)
                    mm.then_inc(inter_ready, 1)

                pe.wait_ge(o_ready, TT)
                pe.wait_ge(ys_split, 2)
                for part in range(2):
                    n = O_GLU - first + part
                    pe.wait_ge(split, n + 1)
                    for b in range(8):
                        m, k = 2 * part + b // HT, b % HT
                        mm = product(bank[m][:], n % SPLIT_SLOTS, b, w_block(b), h_hi[:, k, :], h_lo[:, k, :], k == 0, k == HT - 1)
                    mm.then_inc(used, 1)
                pe.wait_ge(o_step, 2)
                for h in range(GH):
                    for t in range(TT):
                        mm = pe.transpose(bank[4 + h][:, t * P:(t + 1) * P], o[:, t, h * P:(h + 1) * P], table("identity"))
                    mm.then_inc(o_turned, 1)
                pe.wait_ge(gla_y, 2 * GH)
                project(stage, O_O - first, 1, lambda k: (y_s5_hi[:, k, :], y_s5_lo[:, k, :]) if k < HT
                        else (y_gla_hi[:, k - HT, :], y_gla_lo[:, k - HT, :]), lambda k: pe.wait_ge(s5_out, 1))

            def even_mixer(stage):
                for part in range(4):
                    rows_unit(E_Q + part, part, 0, stage, True)
                    if part == 2:
                        sum_squares(stage, True)
                pe.wait_ge(rms_ready, 2)
                for part in range(4):
                    rows_unit(E_K + part, part, 4, stage, False)
                pe.wait_ge(qk_step, 4)
                for part in range(4):
                    rows_unit(E_V + part, part, 0, stage, False)
                pe.wait_ge(qk_step, 8)
                if 2 in order:
                    s5_prepare()
                for m in range(HT):
                    tile_unit(E_X + m, 4 + m, stage)
                pe.wait_ge(v_ready, TT)
                for m in range(HT):
                    tile_unit(E_G + m, m, stage)
                pe.wait_ge(even_in, 32)
                for m in range(HT):
                    if m == 0:
                        pe.wait_ge(x_conv, 3 * HT)
                    if m >= 2:
                        pe.wait_ge(gate_sig, 2 * m - 2)
                    b = 4 + 2 * (m % 2)
                    pe.matmul(bank[b][:], ga[:, m, :], xc[:, m, :], start=True, stop=True).then_inc(gates_made, 1)
                    pe.matmul(bank[b + 1][:], gx[:, m, :], xc[:, m, :], start=True, stop=True).then_inc(gates_made, 1)
                pe.wait_ge(gate_sig, 2 * HT)
                pe.wait_ge(qk_step, QK_STEPS)
                for n in range(2 * HT):
                    which, hp = n // HT, n % HT
                    if n >= 4:
                        pe.wait_ge(qkT_ready, n - 3)
                    for t in range(TT):
                        mm = pe.transpose(bank[4 + n % 4][:, t * P:(t + 1) * P],
                                          qk[:, which, t, hp * P:(hp + 1) * P], table("identity"))
                    mm.then_inc(qk_turned, 1)

                def scores(n):
                    hp, t = divmod(n, TT)
                    if n >= 2:
                        pe.wait_ge(masked, 2 * (n - 1))
                    for e in range(2):
                        rows = slice(64 * e, 64 * e + 64)
                        mm = pe.matmul(bank[2 * e + n % 2][:, 0:(t + 1) * P], qT[rows, hp, t * P:(t + 1) * P],
                                       kT[rows, hp, 0:(t + 1) * P], start=True, stop=True)
                    mm.then_inc(scores_ready, 1)

                def turn(n):
                    t = n % TT
                    pe.wait_ge(probs_ready, 2 * n + 2)
                    if n >= 1:
                        pe.wait_ge(probT_ready, 2 * n)
                    for e in range(2):
                        for j in range(t + 1):
                            mm = pe.transpose(bank[4 + e][:, j * P:(j + 1) * P], prob[:, n % 2, e, j * P:(j + 1) * P],
                                              table("identity"))
                    mm.then_inc(probs_turned, 1)

                def values(n):
                    hp, t = divmod(n, TT)
                    pe.wait_ge(probT_ready, 2 * n + 2)
                    if t == 0 and hp >= 2:
                        pe.wait_ge(att_y, 2 * (hp - 1))
                    for e in range(2):
                        head = 2 * hp + e
                        for j in range(t + 1):
                            mm = pe.matmul(bank[6 + hp % 2][64 * e:64 * e + 64, t * P:(t + 1) * P],
                                           v[:, j, head * HD:(head + 1) * HD], probT[:, n % 2, e, j * P:(j + 1) * P],
                                           start=(j == 0), stop=(j == t))
                    mm.then_inc(pv_done, 1)

                pe.wait_ge(gl_scaled, HT)
                pe.wait_ge(qkT_ready, 2 * HT)
                scores(0)
                scores(1)
                for n in range(ATT_STEPS):
                    turn(n)
                    if n + 2 < ATT_STEPS:
                        scores(n + 2)
                    values(n)
                project(stage, E_O, 1, lambda k: (y_lru_hi[:, k, :], y_lru_lo[:, k, :]) if k < HT
                        else (y_att_hi[:, k - HT, :], y_att_lo[:, k - HT, :]),
                        lambda k: pe.wait_ge(*((lru_y, 1) if k < HT else (att_y, 2 * (k - HT) + 2))))

            pe.wait_ge(consts_set, 3)
            for stage, part in enumerate(order):
                if part == 0:
                    even_mixer(stage)
                if part == 2:
                    odd_mixer(stage)
                if part in (1, 3):
                    mlp(stage, first_unit[part] - first)

        @block.scalar
        def _(act):
            def gain_tile(stage, k, u):
                xk = x[:, bass.ds(k, 1), :].rearrange("p a t -> p (a t)")
                hk = h_hi[:, bass.ds(k, 1), :].rearrange("p a t -> p (a t)")
                act.activation(hk, xk, ACT.Identity, bias=zero[:, 0:1],
                               scale=cols[:, bass.ds(COL["norm"] + KT * order[stage] + k, 1)]).then_inc(gained_hi, 1)
                act.activation(squares[:, u, :], xk, ACT.Square).then_inc(squared, 1)

            def take_x():
                act.wait_ge(consts_set, 3)
                act.wait_ge(inputs_in, 16)
                for k in range(KT):
                    act.wait_ge(x_in[k], 16)
                    if k >= 2:
                        act.wait_ge(added, k - 1)
                    gain_tile(0, k, k % 2)

            def take_residual(stage):
                def tile(i, u, warm):
                    act.wait_ge(x_ready, i * 2 + (KT * stage + u + 1))
                    if warm:
                        act.wait_ge(added, i * 2 + (KT * (stage + 1) + u - 1))
                    gain_tile(stage + 1, i * 2 + u, u)

                for u in range(2):
                    tile(0, u, False)
                with act.Fori(1, KT // 2) as i:
                    for u in range(2):
                        tile(i, u, True)

            def find_rms(stage, mixer):
                act.wait_ge(summed, rms_after(stage) - mixer)
                act.activation(rstd[:], bank[6][:], ACT.Sqrt, bias=eps[:, 0:1], scale=1.0 / D).then_inc(rms_ready, 1)
                if mixer:
                    act.wait_ge(summed, rms_after(stage))
                    act.activation(rstd_t[:], bank[7][:, 0:TT], ACT.Sqrt, bias=eps[:, 0:1], scale=1.0 / D).then_inc(rms_ready, 1)

            def mlp(stage, layer, n0):
                base = FT * (stage // 2 if len(order) == 4 else 0)

                def tile(i, u, warm):
                    j = i * 2 + u
                    act.wait_ge(scaled, i * 2 + (base + u + 1))
                    if warm:
                        act.wait_ge(gelu_done, i * 2 + (base + u - 1))
                    w = COL["mlp_w"] + layer * 3 * FT + 2 * FT
                    b = COL["mlp_b"] + layer * FT
                    act.activation(conv[:, u, :], a_scaled[:, u, :], ACT.Identity,
                                   bias=cols[:, bass.ds(b + j, 1)], scale=cols[:, bass.ds(w + j, 1)]).then_inc(newest_tap, 1)
                    act.wait_ge(conv_done, i * 2 + (base + u + 1))
                    if warm:
                        act.wait_ge(gate_done, i * 2 + (base + u - 1))
                    act.activation(gelu[:, u, :], conv[:, u, :], ACT.Gelu_apprx_tanh).then_inc(gelu_done, 1)

                for u in range(2):
                    tile(0, u, False)
                with act.Fori(1, FT // 2) as i:
                    for u in range(2):
                        tile(i, u, True)

            def s5_phases():
                act.wait_ge(s5_in, 16)
                act.activation(small[:, 0], s5p[:, 2 * PAIRS:3 * PAIRS], ACT.Exp).then_inc(s5_exp, 1)
                act.wait_ge(s5_small, MAG_STEP)
                act.activation(mag[:], mag[:], ACT.Exp).then_inc(s5_exp, 1)
                act.wait_ge(s5_small, TURN_STEPS)
                act.activation(rot_s[:], turns[:], ACT.Sin, scale=TWO_PI).then_inc(s5_sin, 1)
                act.activation(rot_c[:], turns[:], ACT.Sin, scale=TWO_PI / 2).then_inc(s5_sin, 1)

            def s5_prepare():
                act.wait_ge(s5_small, PHASE_STEPS)
                act.dma_start(rot_dram[:, 0], rot_c[:, :, POWERS:ANGLES]).then_inc(s5_rot_stored, 16)
                act.dma_start(rot_dram[:, 1], rot_s[:, :, POWERS:ANGLES]).then_inc(s5_rot_stored, 16)
                act.wait_ge(s5_exp, 2)
                act.activation(small[:, 16], mag[:, :, CH], ACT.Copy).then_inc(s5_exp, 1)
                act.wait_ge(s5_exp, 3)
                act.dma_start(m8_dram, small[:, 16]).then_inc(s5_stored, 16)
                act.wait_ge(s5_prep_mm, 1)
                for e in range(2):
                    act.activation(stage_v[:, :, e, :], bank[4 + e][:, 0:PAIRS * GP].rearrange("p (q c) -> p q c", c=GP),
                                   ACT.Copy).then_inc(s5_v_out, 1)
                act.wait_ge(s5_v_out, 2)
                for e in range(CH):
                    act.dma_start(k_dram[:, :, CH - 1 + e, :], stage_v[e * GP:(e + 1) * GP].rearrange("p q e c -> p (q e) c"))\
                       .then_inc(s5_stored, 16)
                zeros = GP * (CH - 1)
                act.wait_ge(w3_zero, 1)
                act.dma_start(k_dram.rearrange("p (a b) k c -> (p a) b (k c)", b=4)[:, :, 0:zeros],
                              stage_zero[:, 0:4 * zeros].rearrange("p (b n) -> p b n", b=4)).then_inc(s5_stored, 16)
                for n in range(8):
                    act.wait_ge(s5_prep_mm, n + 2)
                    slot = n % W1_SLOTS
                    if n >= W1_SLOTS:
                        act.wait_ge(s5_w1_stored[slot], 16)
                    act.activation(stage_w1[:, slot, :], bank[6 + n % 2][:], ACT.Copy).then_inc(s5_w1_out, 1)
                    act.wait_ge(s5_w1_out, n + 1)
                    act.dma_start(w1_dram[:, n * 512:(n + 1) * 512], stage_w1[:, slot, :]).then_inc(s5_w1_stored[slot], 16)

            def s5_store_output():
                act.wait_ge(s5_bmat, CMAT_STEPS)
                act.dma_start(w2_dram, b_mat[:].rearrange("p r q l c -> p (r q l c)")).then_inc(s5_stored, 16)

            def odd_mixer(stage):
                if 0 not in order:
                    s5_prepare()
                    s5_store_output()
                act.wait_ge(s5_stored, 16 * S5_STORES)
                act.wait_ge(s5_rot_stored, 32)
                for slot in range(W1_SLOTS):
                    act.wait_ge(s5_w1_stored[slot], 32)
                act.dma_start(gkw[:], gk_w).then_inc(gk_in, 16)
                act.dma_start(wst[:].rearrange("p r q n -> p (r q n)"), w1_dram).then_inc(s5_loaded, 16)
                act.dma_start(rot[:], rot_dram).then_inc(s5_rot_in, 16)
                act.dma_start(m8[:], m8_dram).then_inc(s5_rot_in, 16)
                find_rms(stage, 1)
                for m in range(HT):
                    act.wait_ge(u_ready, m + 1)
                    act.dma_start(u_dram[m], u[:, m]).then_inc(u_stored, 16)
                act.wait_ge(u_stored, 16 * HT)
                ud = u_dram.rearrange("m (g p) l c -> p (m g) l c", p=GP)
                for e in range(CH):
                    act.dma_start(u_in[e * GP:(e + 1) * GP], ud[:, :, CH - 1 - e, :]).then_inc(u_loaded, 16)
                for e in range(CH):
                    act.dma_start(w3[e * GP:(e + 1) * GP], k_dram[:, :, e:e + CH, :].rearrange("p g k c -> p g (k c)"))\
                       .then_inc(w3_in, 16)
                act.wait_ge(gk_logs, 2)
                act.activation(e_pos[:], logs[:], ACT.Abs).then_inc(gk_abs, 1)
                act.wait_ge(gk_abs, 1)
                act.activation(e_pos[:], e_pos[:], ACT.Exp, scale=-1.0).then_inc(gk_abs, 1)
                act.wait_ge(gk_abs, 2)
                act.activation(e_pos[:], e_pos[:], ACT.Ln, bias=ones[:, 0:1]).then_inc(gk_abs, 1)
                act.wait_ge(gk_sum, 3)
                act.activation(e_pos[:], logs[:], ACT.Exp, scale=1.0 / 16).then_inc(gk_exp, 1)
                act.activation(e_neg[:], logs[:], ACT.Exp, scale=-1.0 / 16).then_inc(gk_exp, 1)
                act.wait_ge(s5_local, 1)
                act.dma_start(wst[:].rearrange("p r q n -> p (r q n)"), w2_dram).then_inc(s5_w2_loaded, 16)
                act.wait_ge(used, O_V - first + 4)
                for t in range(TT):
                    act.activation(vg[:, t, :], bank[4 + t][:], ACT.Identity, bias=zero[:, 0:1],
                                   scale=rstd_t[:, t:t + 1]).then_inc(vg_ready, 1)
                act.wait_ge(used, O_G - first + 4)
                for t in range(TT):
                    act.activation(sg[:, t, :], bank[t][:], ACT.Silu, scale=rstd_t[:, t:t + 1]).then_inc(sg_ready, 1)
                act.wait_ge(k_turned, 2)
                for i in range(2):
                    act.activation(k_end[:, i, :], bank[i][:], ACT.Copy).then_inc(k_end_ready, 1)
                for e in range(2):
                    for half in range(2):
                        n = 2 * e + half
                        act.wait_ge(s5_y_ready, n + 1)
                        dst = st[:, 0:2].rearrange("p a q c -> p (a q) c")[:, 16 * half + e:16 * half + 16:2, :]
                        act.activation(dst, bank[4 + n][:].rearrange("p (q c) -> p q c", c=CHUNKS), ACT.Copy).then_inc(s5_y_out, 1)
                act.wait_ge(s5_y_out, 4)
                yd = y_dram.rearrange("g p l c -> p g l c")
                for l in range(CH):
                    act.dma_start(yd[:, :, l, :], st[l * GP:(l + 1) * GP, 0:2].rearrange("p a q c -> p (a q) c"))\
                       .then_inc(y_stored, 16)
                act.wait_ge(y_stored, 16 * CH)
                y_in = u_in[:].rearrange("p g c -> p (g c)").rearrange("p (m n) -> p m n", m=HT)
                act.dma_start(y_in, y_dram.rearrange("(m g) p l c -> (g p) m (l c)", m=HT)).then_inc(y_loaded, 16)
                for t in range(TT):
                    act.wait_ge(inter_ready, t // 2 * 2 + 2)
                    for e in range(2):
                        dst = o[:, t, :].rearrange("p (i e d) -> p i e d", i=2, e=2)[:, :, e, :]
                        src = bank[4 + 2 * e + t // 2][:, t % 2 * 256:t % 2 * 256 + 256].rearrange("p (i d) -> p i d", i=2)
                        act.activation(dst, src, ACT.Copy).then_inc(inter_out, 1)
                act.wait_ge(ys_ready, 1)
                act.activation(u_in[:], u_in[:], ACT.Gelu_apprx_tanh).then_inc(ys_gelu, 1)
                for t in range(TT):
                    act.wait_ge(o_ready, t + 1)
                    if t >= 2:
                        act.wait_ge(o_sum, t - 1)
                    act.activation(squares[:, t % 2, :], o[:, t, :], ACT.Square).then_inc(o_squared, 1)
                act.wait_ge(o_sum, TT)
                act.activation(gla_var[:], gla_var[:], ACT.Sqrt, bias=eps[:, 0:1], scale=1.0 / DV).then_inc(o_rms, 1)
                act.wait_ge(used, O_GLU - first + 2)
                sig = st[:, 0:2].rearrange("p a q c -> p (a q c)").rearrange("p (m n) -> p m n", m=HT)
                for m in range(HT):
                    act.activation(sig[:, m], bank[m][:], ACT.Sigmoid, bias=column("glu_b", m)).then_inc(glu_sig, 1)

            def even_mixer(stage):
                find_rms(stage, 1)
                if 2 in order:
                    s5_phases()
                act.wait_ge(lam_step, LAM_ABS)
                act.activation(lam_tmp[:, 0, :], lam_tmp[:, 5, :], ACT.Exp).then_inc(lam_exp, 1)
                act.wait_ge(rstd_ready, 2)
                for which in range(2):
                    act.wait_ge(used, 4 * which + 4)
                    for t in range(TT):
                        n = TT * which + t
                        if n >= 2:
                            act.wait_ge(qk_sum, n - 1)
                        act.activation(squares[:, n % 2, :], bank[4 * which + t][:], ACT.Square,
                                       scale=rstd_t[:, t:t + 1]).then_inc(qk_squared, 1)
                    act.wait_ge(qk_sum, TT * (which + 1))
                    act.activation(qk_var[:, which, :], qk_var[:, which, :], ACT.Sqrt, bias=eps[:, 0:1],
                                   scale=1.0 / HD).then_inc(qk_rms, 1)
                act.wait_ge(used, 12)
                for t in range(TT):
                    act.activation(v[:, t, :], bank[t][:], ACT.Identity, bias=zero[:, 0:1],
                                   scale=rstd_t[:, t:t + 1]).then_inc(v_ready, 1)
                if 2 in order:
                    s5_prepare()
                    act.wait_ge(s5_rot_stored, 32)
                for m in range(HT):
                    act.wait_ge(xl_scaled, m + 1)
                    act.activation(xc[:, m, :], squares[:, m % 2, :], ACT.Identity, bias=column("lru_b", m),
                                   scale=column("lru_w", 3 * HT + m)).then_inc(x_newest, 1)
                if 2 in order:
                    s5_store_output()
                    act.wait_ge(s5_stored, 16 * S5_STORES)
                    for slot in range(W1_SLOTS):
                        act.wait_ge(s5_w1_stored[slot], 32)
                for m in range(HT):
                    b = 4 + 2 * (m % 2)
                    act.wait_ge(gates_made, 2 * m + 1)
                    act.activation(rg[:, m, :], bank[b][:], ACT.Sigmoid, bias=column("gate_a_b", m)).then_inc(gate_sig, 1)
                    act.wait_ge(gates_made, 2 * m + 2)
                    act.activation(ig[:, m, :], bank[b + 1][:], ACT.Sigmoid, bias=column("gate_x_b", m)).then_inc(gate_sig, 1)
                act.wait_ge(gate_sig, 2 * HT)
                act.wait_ge(lam_step, LAM_STEPS)
                for m in range(HT):
                    act.activation(coef[:, m, :], rg[:, m, :], ACT.Tanh, scale=neg_c[:, m:m + 1]).then_inc(lru_exp, 1)
                for m in range(HT):
                    act.activation(decay[:, m, :], rg[:, m, :], ACT.Exp, scale=pos_c[:, m:m + 1]).then_inc(lru_exp, 1)
                act.wait_ge(lru_step, 3)
                act.activation(coef[:], coef[:], ACT.Sqrt, scale=2.0).then_inc(lru_sqrt, 1)
                for m in range(HT):
                    act.wait_ge(gl_scaled, m + 1)
                    act.activation(gg[:, m, :], gg[:, m, :], ACT.Gelu_apprx_tanh).then_inc(gg_ready, 1)
                for n in range(2 * HT):
                    act.wait_ge(qk_turned, n + 1)
                    dst = (qT, kT)[n // HT]
                    act.activation(dst[:, n % HT, :], bank[4 + n % 4][:], ACT.Copy).then_inc(qkT_ready, 1)

                def exps(n):
                    act.wait_ge(negmax_ready, n + 1)
                    w = (n % TT + 1) * P
                    for e in range(2):
                        act.activation(prob[:, n % 2, e, 0:w], prob[:, n % 2, e, 0:w], ACT.Exp,
                                       bias=neg_max[:, n % 2, e:e + 1], scale=HD ** -0.5,
                                       accum_out=row_sum[:, n % 2, e:e + 1]).then_inc(exped, 1)

                def copy_turned(n):
                    w = (n % TT + 1) * P
                    act.wait_ge(probs_turned, n + 1)
                    if n >= 2:
                        act.wait_ge(pv_done, n - 1)
                    for e in range(2):
                        act.activation(probT[:, n % 2, e, 0:w], bank[4 + e][:, 0:w], ACT.Copy).then_inc(probT_ready, 1)

                exps(0)
                for n in range(ATT_STEPS):
                    if n + 1 < ATT_STEPS:
                        exps(n + 1)
                    copy_turned(n)

            take_x()
            if 2 in order and 0 not in order:
                s5_phases()
            for stage, part in enumerate(order):
                if part == 0:
                    even_mixer(stage)
                if part == 2:
                    odd_mixer(stage)
                if part in (1, 3):
                    find_rms(stage, 0)
                    mlp(stage, part // 2, first_unit[part] - first)
                if stage < len(order) - 1:
                    take_residual(stage)

        @block.vector
        def _(dve):
            def low_half(stage, k, gained, u):
                xk = x[:, bass.ds(k, 1), :].rearrange("p a t -> p (a t)")
                hi = h_hi[:, bass.ds(k, 1), :].rearrange("p a t -> p (a t)").bitcast(F32)
                lo = h_lo[:, bass.ds(k, 1), :].rearrange("p a t -> p (a t)")
                dve.wait_ge(gained_hi, gained)
                dve.scalar_tensor_tensor(out=lo, in0=xk, scalar=cols[:, bass.ds(COL["norm"] + KT * order[stage] + k, 1)],
                                         in1=hi, op0=ALU.mult, op1=ALU.subtract).then_inc(h_ready, 1)
                dve.wait_ge(squared, gained)
                dve.tensor_tensor(total[:], total[:], squares[:, u, :], ALU.add).then_inc(added, 1)

            def clear_total(stage):
                dve.memset(total[:], 0.0).then_inc(total_clear, 1)
                dve.wait_ge(total_clear, stage + 1)

            def take_x():
                clear_total(0)
                dve.wait_ge(inputs_in, 16)
                for k in range(KT):
                    if k >= 1:
                        dve.wait_ge(added, k)
                    low_half(0, k, k + 1, k % 2)

            def find_rstd(stage, mixer):
                dve.wait_ge(rms_ready, rms_after(stage) - mixer)
                dve.reciprocal(rstd[:], rstd[:]).then_inc(rstd_ready, 1)
                if mixer:
                    dve.wait_ge(rms_ready, rms_after(stage))
                    dve.reciprocal(rstd_t[:], rstd_t[:]).then_inc(rstd_ready, 1)
                dve.wait_ge(rstd_ready, rms_after(stage))

            def add_residual(stage, n1, per_tile):
                last = stage == len(order) - 1

                def tile(i, u):
                    m = i * 2 + u
                    dve.wait_ge(used, i * (2 * per_tile) + (n1 + per_tile * (u + 1)))
                    xm = x[:, bass.ds(m, 1), :].rearrange("p a t -> p (a t)")
                    dve.tensor_tensor(xm, bank[4 + u][:], xm, ALU.add).then_inc(x_ready, 1)
                    if not last:
                        dve.wait_ge(added, i * 2 + (KT * (stage + 1) + u))
                        low_half(stage + 1, m, i * 2 + (KT * (stage + 1) + u + 1), u)

                if not last:
                    dve.wait_ge(used, n1 + 1)
                    clear_total(stage + 1)
                with dve.Fori(0, KT // 2) as i:
                    for u in range(2):
                        tile(i, u)

            def mlp(stage, layer, n0):
                base = FT * (stage // 2 if len(order) == 4 else 0)

                def tile(i, u):
                    j = i * 2 + u
                    w = COL["mlp_w"] + layer * 3 * FT
                    dve.wait_ge(used, i * 4 + (n0 + 2 * u + 1))
                    dve.tensor_tensor(a_scaled[:, u, :], bank[u][:], rstd[:], ALU.mult).then_inc(scaled, 1)
                    dve.wait_ge(newest_tap, i * 2 + (base + u + 1))
                    dve.scalar_tensor_tensor(out=conv[:, u, 1:S], in0=a_scaled[:, u, 0:S - 1],
                                             scalar=cols[:, bass.ds(w + FT + j, 1)], in1=conv[:, u, 1:S],
                                             op0=ALU.mult, op1=ALU.add).then_inc(middle_tap, 1)
                    dve.wait_ge(middle_tap, i * 2 + (base + u + 1))
                    dve.scalar_tensor_tensor(out=conv[:, u, 2:S], in0=a_scaled[:, u, 0:S - 2],
                                             scalar=cols[:, bass.ds(w + j, 1)], in1=conv[:, u, 2:S],
                                             op0=ALU.mult, op1=ALU.add).then_inc(conv_done, 1)
                    dve.wait_ge(gelu_done, i * 2 + (base + u + 1))
                    dve.wait_ge(used, i * 4 + (n0 + 2 * u + 2))
                    dve.tensor_tensor(gate[:, u, :], bank[2 + u][:], gelu[:, u, :], ALU.mult).then_inc(gate_raw, 1)
                    dve.wait_ge(gate_raw, i * 2 + (base + u + 1))
                    dve.tensor_tensor(gate[:, u, :], gate[:, u, :], rstd[:], ALU.mult).then_inc(gate_done, 1)
                    dve.wait_ge(gate_done, i * 2 + (base + u + 1))
                    gj_hi = g_hi[:, bass.ds(j, 1), :].rearrange("p a t -> p (a t)")
                    gj_lo = g_lo[:, bass.ds(j, 1), :].rearrange("p a t -> p (a t)")
                    dve.tensor_copy(gj_hi, gate[:, u, :]).then_inc(gate_hi_done, 1)
                    dve.wait_ge(gate_hi_done, i * 2 + (base + u + 1))
                    dve.tensor_tensor(gj_lo, gate[:, u, :], gj_hi.bitcast(F32), ALU.subtract).then_inc(gate_ready, 1)

                with dve.Fori(0, FT // 2) as i:
                    for u in range(2):
                        tile(i, u)

            def lru_constants():
                lam = cols[:, COL["lambda"]:COL["lambda"] + HT]
                z, w, w2, acc, neg, tmp = (lam_tmp[:, i, :] for i in range(6))
                step = [0]

                def then(ins):
                    ins.then_inc(lam_step, 1)
                    step[0] += 1
                    dve.wait_ge(lam_step, step[0])

                dve.wait_ge(inputs_in, 32)
                then(dve.tensor_scalar(neg, lam, -1.0, 0.0, ALU.mult, ALU.max))
                then(dve.scalar_tensor_tensor(out=tmp, in0=neg, scalar=-2.0, in1=lam, op0=ALU.mult, op1=ALU.subtract))
                assert step[0] == LAM_ABS
                dve.wait_ge(lam_exp, 1)
                then(dve.tensor_scalar(tmp, z, 2.0, None, ALU.add))
                then(dve.reciprocal(tmp, tmp))
                then(dve.tensor_tensor(w, z, tmp, ALU.mult))
                then(dve.tensor_tensor(w2, w, w, ALU.mult))
                then(dve.tensor_scalar(acc, w2, ATANH[-1], ATANH[-2], ALU.mult, ALU.add))
                for c in ATANH[-3::-1]:
                    then(dve.tensor_tensor(acc, acc, w2, ALU.mult))
                    then(dve.tensor_scalar(acc, acc, c, None, ALU.add))
                then(dve.tensor_tensor(acc, acc, w, ALU.mult))
                then(dve.scalar_tensor_tensor(out=acc, in0=acc, scalar=2.0, in1=neg, op0=ALU.mult, op1=ALU.add))
                then(dve.tensor_scalar(neg_c[:], acc, 8.0, None, ALU.mult))
                then(dve.tensor_scalar(pos_c[:], acc, -8.0, None, ALU.mult))
                assert step[0] == LAM_STEPS

            def s5_phases():
                lr, li = s5p[:, 0:PAIRS], s5p[:, PAIRS:2 * PAIRS]
                step, zr, th, q, f, fh, fl = (small[:, i] for i in range(7))
                done = [0]

                def then(ins):
                    ins.then_inc(s5_small, 1)
                    done[0] += 1
                    dve.wait_ge(s5_small, done[0])

                def spread(a, n):
                    return a.unsqueeze(2).broadcast_to([P, PAIRS, n])

                ks = table("angles").unsqueeze(1).broadcast_to([P, PAIRS, ANGLES])
                dve.memset(stage_zero, 0.0).then_inc(w3_zero, 1)
                dve.wait_ge(inputs_in, 32)
                dve.wait_ge(s5_exp, 1)
                then(dve.tensor_tensor(zr, lr, step, ALU.mult))
                then(dve.tensor_tensor(mag[:], ks[:, :, 0:POWERS], spread(zr, POWERS), ALU.mult))
                assert done[0] == MAG_STEP
                then(dve.tensor_tensor(th, li, step, ALU.mult))
                then(dve.tensor_scalar(q, th, 1 / (2 * np.pi), ROUND, ALU.mult, ALU.add))
                then(dve.tensor_scalar(q, q, ROUND, None, ALU.subtract))
                for part in PI_PARTS:
                    then(dve.scalar_tensor_tensor(out=th, in0=q, scalar=-part, in1=th, op0=ALU.mult, op1=ALU.add))
                then(dve.tensor_scalar(f, th, 1 / (2 * np.pi), None, ALU.mult))
                then(dve.tensor_scalar(fh, f, ROUND12, ROUND12, ALU.add, ALU.subtract))
                then(dve.tensor_tensor(fl, f, fh, ALU.subtract))
                then(dve.tensor_tensor(turns[:], ks, spread(fh, ANGLES), ALU.mult))
                then(dve.tensor_scalar(rot_s[:], turns[:], ROUND, ROUND, ALU.add, ALU.subtract))
                then(dve.tensor_tensor(turns[:], turns[:], rot_s[:], ALU.subtract))
                then(dve.tensor_tensor(rot_c[:], ks, spread(fl, ANGLES), ALU.mult))
                then(dve.tensor_tensor(turns[:], turns[:], rot_c[:], ALU.add))
                then(dve.tensor_scalar(rot_s[:], turns[:], ROUND, ROUND, ALU.add, ALU.subtract))
                then(dve.tensor_tensor(turns[:], turns[:], rot_s[:], ALU.subtract))
                assert done[0] == TURN_STEPS
                dve.wait_ge(s5_sin, 2)
                then(dve.tensor_tensor(turns[:], rot_c[:], rot_c[:], ALU.mult))
                then(dve.tensor_scalar(rot_c[:], turns[:], -2.0, 1.0, ALU.mult, ALU.add))
                assert done[0] == PHASE_STEPS

            def s5_matrices():
                lr, li = s5p[:, 0:PAIRS], s5p[:, PAIRS:2 * PAIRS]

                def param(i):
                    c = 3 * PAIRS + i * PAIRS * GP
                    return s5p[:, c:c + PAIRS * GP].rearrange("p (q c) -> p q c", c=GP)

                br, bi, cr_, ci_ = (param(i) for i in range(4))
                den, am1, cr, ci, t1, t2, t3, t4 = (small[:, i] for i in range(7, 15))
                ar, ai = pow_r[:, :, 1], pow_i[:, :, 1]
                done = [0]

                def then(*steps):
                    for ins in steps:
                        ins.then_inc(s5_bmat, 1)
                        done[0] += 1
                    dve.wait_ge(s5_bmat, done[0])

                def spread(a):
                    return a.unsqueeze(2).broadcast_to([P, PAIRS, GP])

                dve.wait_ge(s5_exp, 2)
                then(dve.tensor_tensor(pow_r[:], mag[:], rot_c[:, :, 0:POWERS], ALU.mult),
                     dve.tensor_tensor(pow_i[:], mag[:], rot_s[:, :, 0:POWERS], ALU.mult),
                     dve.tensor_tensor(t1, lr, lr, ALU.mult), dve.tensor_tensor(t2, li, li, ALU.mult))
                then(dve.tensor_tensor(den, t1, t2, ALU.add), dve.tensor_scalar(am1, ar, -1.0, None, ALU.add))
                then(dve.reciprocal(den, den), dve.tensor_tensor(t1, am1, lr, ALU.mult),
                     dve.tensor_tensor(t2, ai, li, ALU.mult), dve.tensor_tensor(t3, ai, lr, ALU.mult),
                     dve.tensor_tensor(t4, am1, li, ALU.mult))
                then(dve.tensor_tensor(cr, t1, t2, ALU.add), dve.tensor_tensor(ci, t3, t4, ALU.subtract))
                then(dve.tensor_tensor(cr, cr, den, ALU.mult), dve.tensor_tensor(ci, ci, den, ALU.mult))
                then(dve.tensor_tensor(bb[:, 0], br, spread(cr), ALU.mult), dve.tensor_tensor(bb[:, 1], bi, spread(ci), ALU.mult),
                     dve.tensor_tensor(bb[:, 2], bi, spread(cr), ALU.mult), dve.tensor_tensor(bb[:, 3], br, spread(ci), ALU.mult))
                then(dve.tensor_tensor(bb[:, 0], bb[:, 0], bb[:, 1], ALU.subtract),
                     dve.tensor_tensor(bb[:, 2], bb[:, 2], bb[:, 3], ALU.add))
                then(dve.tensor_scalar(bb[:, 3], ci_, -1.0, None, ALU.mult))

                def product(power, re, im, conj):
                    a = [t[:, :, power:power + CH].unsqueeze(3).broadcast_to([P, PAIRS, CH, GP]) for t in (pow_r, pow_i)]
                    b = [t.unsqueeze(2).broadcast_to([P, PAIRS, CH, GP]) for t in (re, im)]
                    yield dve.tensor_tensor(b_mat[:, 0], b[0], a[0], ALU.mult), dve.tensor_tensor(t_mat[:, 0], b[1], a[1], ALU.mult)
                    yield (dve.tensor_tensor(b_mat[:, 0], b_mat[:, 0], t_mat[:, 0], ALU.add if conj else ALU.subtract),
                           dve.tensor_tensor(b_mat[:, 1], b[1], a[0], ALU.mult), dve.tensor_tensor(t_mat[:, 1], b[0], a[1], ALU.mult))
                    yield (dve.tensor_tensor(b_mat[:, 1], b_mat[:, 1], t_mat[:, 1], ALU.subtract if conj else ALU.add),)

                for steps in product(0, bb[:, 0], bb[:, 2], False):
                    then(*steps)
                assert done[0] == BMAT_STEPS
                return then, product, cr_, done

            def s5_output_matrices(then, product, c_re, done):
                dve.wait_ge(s5_prep_mm, 9)
                for steps in product(1, c_re, bb[:, 3], True):
                    then(*steps)
                assert done[0] == CMAT_STEPS

            def odd_mixer(stage):
                for m in range(HT):
                    dve.wait_ge(used, O_U - first + m + 1)
                    dve.tensor_tensor(u[:, m], bank[m][:].rearrange("p (c l) -> p l c", l=CH),
                                      rstd[:].rearrange("p (c l) -> p l c", l=CH), ALU.mult).then_inc(u_ready, 1)
                dve.wait_ge(used, O_GK - first + 1)
                dve.tensor_tensor(squares[0:16, 0, :], bank[4][0:16, :], rstd[0:16, :], ALU.mult).then_inc(gk_ready, 1)
                for i in range(2):
                    dve.wait_ge(gate_pre, i + 1)
                    dve.tensor_scalar(logs[:, i, :], bank[5 + i][:], column("gk_b", i), None, ALU.add).then_inc(gk_logs, 1)
                dve.wait_ge(gk_logs, 2)
                dve.wait_ge(gk_abs, 3)
                flat_logs = logs[:].rearrange("p i t -> p (i t)")
                dve.scalar_tensor_tensor(out=flat_logs, in0=flat_logs, scalar=0.0, in1=e_pos[:].rearrange("p i t -> p (i t)"),
                                         op0=ALU.min, op1=ALU.subtract).then_inc(gk_sum, 1)
                dve.wait_ge(gk_sum, 1)
                for i in range(2):
                    dve.tensor_tensor_scan(logs[:, i, :], table("chunk_keep"), logs[:, i, :], 0.0, ALU.mult, ALU.add).then_inc(gk_sum, 1)
                dve.wait_ge(gk_exp, 2)
                dve.tensor_copy(chunk_decay[:], e_pos[:].rearrange("p i (n c) -> p i n c", c=GC)[:, :, :, GC - 1]).then_inc(gk_step, 1)
                dve.wait_ge(gk_step, 1)
                for e in (e_pos, e_neg):
                    dve.tensor_tensor(e[:], e[:], rstd[:].unsqueeze(1).broadcast_to([P, 2, S]), ALU.mult).then_inc(gk_scaled, 1)
                dve.wait_ge(gk_scaled, 2)
                for i in range(2):
                    dve.wait_ge(used, O_Q - first + i + 1)
                    dve.scalar_tensor_tensor(out=e_pos[:, i, :], in0=bank[(7, 4)[i]][:], scalar=64 ** -0.5, in1=e_pos[:, i, :],
                                             op0=ALU.mult, op1=ALU.mult).then_inc(gk_dec, 1)
                for i in range(2):
                    dve.wait_ge(used, O_K - first + i + 1)
                    dve.tensor_tensor(e_neg[:, i, :], bank[5 + i][:], e_neg[:, i, :], ALU.mult).then_inc(gk_dec, 1)
                dve.wait_ge(gk_dec, 4)
                for i in range(2):
                    dve.tensor_tensor(logs[:, i, :].rearrange("p (n c) -> p n c", c=GC),
                                      e_neg[:, i, :].rearrange("p (n c) -> p n c", c=GC),
                                      chunk_decay[:, i, :].unsqueeze(2).broadcast_to([P, GN, GC]), ALU.mult).then_inc(gk_dec, 1)

                a, b_, c, d_, e_ = h_full_pairs, square_pairs, st[:, 0], st[:, 1], st[:, 2]
                cos_, sin_ = rot[:, 0], rot[:, 1]
                done = [0]

                def then(*steps):
                    for ins in steps:
                        ins.then_inc(s5_step, 1)
                        done[0] += 1
                    dve.wait_ge(s5_step, done[0])

                def local(ri):
                    return [bank[2 * ri + i][:].rearrange("p (q c) -> p q c", c=CHUNKS) for i in range(2)]

                def times(out, ri, by):
                    return [dve.tensor_tensor(out[:, 8 * i:8 * i + 8], local(ri)[i], by[:, 8 * i:8 * i + 8], ALU.mult) for i in range(2)]

                dve.wait_ge(s5_local, 1)
                dve.wait_ge(s5_rot_in, 32)
                dve.tensor_copy(d_, m8[:].unsqueeze(2).broadcast_to([P, PAIRS, CHUNKS])).then_inc(s5_coef, 1)
                times_all = times(a, 0, cos_) + times(c, 1, cos_) + times(b_, 1, sin_) + times(e_, 0, sin_)
                last_reads = times_all
                for n, ins in enumerate(last_reads):
                    if n % 2:
                        ins.then_inc(s5_step, 1)
                    else:
                        ins.then_inc(s5_half, 1)
                done[0] = 4
                dve.wait_ge(s5_step, 4)
                dve.wait_ge(s5_half, 4)
                dve.wait_ge(s5_coef, 1)
                then(dve.tensor_tensor(a, a, b_, ALU.add), dve.tensor_tensor(c, c, e_, ALU.subtract),
                     dve.memset(d_[:, :, 0:1], 0.0))
                flat = [t.rearrange("p q c -> p (q c)") for t in (a, c, d_)]
                then(dve.tensor_tensor_scan(flat[0], flat[2], flat[0], 0.0, ALU.mult, ALU.add),
                     dve.tensor_tensor_scan(flat[1], flat[2], flat[1], 0.0, ALU.mult, ALU.add))
                then(dve.tensor_tensor(d_, a, cos_, ALU.mult), dve.tensor_tensor(b_, c, sin_, ALU.mult),
                     dve.memset(e_[:, :, 0:1], 0.0))
                n_ = CHUNKS
                then(dve.tensor_tensor(e_[:, :, 1:n_], d_[:, :, 0:n_ - 1], b_[:, :, 0:n_ - 1], ALU.subtract))
                then(dve.tensor_tensor(d_, a, sin_, ALU.mult), dve.tensor_tensor(b_, c, cos_, ALU.mult))
                then(dve.tensor_tensor(a[:, :, 1:n_], d_[:, :, 0:n_ - 1], b_[:, :, 0:n_ - 1], ALU.add),
                     dve.memset(a[:, :, 0:1], 0.0))
                assert done[0] == S5_STEPS

                for t in range(TT):
                    dve.wait_ge(sg_ready, t + 1)
                    g4 = sg[:, t, :].rearrange("p (h d) -> p h d", d=DV)
                    gain = cols[:, COL["gla_norm"]:COL["gla_norm"] + DV].unsqueeze(1).broadcast_to([P, GH, DV])
                    dve.tensor_tensor(g4, g4, gain, ALU.mult).then_inc(sg_gain, 1)
                dve.wait_ge(s5_y_ready, 4)
                dve.memset(state[:, 0], 0.0).then_inc(state_step, 1)
                for h in range(GH):
                    dve.wait_ge(att_ready, h + 1)
                    causal = table("chunk_causal").unsqueeze(1).broadcast_to([P, TT, P])
                    dve.tensor_tensor(attT[:, h, :].rearrange("p (t c) -> p t c", c=P),
                                      bank[(2, 3, 0, 1)[h]][:].rearrange("p (t c) -> p t c", c=P), causal, ALU.mult).then_inc(attT_ready, 1)
                for n in range(GN - 1):
                    dve.wait_ge(kv_ready, min(n // 4 * 4 + 4, GN - 1))
                    dve.wait_ge(state_step, 1 + 2 * n)
                    for i in range(2):
                        col = (n // 2 % 2) * 256 + i * DV
                        dve.scalar_tensor_tensor(out=state[:, n + 1, i], in0=state[:, n, i], scalar=chunk_decay[:, i, n:n + 1],
                                                 in1=bank[4 + 2 * (n % 2) + n // 4][:, col:col + DV],
                                                 op0=ALU.mult, op1=ALU.add).then_inc(state_step, 1)
                dve.wait_ge(y_loaded, 16)
                uf = u[:].rearrange("p m l c -> p m (l c)")
                y_in = u_in[:].rearrange("p g c -> p (g c)").rearrange("p (m n) -> p m n", m=HT)
                for m in range(HT):
                    ins = dve.scalar_tensor_tensor(out=y_in[:, m], in0=uf[:, m], scalar=column("s5_d", m), in1=y_in[:, m],
                                                   op0=ALU.mult, op1=ALU.add)
                ins.then_inc(ys_ready, 1)
                for t in range(TT):
                    dve.wait_ge(intra_ready, t + 1)
                    dve.wait_ge(inter_out, 2 * t + 2)
                    dve.tensor_tensor(o[:, t, :], bank[t][:], o[:, t, :], ALU.add).then_inc(o_ready, 1)
                dve.wait_ge(used, O_G - first + 4)
                dve.wait_ge(ys_gelu, 1)
                dve.tensor_copy(h_hi[:, 0:HT, :], y_in).then_inc(ys_split, 1)
                dve.wait_ge(ys_split, 1)
                dve.tensor_tensor(h_lo[:, 0:HT, :], y_in, h_hi[:, 0:HT, :].bitcast(F32), ALU.subtract).then_inc(ys_split, 1)
                for t in range(TT):
                    dve.wait_ge(o_squared, t + 1)
                    dve.tensor_reduce(gla_var[:, t * GH:(t + 1) * GH], squares[:, t % 2, :].rearrange("p (h d) -> p h d", d=DV),
                                      AX_X, ALU.add).then_inc(o_sum, 1)
                dve.wait_ge(o_rms, 1)
                dve.reciprocal(gla_var[:], gla_var[:]).then_inc(o_inv, 1)
                dve.wait_ge(o_inv, 1)
                o16 = o[:].rearrange("p t (h d) -> p (t h) d", d=DV)
                dve.tensor_tensor(o16, o16, gla_var[:].unsqueeze(2).broadcast_to([P, TT * GH, DV]), ALU.mult).then_inc(o_step, 1)
                dve.wait_ge(o_step, 1)
                dve.wait_ge(sg_gain, TT)
                dve.tensor_tensor(o[:], o[:], sg[:], ALU.mult).then_inc(o_step, 1)
                sig = st[:, 0:2].rearrange("p a q c -> p (a q c)").rearrange("p (m n) -> p m n", m=HT)
                dve.wait_ge(glu_sig, HT)
                dve.tensor_tensor(y_in, y_in, sig, ALU.mult).then_inc(s5_gated, 1)
                dve.wait_ge(s5_gated, 1)
                for m in range(HT):
                    in_time = y_in[:, m].rearrange("p (l c) -> p c l", c=CHUNKS)
                    hi = y_s5_hi[:, m, :].rearrange("p (c l) -> p c l", l=CH)
                    dve.tensor_copy(hi, in_time).then_inc(s5_gated, 1)
                    dve.wait_ge(s5_gated, m + 2)
                    ins = dve.tensor_tensor(y_s5_lo[:, m, :].rearrange("p (c l) -> p c l", l=CH), in_time, hi.bitcast(F32), ALU.subtract)
                ins.then_inc(s5_out, 1)
                for h in range(GH):
                    dve.wait_ge(o_turned, h + 1)
                    y_hi, y_lo = y_gla_hi[:, h, :], y_gla_lo[:, h, :]
                    dve.tensor_copy(y_hi, bank[4 + h][:]).then_inc(gla_y, 1)
                    dve.wait_ge(gla_y, 2 * h + 1)
                    dve.tensor_tensor(y_lo, bank[4 + h][:], y_hi.bitcast(F32), ALU.subtract).then_inc(gla_y, 1)

            def even_mixer(stage):
                if 2 in order:
                    s5_phases()
                lru_constants()
                for which in range(2):
                    var = qk_var[:, which, :]
                    for t in range(TT):
                        n = TT * which + t
                        dve.wait_ge(qk_squared, n + 1)
                        dve.tensor_reduce(var[:, t * HEADS:(t + 1) * HEADS],
                                          squares[:, n % 2, :].rearrange("p (h d) -> p h d", d=HD),
                                          AX_X, ALU.add).then_inc(qk_sum, 1)
                    dve.wait_ge(qk_rms, which + 1)
                    dve.reciprocal(var, var).then_inc(qk_inv, 1)
                    dve.wait_ge(qk_inv, which + 1)
                    heads = var.rearrange("p (t h) -> p t h", h=HEADS)
                    dve.tensor_tensor(heads, heads, rstd_t[:].unsqueeze(2).broadcast_to([P, TT, HEADS]), ALU.mult).then_inc(q_inv_scaled, 1)
                    dve.wait_ge(q_inv_scaled, which + 1)
                    for t in range(TT):
                        inv = var[:, t * HEADS:(t + 1) * HEADS].unsqueeze(2).broadcast_to([P, HEADS, HD])
                        dve.tensor_tensor(qk[:, which, t, :].rearrange("p (h d) -> p h d", d=HD),
                                          bank[4 * which + t][:].rearrange("p (h d) -> p h d", d=HD), inv,
                                          ALU.mult).then_inc(qk_step, 1)
                if 2 in order:
                    matrices = s5_matrices()
                for which in range(2):
                    a = qk[:, which].rearrange("p t (h d) -> p (t h) d", d=HD)
                    gain = cols[:, COL[("q_norm", "k_norm")[which]]:][:, 0:HD].unsqueeze(1).broadcast_to([P, TT * HEADS, HD])
                    dve.wait_ge(qk_step, 4 * which + 4)
                    base = 2 * TT + 3 * which
                    dve.tensor_tensor(a, a, gain, ALU.mult).then_inc(qk_step, 1)
                    dve.wait_ge(qk_step, base + 1)
                    r = qk[:, which].rearrange("p t (h d) -> p t h d", d=HD)
                    x1, x2 = r[:, :, :, 0:ROPE], r[:, :, :, ROPE:2 * ROPE]
                    c, sn = (table(n).rearrange("p (t d) -> p t d", d=ROPE).unsqueeze(2).broadcast_to([P, TT, HEADS, ROPE])
                             for n in ("cos", "sin"))
                    for i, (xx, tt_) in enumerate(((x1, c), (x2, sn), (x2, c), (x1, sn))):
                        op = dve.tensor_tensor(rope_tmp[:, i], xx, tt_, ALU.mult)
                        op.then_inc(qk_rope, 1)
                    dve.wait_ge(qk_rope, 4 * (which + 1))
                    dve.tensor_tensor(x1, rope_tmp[:, 0], rope_tmp[:, 1], ALU.subtract).then_inc(qk_step, 1)
                    dve.tensor_tensor(x2, rope_tmp[:, 2], rope_tmp[:, 3], ALU.add).then_inc(qk_step, 1)
                    if which == 0:
                        dve.wait_ge(qk_step, 2 * TT + 3)

                for m in range(HT):
                    dve.wait_ge(used, E_X + m + 1)
                    dve.tensor_tensor(squares[:, m % 2, :], bank[4 + m][:], rstd[:], ALU.mult).then_inc(xl_scaled, 1)
                    dve.wait_ge(x_newest, m + 1)
                    for i in range(3):
                        back = i + 1
                        dve.scalar_tensor_tensor(out=xc[:, m, back:S], in0=squares[:, m % 2, 0:S - back],
                                                 scalar=column("lru_w", (3 - back) * HT + m), in1=xc[:, m, back:S],
                                                 op0=ALU.mult, op1=ALU.add).then_inc(x_conv, 1)
                        dve.wait_ge(x_conv, 3 * m + i + 1)
                if 2 in order:
                    s5_output_matrices(*matrices)
                    dve.wait_ge(s5_stored, 16 * S5_STORES)
                for m in range(HT):
                    dve.wait_ge(used, E_G + m + 1)
                    dve.tensor_tensor(gg[:, m, :], bank[m][:], rstd[:], ALU.mult).then_inc(gl_scaled, 1)
                dve.wait_ge(lru_exp, 2 * HT)
                dve.tensor_scalar(rg[:], coef[:], 1.0, None, ALU.add).then_inc(lru_step, 1)
                dve.wait_ge(lru_step, 1)
                dve.reciprocal(rg[:], rg[:]).then_inc(lru_step, 1)
                dve.wait_ge(lru_step, 2)
                dve.tensor_tensor(coef[:], coef[:], rg[:], ALU.mult).then_inc(lru_step, 1)
                dve.tensor_tensor(ig[:], ig[:], xc[:], ALU.mult).then_inc(lru_step, 1)
                dve.wait_ge(lru_step, 4)
                dve.wait_ge(lru_sqrt, 1)
                dve.tensor_tensor(ig[:], ig[:], coef[:], ALU.mult).then_inc(lru_step, 1)
                dve.wait_ge(lru_step, 5)
                for m in range(HT):
                    dve.tensor_tensor_scan(rg[:, m, :], decay[:, m, :], ig[:, m, :], 0.0, ALU.mult,
                                           ALU.add).then_inc(lru_step, 1)
                dve.wait_ge(lru_step, 5 + HT)
                dve.wait_ge(gg_ready, HT)
                dve.tensor_tensor(rg[:], rg[:], gg[:], ALU.mult).then_inc(lru_step, 1)
                dve.wait_ge(lru_step, 6 + HT)
                dve.tensor_copy(y_lru_hi[:], rg[:]).then_inc(lru_step, 1)
                dve.wait_ge(lru_step, 7 + HT)
                dve.tensor_tensor(y_lru_lo[:], rg[:], y_lru_hi[:].bitcast(F32), ALU.subtract).then_inc(lru_y, 1)
                dve.wait_ge(lru_y, 1)

                def mask_scores(n):
                    t = n % TT
                    w = (t + 1) * P
                    dve.wait_ge(scores_ready, n + 1)
                    if n >= 2:
                        dve.wait_ge(probs_turned, n - 1)
                    for e in range(2):
                        dve.tensor_tensor_reduce(prob[:, n % 2, e, 0:w], bank[2 * e + n % 2][:, 0:w],
                                                 table("mask")[:, S - w:S], 1.0, NEVER, ALU.add, ALU.max,
                                                 row_max[:, n % 2, e:e + 1]).then_inc(masked, 1)
                    dve.wait_ge(masked, 2 * n + 2)
                    dve.tensor_scalar(neg_max[:, n % 2, :], row_max[:, n % 2, :], -HD ** -0.5, None,
                                      ALU.mult).then_inc(negmax_ready, 1)

                def normalise(n):
                    w = (n % TT + 1) * P
                    dve.wait_ge(exped, 2 * n + 2)
                    dve.reciprocal(row_inv[:, n % 2, :], row_sum[:, n % 2, :]).then_inc(rinv_ready, 1)
                    dve.wait_ge(rinv_ready, n + 1)
                    for e in range(2):
                        dve.tensor_scalar(prob[:, n % 2, e, 0:w], prob[:, n % 2, e, 0:w], row_inv[:, n % 2, e:e + 1],
                                          None, ALU.mult).then_inc(probs_ready, 1)

                def take_heads(hp):
                    dve.wait_ge(pv_done, TT * (hp + 1))
                    y_hi, y_lo = y_att_hi[:, hp, :], y_att_lo[:, hp, :]
                    dve.tensor_copy(y_hi, bank[6 + hp % 2][:]).then_inc(att_y, 1)
                    dve.wait_ge(att_y, 2 * hp + 1)
                    dve.tensor_tensor(y_lo, bank[6 + hp % 2][:], y_hi.bitcast(F32), ALU.subtract).then_inc(att_y, 1)

                mask_scores(0)
                mask_scores(1)
                for n in range(ATT_STEPS):
                    normalise(n)
                    if n + 2 < ATT_STEPS:
                        mask_scores(n + 2)
                    if n % TT == 1 and n > TT:
                        take_heads(n // TT - 1)
                take_heads(HT - 1)

            take_x()
            if 2 in order and 0 not in order:
                s5_phases()
            for stage, part in enumerate(order):
                find_rstd(stage, 1 - part % 2)
                if part == 0:
                    even_mixer(stage)
                    add_residual(stage, E_O, 1)
                if part == 2:
                    if 0 not in order:
                        s5_output_matrices(*s5_matrices())
                    odd_mixer(stage)
                    add_residual(stage, O_O - first, 1)
                if part in (1, 3):
                    mlp(stage, part // 2, first_unit[part] - first)
                    add_residual(stage, first_unit[part] - first + 2 * FT, 3)


PARTS = (0, 1, 2, 3)


def by_tiles(w):
    k, n = w.shape
    t = w.reshape(k // (8 * P), 8, P, n // P, P)
    return np.ascontiguousarray(t.transpose(3, 0, 2, 1, 4)).reshape(-1, P, UNIT)


def by_rows(w):
    return np.ascontiguousarray(w.reshape(4, 2, P, 512).transpose(0, 2, 1, 3)).reshape(-1, P, UNIT)


def on_partitions(v):
    return np.ascontiguousarray(v.reshape(-1, P).T)


def make_tables():
    back = np.arange(P)[:, None] + (S - P) - np.arange(S)[None, :]
    count = sum(((back >= 0) & (back % dil == 0) & (back <= BACK * dil)).astype(np.float32) for _, dil in PATTERNS)
    mask = np.where(count > 0, np.log(np.maximum(count, 1)) * HD ** 0.5, NEVER)
    inv = np.float32(500000.0) ** (-np.arange(0, 2 * ROPE, 2, dtype=np.float32) / np.float32(2 * ROPE))
    angle = np.arange(S, dtype=np.float32)[:, None] * inv[None, :]
    step, chunk = np.arange(P), np.arange(P) // GC
    parts = {
        "identity": np.eye(P), "mask": mask,
        "angles": np.broadcast_to(np.concatenate([np.arange(POWERS), CH * np.arange(CHUNKS)]), (P, ANGLES)),
        "chunk_keep": np.broadcast_to(np.arange(S) % GC != 0, (P, S)),
        "chunk_causal": (step[:, None] <= step[None, :]) & (chunk[:, None] == chunk[None, :]),
    }
    for name, f in (("cos", np.cos), ("sin", np.sin)):
        parts[name] = f(angle).reshape(TT, P, ROPE).transpose(1, 0, 2).reshape(P, -1)
    return np.ascontiguousarray(np.concatenate([parts[n] for n, _ in _TABLES], axis=1).astype(np.float32))


def block_diagonal(w):
    out = np.zeros((P, HT, P), w.dtype)
    for b in range(8):
        at = slice(64 * (b % 2), 64 * (b % 2) + 64)
        out[at, b // 2, at] = w[b]
    return out


def lay_out(x, e_norm, e_w_in, e_w_out, e_conv_w, e_conv_b, e_gate_a_w, e_gate_a_b, e_gate_x_w, e_gate_x_b,
            e_lambda, e_q_norm, e_k_norm, o_lambda_re, o_lambda_im, o_b_re, o_b_im, o_c_re, o_c_im, o_d, o_log_step,
            o_glu_b, o_gk_w, o_gk_b, o_gla_norm, o_norm, o_w_in, o_glu_w, o_w_out, f_norm, f_w_in, f_conv_w, f_conv_b, f_w_out):
    def cut(w, sizes):
        return np.split(w, np.cumsum(sizes)[:-1], axis=1)

    ex, eg, eq, ek, ev = cut(e_w_in[0], [512] * 5)
    ou, oq, ok, ov, og, ogk = cut(o_w_in[0], [512, 256, 256, 512, 512, 16])
    ogk = np.pad(ogk, ((0, 0), (0, P - 16)))

    def mlp(layer):
        up = by_tiles(f_w_in[layer]).reshape(2, FT, P, UNIT).transpose(1, 0, 2, 3).reshape(-1, P, UNIT)
        return [up, by_tiles(f_w_out[layer])]

    glu = o_glu_w[0].reshape(HT, P, HT, P).transpose(2, 0, 1, 3).reshape(2, 8, P, P).transpose(0, 2, 1, 3).reshape(2, P, UNIT)
    units = np.concatenate(
        [by_rows(eq), by_rows(ek), by_rows(ev), by_tiles(ex), by_tiles(eg), by_tiles(e_w_out[0])] + mlp(0)
        + [by_tiles(ou), by_tiles(ogk), by_tiles(oq), by_tiles(ok), by_rows(ov), by_rows(og), glu, by_tiles(o_w_out[0])]
        + mlp(1))
    assert units.shape == (N_UNITS, P, UNIT)
    columns = {
        "norm": np.concatenate([on_partitions(v) for v in (e_norm[0], f_norm[0], o_norm[0], f_norm[1])], axis=1),
        "mlp_w": on_partitions(f_conv_w), "mlp_b": on_partitions(f_conv_b),
        "lru_w": on_partitions(e_conv_w), "lru_b": on_partitions(e_conv_b), "gate_a_b": on_partitions(e_gate_a_b),
        "gate_x_b": on_partitions(e_gate_x_b), "lambda": on_partitions(e_lambda),
        "s5_d": on_partitions(o_d), "glu_b": on_partitions(o_glu_b), "gk_b": on_partitions(o_gk_b),
        "gla_norm": np.broadcast_to(o_gla_norm, (P, DV)),
        "q_norm": np.broadcast_to(e_q_norm, (P, HD)), "k_norm": np.broadcast_to(e_k_norm, (P, HD)),
    }
    columns = np.concatenate([columns[n] for n, _ in _COLUMNS], axis=1)
    assert columns.shape == (P, N_COLS)

    def states(a):
        return a.reshape(PAIRS, 2, ST, -1).transpose(1, 2, 0, 3).reshape(P, -1)

    s5 = np.concatenate([states(o_lambda_re[0]), states(o_lambda_im[0]),
                         states(np.broadcast_to(o_log_step[0][:, None], (2 * PAIRS, ST))),
                         states(o_b_re[0]), states(o_b_im[0]),
                         states(o_c_re[0].transpose(0, 2, 1)), states(o_c_im[0].transpose(0, 2, 1))], axis=1)
    return {"s5": np.ascontiguousarray(s5), "gk_w": np.ascontiguousarray(o_gk_w[0]),
            "xT": np.ascontiguousarray(x[0].T), "units": units, "columns": np.ascontiguousarray(columns),
            "tables": make_tables(), "gates_a": block_diagonal(e_gate_a_w[0]), "gates_x": block_diagonal(e_gate_x_w[0])}


def kernel(**inputs):
    import concourse.bacc as bacc
    from concourse.bass_utils import run_bass_kernel_spmd

    arrays = lay_out(**{n: np.asarray(a) for n, a in inputs.items()})
    nc = bacc.Bacc("TRN2", target_bir_lowering=False, num_devices=1)
    args = {n: nc.dram_tensor(n, a.shape, F32, kind="ExternalInput").ap() for n, a in arrays.items()}
    outT = nc.dram_tensor("outT", (D, S), F32, kind="ExternalOutput").ap()
    build(nc, PARTS, outT=outT, **args)
    r = run_bass_kernel_spmd(nc, [arrays], core_ids=[0])
    return np.ascontiguousarray(r.results[0]["outT"].T)[None]
```

```python
from contextlib import ExitStack

import numpy as np

import concourse.bass as bass
from concourse import mybir

ALU = mybir.AluOpType
ACT = mybir.ActivationFunctionType
AX_X = mybir.AxisListType.X
F32 = mybir.dt.float32
F32R = mybir.dt.float32r
I32 = mybir.dt.int32

P = 128
D = 1024
S = 512
KT = D // P
HALF = D // 2
HT = HALF // P
FF = 3 * D
FT = FF // P
TT = S // P
EPS = 1e-6
HEADS, HD = 8, 64
ROPE = 8
PATTERNS = ((128, 1), (512, 4), (2048, 16))
BACK = 128
NEVER = -1e30
ATT_STEPS = HEADS // 2 * TT
LRU_STEP = ATT_STEPS - 3 * HT - 1
QK_STEPS = 2 * TT + 6
ATANH = [1.0 / n for n in range(1, 16, 2)]
LAM_ABS = 2

CH, PAIRS, GP, ST = 8, 16, 16, 64
CHUNKS = S // CH
POWERS = CH + 1
ANGLES = POWERS + CHUNKS
ROUND = 1.5 * 2 ** 23
ROUND12 = 1.5 * 2 ** 11
TWO_PI = 6.2831850
PI_PARTS = (6.28125, 0.0019350051879882812, 3.0200665743e-07)
S5_STORES = 2 + CH
LN2_PARTS = (0.693359375, -2.12194440e-4)
W1_SLOTS = HT
S5_COLS = 3 * PAIRS + 4 * PAIRS * GP
TURN_STEPS, PHASE_STEPS, MAG_STEPS = 32, 34, 55
BMAT_STEPS, CMAT_STEPS = 28, 34
S5_STEPS = 17

GH, DV, GC = 4, 128, 64
GN = S // GC
LAM_STEPS = LAM_ABS + 5 + 2 * (len(ATANH) - 2) + 4

UNIT = 8 * P
E_Q, E_K, E_V, E_X, E_G, E_O = 0, 4, 8, 12, 16, 20
FIRST_MLP = 28
MLP_UNITS = 2 * FT + 3 * KT
O_U = FIRST_MLP + MLP_UNITS
O_GK, O_Q, O_K, O_V, O_G, O_GLU, O_O = O_U + 4, O_U + 5, O_U + 7, O_U + 9, O_U + 13, O_U + 17, O_U + 19
SECOND_MLP = O_O + 8
N_UNITS = SECOND_MLP + MLP_UNITS
RAW_SLOTS = 4
SPLIT_SLOTS = 2

_COLUMNS = [("norm", 4 * KT), ("mlp_w", 2 * 3 * FT), ("mlp_b", 2 * FT),
            ("lru_w", 4 * HT), ("lru_b", HT), ("gate_a_b", HT), ("gate_x_b", HT), ("lambda", HT),
            ("q_norm", HD), ("k_norm", HD),
            ("s5_d", HT), ("glu_b", HT), ("gk_b", 2), ("gla_norm", DV)]
COL = {}
for _name, _n in _COLUMNS:
    COL[_name] = sum(n for _, n in _COLUMNS[:len(COL)])
N_COLS = sum(n for _, n in _COLUMNS)


_TABLES = [("identity", P), ("mask", S), ("cos", TT * ROPE), ("sin", TT * ROPE), ("angles", ANGLES),
           ("chunk_keep", S), ("chunk_causal", P)]
TAB = {}
for _name, _n in _TABLES:
    TAB[_name] = sum(n for _, n in _TABLES[:len(TAB)])
N_TAB = sum(n for _, n in _TABLES)


def build(nc, parts, xT, units, columns, tables, gates_a, gates_x, s5, gk_w, outT):
    with ExitStack() as ctx:
        def sb(name, shape, dt=F32, where=ctx):
            return where.enter_context(nc.sbuf_tensor(name, shape, dt))

        def sem(name):
            return ctx.enter_context(nc.semaphore(name))

        bank = [ctx.enter_context(nc.psum_tensor(f"bank{b}", [P, 512], F32)) for b in range(8)]

        x = sb("x", [P, KT, S])
        h_hi = sb("h_hi", [P, KT, S], F32R)
        h_lo = sb("h_lo", [P, KT, S], F32R)
        raw = sb("raw", [P, RAW_SLOTS, UNIT])
        w_hi = sb("w_hi", [P, SPLIT_SLOTS, UNIT], F32R)
        w_lo = sb("w_lo", [P, SPLIT_SLOTS, UNIT], F32R)
        cols = sb("cols", [P, N_COLS])
        ones = sb("ones", [P, P])
        eps = sb("eps", [P, 1])
        zero = sb("zero", [P, 1])
        tabs = sb("tabs", [P, N_TAB])
        squares = sb("squares", [P, 2, S])
        total = sb("total", [P, S])
        rstd = sb("rstd", [P, S])
        rstd_t = sb("rstd_t", [P, TT])
        spare = sb("spare", [P, 2, S])

        landed = [sem(f"landed{s}") for s in range(RAW_SLOTS)]
        hi_split = sem("hi_split")
        split = sem("split")
        used = sem("used")
        inputs_in = sem("inputs_in")
        consts_set = sem("consts_set")
        x_ready = sem("x_ready")
        x_in = [sem(f"x_in{k}") for k in range(KT)]
        gained_hi = sem("gained_hi")
        squared = sem("squared")
        total_clear = sem("total_clear")
        added = sem("added")
        summed = sem("summed")
        rms_ready = sem("rms_ready")
        rstd_ready = sem("rstd_ready")
        h_ready = sem("h_ready")
        scaled = sem("scaled")
        gate_raw = sem("gate_raw")
        newest_tap = sem("newest_tap")
        middle_tap = sem("middle_tap")
        conv_done = sem("conv_done")
        gelu_done = sem("gelu_done")
        gate_done = sem("gate_done")
        gate_hi_done = sem("gate_hi_done")
        gate_ready = sem("gate_ready")
        out_stored = sem("out_stored")
        s5_in = sem("s5_in")
        s5_m8 = sem("s5_m8")
        s5_diag = sem("s5_diag")
        s5_w2_stored = sem("s5_w2_stored")
        s5_small = sem("s5_small")
        s5_sin = sem("s5_sin")
        s5_bmat = sem("s5_bmat")
        s5_prep_mm = sem("s5_prep_mm")
        s5_w1_out = sem("s5_w1_out")
        s5_v_out = sem("s5_v_out")
        s5_stored = sem("s5_stored")
        s5_rot_stored = sem("s5_rot_stored")
        s5_w1_stored = [sem(f"s5_w1_stored{n}") for n in range(W1_SLOTS)]
        gl_scaled = sem("gl_scaled")
        xl_scaled = sem("xl_scaled")
        q_inv_scaled = sem("q_inv_scaled")
        gk_scaled = sem("gk_scaled")
        s5_loaded = sem("s5_loaded")
        s5_w2_loaded = sem("s5_w2_loaded")
        w3_zero = sem("w3_zero")
        w3_in = sem("w3_in")
        gk_in = sem("gk_in")
        u_ready = sem("u_ready")
        u_stored = sem("u_stored")
        u_loaded = sem("u_loaded")
        gk_ready = sem("gk_ready")
        gate_pre = sem("gate_pre")
        gk_abs = sem("gk_abs")
        gk_logs = sem("gk_logs")
        gk_sum = sem("gk_sum")
        gk_exp = sem("gk_exp")
        gk_dec = sem("gk_dec")
        s5_local = sem("s5_local")
        starts_clear = sem("starts_clear")
        s5_step = sem("s5_step")
        s5_coef = sem("s5_coef")
        s5_half = sem("s5_half")
        s5_rot_in = sem("s5_rot_in")
        s5_gated = sem("s5_gated")
        gk_step = sem("gk_step")
        o_inv = sem("o_inv")
        s5_y_ready = sem("s5_y_ready")
        s5_y_out = sem("s5_y_out")
        y_stored = sem("y_stored")
        y_loaded = sem("y_loaded")
        ys_ready = sem("ys_ready")
        ys_gelu = sem("ys_gelu")
        ys_split = sem("ys_split")
        glu_sig = sem("glu_sig")
        s5_out = sem("s5_out")
        vg_ready = sem("vg_ready")
        sg_ready = sem("sg_ready")
        sg_gain = sem("sg_gain")
        k_turned = sem("k_turned")
        k_end_ready = sem("k_end_ready")
        att_ready = sem("att_ready")
        attT_ready = sem("attT_ready")
        kv_ready = sem("kv_ready")
        state_step = sem("state_step")
        intra_ready = sem("intra_ready")
        inter_ready = sem("inter_ready")
        inter_out = sem("inter_out")
        o_ready = sem("o_ready")
        o_squared = sem("o_squared")
        o_sum = sem("o_sum")
        o_rms = sem("o_rms")
        o_step = sem("o_step")
        o_turned = sem("o_turned")
        gla_y = sem("gla_y")
        gla_hi = sem("gla_hi")
        s5_hi = sem("s5_hi")
        even_in = sem("even_in")
        qk_squared = sem("qk_squared")
        qk_sum = sem("qk_sum")
        qk_rms = sem("qk_rms")
        qk_step = sem("qk_step")
        v_ready = sem("v_ready")
        x_newest = sem("x_newest")
        x_conv = sem("x_conv")
        lam_step = sem("lam_step")
        qk_rope = sem("qk_rope")
        qk_inv = sem("qk_inv")
        lam_exp = sem("lam_exp")
        gates_made = sem("gates_made")
        gate_sig = sem("gate_sig")
        lru_exp = sem("lru_exp")
        lru_in = sem("lru_in")
        lru_step = sem("lru_step")
        lru_sqrt = sem("lru_sqrt")
        gg_ready = sem("gg_ready")
        lru_y = sem("lru_y")
        qk_turned = sem("qk_turned")
        qkT_ready = sem("qkT_ready")
        scores_ready = sem("scores_ready")
        masked = sem("masked")
        negmax_ready = sem("negmax_ready")
        exped = sem("exped")
        rinv_ready = sem("rinv_ready")
        probs_ready = sem("probs_ready")
        probs_turned = sem("probs_turned")
        probT_ready = sem("probT_ready")
        pv_done = sem("pv_done")
        att_y = sem("att_y")

        spare_pairs = spare[:].rearrange("p a (q c) -> p (a q) c", c=CHUNKS)
        square_pairs = squares[:].rearrange("p a (q c) -> p (a q) c", c=CHUNKS)

        def column(name, i=0):
            c = COL[name] + i
            return cols[:, c:c + 1]

        def table(name):
            return tabs[:, TAB[name]:TAB[name] + dict(_TABLES)[name]]

        even_mem = ExitStack()
        v = sb("v", [P, TT, HALF], F32, even_mem)
        qT = sb("qT", [P, HT, S], F32, even_mem)
        kT = sb("kT", [P, HT, S], F32, even_mem)
        qk_mem = ExitStack()
        qk = sb("qk", [P, 2, TT, HALF], F32, qk_mem)
        qk_mem.close()
        y_att_hi = sb("y_att_hi", [P, HT, S], F32R, even_mem)
        y_att_lo = sb("y_att_lo", [P, HT, S], F32R, even_mem)
        qk_var = sb("qk_var", [P, 2, TT * HEADS], F32, even_mem)
        rope_tmp = sb("rope_tmp", [P, 4, TT, HEADS, ROPE], F32, even_mem)
        ga = sb("ga", [P, HT, P], F32, even_mem)
        gx = sb("gx", [P, HT, P], F32, even_mem)
        lam_tmp = sb("lam_tmp", [P, 6, HT], F32, even_mem)
        neg_c = sb("neg_c", [P, HT], F32, even_mem)
        pos_c = sb("pos_c", [P, HT], F32, even_mem)
        row_max = sb("row_max", [P, 2, 2], F32, even_mem)
        neg_max = sb("neg_max", [P, 2, 2], F32, even_mem)
        row_sum = sb("row_sum", [P, 2, 2], F32, even_mem)
        row_inv = sb("row_inv", [P, 2, 2], F32, even_mem)
        lru_mem = ExitStack()
        xc = sb("xc", [P, HT, S], F32, lru_mem)
        rg = sb("rg", [P, HT, S], F32, lru_mem)
        ig = sb("ig", [P, HT, S], F32, lru_mem)
        decay = sb("decay", [P, HT, S], F32, lru_mem)
        coef = sb("coef", [P, HT, S], F32, lru_mem)
        prob = sb("prob", [P, 2, 2, S], F32, lru_mem)
        probT = sb("probT", [P, 2, 2, S], F32, lru_mem)
        lru_mem.close()
        lru_out_mem = ExitStack()
        sb("at_xc_rg", [P, 2, HT, S], F32, lru_out_mem)
        y_lru_hi = sb("y_lru_hi", [P, HT, S], F32R, lru_out_mem)
        y_lru_lo = sb("y_lru_lo", [P, HT, S], F32R, lru_out_mem)
        lru_out_mem.close()
        prep_mem = ExitStack()
        turns = sb("turns", [P, PAIRS, ANGLES], F32, prep_mem)
        rot_s = sb("rot_s", [P, PAIRS, ANGLES], F32, prep_mem)
        rot_c = sb("rot_c", [P, PAIRS, ANGLES], F32, prep_mem)
        small = sb("small", [P, 18, PAIRS], F32, prep_mem)
        mag = sb("mag", [P, PAIRS, POWERS], F32, prep_mem)
        pow_r = sb("pow_r", [P, PAIRS, POWERS], F32, prep_mem)
        pow_i = sb("pow_i", [P, PAIRS, POWERS], F32, prep_mem)
        s5p = sb("s5p", [P, S5_COLS], F32, prep_mem)
        bb = sb("bb", [P, 4, PAIRS, GP], F32, prep_mem)
        b_mat = sb("b_mat", [P, 2, PAIRS, CH, GP], F32, prep_mem)
        t_mat = sb("t_mat", [P, 2, PAIRS, CH, GP], F32, prep_mem)
        stage_w1 = kT
        stage_v = qT[:, 0, :]
        stage_zero = qT[:, 1, :]
        c_diag = qT[:, 2:4, :].rearrange("p r (q c) -> p r q c", c=2 * GP)
        prep_mem.close()
        even_mem.close()

        odd_mem = ExitStack()
        e_pos = sb("e_pos", [P, 2, S], F32, odd_mem)
        e_neg = sb("e_neg", [P, 2, S], F32, odd_mem)
        logs = sb("logs", [P, 2, S], F32, odd_mem)
        vg_mem = ExitStack()
        vg = sb("vg", [P, TT, HALF], F32, vg_mem)
        vg_mem.close()
        y_gla_hi = sb("y_gla_hi", [P, GH, S], F32R, odd_mem)
        sg_mem = ExitStack()
        start_im = sb("start_im", [P, PAIRS, 2, CHUNKS], F32, sg_mem)
        sg_mem.close()
        sg = sb("sg", [P, TT, HALF], F32, odd_mem)
        gkw = sb("gkw", [16, 2 * P], F32, odd_mem)
        chunk_decay = sb("chunk_decay", [P, 2, GN], F32, odd_mem)
        gla_var = sb("gla_var", [P, TT * GH], F32, odd_mem)
        m8 = sb("m8", [P, PAIRS], F32, odd_mem)
        s5_mem = ExitStack()
        wst = sb("wst", [P, 2, PAIRS, P], F32, s5_mem)
        w3 = sb("w3", [P, 2 * PAIRS, CH * GP], F32, s5_mem)
        rot = sb("rot", [P, 2, PAIRS, CHUNKS], F32, s5_mem)
        u_in = sb("u_in", [P, 2 * PAIRS, CHUNKS], F32, s5_mem)
        u = sb("u", [P, HT, CH, CHUNKS], F32, s5_mem)
        st = sb("st", [P, 3, PAIRS, CHUNKS], F32, s5_mem)
        start_re = sb("start_re", [P, PAIRS, 2, CHUNKS], F32, s5_mem)
        s5_mem.close()
        gla_mem = ExitStack()
        attT = sb("attT", [P, GH, S], F32, gla_mem)
        state = sb("state", [P, GN, 2, DV], F32, gla_mem)
        o = sb("o", [P, TT, HALF], F32, gla_mem)
        k_end = sb("k_end", [P, 2, S], F32, gla_mem)
        sb("beside_w3", [P, 2, S], F32, gla_mem)
        ys_hi = sb("ys_hi", [P, HT, S], F32R, gla_mem)
        sb("at_u_in", [P, HT, S], F32, gla_mem)
        ys_lo = sb("ys_lo", [P, HT, S], F32R, gla_mem)
        gla_mem.close()
        out_mem = ExitStack()
        y_gla_lo = sb("y_gla_lo", [P, GH, S], F32R, out_mem)
        y_s5_hi = sb("y_s5_hi", [P, HT, S], F32R, out_mem)
        sb("at_o", [P, TT, HALF], F32, out_mem)
        y_s5_lo = sb("y_s5_lo", [P, HT, S], F32R, out_mem)
        out_mem.close()
        odd_mem.close()

        def scratch(name, shape):
            return nc.dram_tensor(name, shape, F32, kind="Internal").ap()

        w1_dram = scratch("w1_dram", [P, 2 * PAIRS * P])
        w2_dram = scratch("w2_dram", [P, 2 * PAIRS * P])
        k_dram = scratch("k_dram", [GP, 2 * PAIRS, 2 * CH - 1, GP])
        rot_dram = scratch("rot_dram", [P, 2, PAIRS, CHUNKS])
        m8_dram = scratch("m8_dram", [P, PAIRS])
        u_dram = scratch("u_dram", [HT, P, CH, CHUNKS])
        y_dram = scratch("y_dram", [2 * PAIRS, GP, CH, CHUNKS])

        mlp_mem = ExitStack()
        g_hi = sb("g_hi", [P, FT, S], F32R, mlp_mem)
        g_lo = sb("g_lo", [P, FT, S], F32R, mlp_mem)
        conv = sb("conv", [P, 2, S], F32, mlp_mem)
        gelu = sb("gelu", [P, 2, S], F32, mlp_mem)
        gate = spare
        a_scaled = squares
        mlp_mem.close()

        order = [p for p in range(4) if p in parts]
        first_unit = {1: FIRST_MLP, 3: SECOND_MLP}
        stream = []
        for p in order:
            lo, hi = [(0, FIRST_MLP), (FIRST_MLP, O_U), (O_U, SECOND_MLP), (SECOND_MLP, N_UNITS)][p]
            stream += range(lo, hi)
        assert stream == list(range(stream[0], stream[-1] + 1))
        first = stream[0]
        n_stream = len(stream)

        def xl(m):
            return (squares, spare)[m // 2][:, m % 2, :]

        def rms_after(stage):
            return sum(2 - p % 2 for p in order[:stage + 1])

        block = ctx.enter_context(nc.Block())

        @block.sync
        def _(sp):
            sp.dma_start(cols[:], columns).then_inc(inputs_in, 16)
            xt = xT.rearrange("(k p) t -> k p t", p=P)
            ot = outT.rearrange("(k p) t -> k p t", p=P)
            for n in range(RAW_SLOTS):
                sp.dma_start(raw[:, n, :], units[first + n]).then_inc(landed[n], 16)
                for k in range(KT // RAW_SLOTS * n, KT // RAW_SLOTS * (n + 1)):
                    sp.dma_start(x[:, k, :], xt[k]).then_inc(x_in[k], 16)
            sp.dma_start(tabs[:], tables).then_inc(inputs_in, 16)
            if 2 in order:
                sp.dma_start(s5p[:], s5).then_inc(s5_in, 16)
            if 0 in order:
                sp.dma_start(ga[:], gates_a).then_inc(even_in, 16)
                sp.dma_start(gx[:], gates_x).then_inc(even_in, 16)

            def load(n, slot):
                return sp.dma_start(raw[:, slot, :], units[first + n]).then_inc(landed[slot], 16)

            rounds = n_stream // RAW_SLOTS
            with sp.Fori(1, rounds) as r:
                for slot in range(RAW_SLOTS):
                    sp.wait_ge(split, (r - 1) * RAW_SLOTS + slot + 1)
                    sp.dma_start(raw[:, slot, :], units[bass.ds(first + r * RAW_SLOTS + slot, 1), :, :]
                                 .rearrange("a p n -> (a p) n")).then_inc(landed[slot], 16)
            for n in range(rounds * RAW_SLOTS, n_stream):
                sp.wait_ge(split, n - RAW_SLOTS + 1)
                load(n, n % RAW_SLOTS)
            for k in range(KT):
                sp.wait_ge(x_ready, KT * (len(order) - 1) + k + 1)
                sp.dma_start(ot[k], x[:, k, :]).then_inc(out_stored, 16)
            sp.wait_ge(out_stored, 16 * KT)

        @block.gpsimd
        def _(pool):
            pool.memset(ones[:], 1.0).then_inc(consts_set, 1)
            pool.memset(eps[:], EPS).then_inc(consts_set, 1)
            pool.memset(zero[:], 0.0).then_inc(consts_set, 1)
            pool.wait_ge(consts_set, 3)

            def halves(slot, half, done):
                pool.tensor_tensor(w_hi[:, half, :], raw[:, slot, :], zero[:, 0:1].to_broadcast([P, UNIT]), ALU.add).then_inc(hi_split, 1)
                pool.wait_ge(hi_split, done)
                pool.tensor_tensor(w_lo[:, half, :], raw[:, slot, :], w_hi[:, half, :].bitcast(F32),
                                   ALU.subtract).then_inc(split, 1)

            def one(n):
                pool.wait_ge(landed[n % RAW_SLOTS], 16 * (n // RAW_SLOTS + 1))
                if n >= SPLIT_SLOTS:
                    pool.wait_ge(used, n - SPLIT_SLOTS + 1)
                halves(n % RAW_SLOTS, n % SPLIT_SLOTS, n + 1)

            for n in range(RAW_SLOTS):
                one(n)
            rounds = n_stream // RAW_SLOTS
            with pool.Fori(1, rounds) as r:
                for slot in range(RAW_SLOTS):
                    pool.wait_ge(landed[slot], r * 16 + 16)
                    pool.wait_ge(used, r * RAW_SLOTS + (slot - SPLIT_SLOTS + 1))
                    halves(slot, slot % SPLIT_SLOTS, r * RAW_SLOTS + (slot + 1))
            for n in range(rounds * RAW_SLOTS, n_stream):
                one(n)

        @block.tensor
        def _(pe):
            def sum_squares(stage, mixer):
                pe.wait_ge(added, KT * (stage + 1))
                pe.matmul(bank[6][:], ones[:], total[:], start=True, stop=True).then_inc(summed, 1)
                if mixer:
                    for t in range(TT):
                        mm = pe.matmul(bank[7][:, t:t + 1], total[:, t * P:(t + 1) * P], ones[:, 0:1], start=True, stop=True)
                    mm.then_inc(summed, 1)

            def product(out, slot, b, w_at, mov_hi, mov_lo, start, stop):
                hi, lo = w_hi[:, slot, w_at], w_lo[:, slot, w_at]
                pe.matmul(out, hi, mov_hi, start=start, stop=False)
                pe.matmul(out, hi, mov_lo, start=False, stop=False)
                return pe.matmul(out, lo, mov_hi, start=False, stop=stop)

            def w_block(b):
                return slice(b * P, (b + 1) * P)

            def mlp(stage, n0):
                base = FT * (stage // 2 if len(order) == 4 else 0)

                def up(i, u, wait_h):
                    for which, free in enumerate((scaled, gate_raw)):
                        slot = (n0 + which) % SPLIT_SLOTS
                        pe.wait_ge(split, i * 4 + (n0 + 2 * u + which + 1))
                        if not wait_h:
                            pe.wait_ge(free, i * 2 + (base + u - 1))
                        for k in range(KT):
                            if wait_h and u == 0 and which == 0:
                                pe.wait_ge(h_ready, KT * stage + k + 1)
                            mm = product(bank[2 * which + u][:], slot, k, w_block(k), h_hi[:, k, :], h_lo[:, k, :],
                                         k == 0, k == KT - 1)
                        mm.then_inc(used, 1)
                        if wait_h and u == 0 and which == 0:
                            sum_squares(stage, False)

                for u in range(2):
                    up(0, u, True)
                with pe.Fori(1, FT // 2) as i:
                    for u in range(2):
                        up(i, u, False)
                n1 = n0 + 2 * FT
                project(stage, n1, 3, lambda k: (g_hi[:, k, :], g_lo[:, k, :]), lambda k: pe.wait_ge(gate_ready, base + k + 1))

            def project(stage, n1, per_tile, y, wait_y):
                def tile(i, u, first_time):
                    for part in range(per_tile):
                        n = n1 + per_tile * u + part
                        pe.wait_ge(split, i * (2 * per_tile) + (n + 1))
                        if part == 0 and not first_time:
                            pe.wait_ge(x_ready, i * 2 + (KT * stage + u - 1))
                        for b in range(8):
                            k = part * 8 + b
                            if first_time and u == 0:
                                wait_y(k)
                            mm = product(bank[4 + u][:], n % SPLIT_SLOTS, b, w_block(b), *y(k),
                                         k == 0, k == 8 * per_tile - 1)
                        mm.then_inc(used, 1)

                for u in range(2):
                    tile(0, u, True)
                with pe.Fori(1, KT // 2) as i:
                    for u in range(2):
                        tile(i, u, False)

            def rows_unit(n, part, banks, stage, first_time):
                pe.wait_ge(split, n + 1)
                slot = n % SPLIT_SLOTS
                for b in range(2):
                    k = 2 * part + b
                    if first_time:
                        pe.wait_ge(h_ready, KT * stage + k + 1)
                    cols_ = slice(b * 512, (b + 1) * 512)
                    for t in range(TT):
                        out, at = bank[banks + t][:], slice(t * P, (t + 1) * P)
                        pe.matmul(out, h_hi[:, k, at], w_hi[:, slot, cols_], start=(k == 0), stop=False)
                        pe.matmul(out, h_hi[:, k, at], w_lo[:, slot, cols_], start=False, stop=False)
                        mm = pe.matmul(out, h_lo[:, k, at], w_hi[:, slot, cols_], start=False, stop=(k == KT - 1))
                mm.then_inc(used, 1)

            def tile_unit(n, b_out, stage, first_time=False):
                pe.wait_ge(split, n + 1)
                for k in range(KT):
                    if first_time:
                        pe.wait_ge(h_ready, KT * stage + k + 1)
                    mm = product(bank[b_out][:], n % SPLIT_SLOTS, k, w_block(k), h_hi[:, k, :], h_lo[:, k, :],
                                 k == 0, k == KT - 1)
                mm.then_inc(used, 1)

            def s5_prepare():
                pe.wait_ge(s5_bmat, BMAT_STEPS)
                pe.wait_ge(s5_diag, 4)
                for q in range(PAIRS):
                    out = bank[4][:, q * 2 * GP:(q + 1) * 2 * GP]
                    pe.matmul(out, b_mat[:, 0, q].rearrange("p l c -> p (l c)"), c_diag[:, 0, q], start=True, stop=False)
                    mm = pe.matmul(out, b_mat[:, 1, q].rearrange("p l c -> p (l c)"), c_diag[:, 1, q], start=False, stop=True)
                mm.then_inc(s5_prep_mm, 1)
                for n in range(8):
                    if n >= 3:
                        pe.wait_ge(s5_w1_out, n - 2)
                    for i in range(4):
                        q = 4 * n + i
                        mm = pe.transpose(bank[5 + n % 3][:, i * P:(i + 1) * P],
                                          b_mat[:, q // PAIRS, q % PAIRS].rearrange("p l c -> p (l c)"), table("identity"))
                    mm.then_inc(s5_prep_mm, 1)
                pe.wait_ge(s5_v_out, 1)
                pe.wait_ge(s5_w1_out, 8)

            def odd_mixer(stage):
                n0 = O_U - first
                if 0 not in order:
                    s5_prepare()
                tile_unit(n0, 0, stage, True)
                sum_squares(stage, True)
                for m in range(1, HT):
                    tile_unit(n0 + m, m, stage)
                tile_unit(O_GK - first, 4, stage)
                pe.wait_ge(rms_ready, rms_after(stage))
                pe.wait_ge(gk_ready, 1)
                pe.wait_ge(gk_in, 16)
                for i in range(2):
                    pe.matmul(bank[5 + i][:], gkw[:, i * P:(i + 1) * P], squares[0:16, 0, :], start=True,
                              stop=True).then_inc(gate_pre, 1)
                tile_unit(O_Q - first, 7, stage)
                tile_unit(O_Q - first + 1, 4, stage)
                pe.wait_ge(gk_logs, 2)
                tile_unit(O_K - first, 5, stage)
                tile_unit(O_K - first + 1, 6, stage)

                pe.wait_ge(u_ready, HT)
                pe.wait_ge(u_loaded, 16 * CH)
                pe.wait_ge(s5_loaded, 16)
                for ri in range(2):
                    for q in range(PAIRS):
                        for e in range(2):
                            mm = pe.matmul(bank[2 * ri + q // 8][64 * e:64 * e + 64, q % 8 * CHUNKS:(q % 8 + 1) * CHUNKS],
                                           wst[:, ri, q, 64 * e:64 * e + 64], u_in[:, 2 * q + e, :], start=True, stop=True)
                mm.then_inc(s5_local, 1)

                pe.wait_ge(gk_dec, 4)
                for part in range(4):
                    rows_unit(O_V - first + part, part, 4, stage, False)
                pe.wait_ge(vg_ready, TT)
                pe.wait_ge(w3_in, 16 * CH)
                pe.wait_ge(s5_w2_loaded, 16)
                pe.wait_ge(s5_step, S5_STEPS)
                for n in range(HT):
                    for q in range(4 * n, 4 * n + 4):
                        pair = slice(q % 4 * P, (q % 4 + 1) * P)
                        pe.matmul(bank[4 + n][:, pair], wst[:, 0, q, :], start_re[:, q].rearrange("p e c -> p (e c)"), start=True, stop=False)
                        pe.matmul(bank[4 + n][:, pair], wst[:, 1, q, :], start_im[:, q].rearrange("p e c -> p (e c)"), start=False, stop=False)
                        for e in range(2):
                            at = q % 4 * P + e * CHUNKS
                            mm = pe.matmul(bank[4 + n][:, at:at + CHUNKS], w3[:, 2 * q + e, :], u_in[:, 2 * q + e, :], start=False, stop=(e == 1))
                    mm.then_inc(s5_y_ready, 1)

                pe.wait_ge(gk_dec, 6)
                for i in range(2):
                    for t in range(TT):
                        mm = pe.transpose(bank[i][:, t * P:(t + 1) * P], logs[:, i, t * P:(t + 1) * P], table("identity"))
                    mm.then_inc(k_turned, 1)
                for h in range(GH):
                    b = (2, 3, 0, 1)[h]
                    if h >= 2:
                        pe.wait_ge(k_end_ready, 2)
                    rows = slice(64 * (h % 2), 64 * (h % 2) + 64)
                    for t in range(TT):
                        at = slice(t * P, (t + 1) * P)
                        mm = pe.matmul(bank[b][:, at], e_neg[rows, h // 2, at], e_pos[rows, h // 2, at], start=True, stop=True)
                    mm.then_inc(att_ready, 1)
                pe.wait_ge(s5_y_out, 4)
                for n in range(GN - 1):
                    rows = slice(64 * (n % 2), 64 * (n % 2) + 64)
                    for h in range(GH):
                        col = (n // 2 % 2) * 256 + (h // 2) * DV
                        mm = pe.matmul(bank[4 + 2 * (n % 2) + n // 4][64 * (h % 2):64 * (h % 2) + 64, col:col + DV],
                                       k_end[rows, h // 2, n // 2 * P + 64 * (h % 2):n // 2 * P + 64 * (h % 2) + 64],
                                       vg[rows, n // 2, h * DV:(h + 1) * DV], start=True, stop=True)
                    mm.then_inc(kv_ready, 1)
                pe.wait_ge(attT_ready, GH)
                for t in range(TT):
                    for h in range(GH):
                        mm = pe.matmul(bank[t][:, h * DV:(h + 1) * DV], attT[:, h, t * P:(t + 1) * P],
                                       vg[:, t, h * DV:(h + 1) * DV], start=True, stop=True)
                    mm.then_inc(intra_ready, 1)
                pe.wait_ge(state_step, 1 + 2 * (GN - 1))
                for t in range(TT):
                    for e in range(2):
                        for n in (2 * t, 2 * t + 1):
                            for i in range(2):
                                rows = slice(64 * e, 64 * e + 64)
                                col = (t % 2) * 256 + i * DV
                                mm = pe.matmul(bank[4 + 2 * e + t // 2][64 * (n % 2):64 * (n % 2) + 64, col:col + DV],
                                               e_pos[rows, i, n * GC:(n + 1) * GC], state[rows, n, i, :],
                                               start=True, stop=True)
                    mm.then_inc(inter_ready, 1)

                pe.wait_ge(o_ready, TT)
                for part in range(4):
                    rows_unit(O_G - first + part, part, 0, stage, False)
                pe.wait_ge(ys_split, 2)
                for part in range(2):
                    n = O_GLU - first + part
                    pe.wait_ge(split, n + 1)
                    for b in range(8):
                        m, k = 2 * part + b // HT, b % HT
                        mm = product(bank[4 + m][:], n % SPLIT_SLOTS, b, w_block(b), ys_hi[:, k, :], ys_lo[:, k, :], k == 0, k == HT - 1)
                    mm.then_inc(used, 1)
                pe.wait_ge(o_step, 2)
                for h in range(GH):
                    for t in range(TT):
                        mm = pe.transpose(bank[h][:, t * P:(t + 1) * P], o[:, t, h * P:(h + 1) * P], table("identity"))
                    mm.then_inc(o_turned, 1)
                project(stage, O_O - first, 1, lambda k: (y_s5_hi[:, k, :], y_s5_lo[:, k, :]) if k < HT
                        else (y_gla_hi[:, k - HT, :], y_gla_lo[:, k - HT, :]), lambda k: pe.wait_ge(*((s5_out, k + 1) if k < HT else (gla_y, k - HT + 1))))

            def even_mixer(stage):
                for part in range(4):
                    rows_unit(E_Q + part, part, 0, stage, True)
                    if part == 2:
                        sum_squares(stage, True)
                pe.wait_ge(rms_ready, 2)
                for part in range(4):
                    rows_unit(E_K + part, part, 4, stage, False)
                pe.wait_ge(qk_step, 4)
                for part in range(4):
                    rows_unit(E_V + part, part, 0, stage, False)
                pe.wait_ge(qk_step, 8)
                for m in range(HT):
                    tile_unit(E_X + m, 4 + m, stage)
                pe.wait_ge(xl_scaled, HT)
                if 2 in order:
                    s5_prepare()
                pe.wait_ge(v_ready, TT)
                tile_unit(E_G, 0, stage)
                pe.wait_ge(qk_step, QK_STEPS)
                for n in range(2 * HT):
                    which, hp = n // HT, n % HT
                    if n == HT:
                        tile_unit(E_G + 1, 1, stage)
                    if n >= HT:
                        pe.wait_ge(qkT_ready, n - HT + 1)
                    for t in range(TT):
                        mm = pe.transpose(bank[4 + n % 4][:, t * P:(t + 1) * P],
                                          qk[:, which, t, hp * P:(hp + 1) * P], table("identity"))
                    mm.then_inc(qk_turned, 1)
                pe.wait_ge(even_in, 32)
                for m in range(HT):
                    if m == 0:
                        pe.wait_ge(x_conv, 3 * HT)
                    if m >= 2:
                        pe.wait_ge(gate_sig, 2 * m - 2)
                    if m == 0:
                        pe.wait_ge(qkT_ready, 2 * HT)
                    b = 4 + 2 * (m % 2)
                    pe.matmul(bank[b][:], ga[:, m, :], xc[:, m, :], start=True, stop=True).then_inc(gates_made, 1)
                    pe.matmul(bank[b + 1][:], gx[:, m, :], xc[:, m, :], start=True, stop=True).then_inc(gates_made, 1)
                for m in range(2, HT):
                    tile_unit(E_G + m, m, stage)
                def scores(n):
                    hp, t = divmod(n, TT)
                    if n >= 2:
                        pe.wait_ge(masked, 2 * (n - 1))
                    for e in range(2):
                        rows = slice(64 * e, 64 * e + 64)
                        mm = pe.matmul(bank[2 * e + n % 2][:, 0:(t + 1) * P], qT[rows, hp, t * P:(t + 1) * P],
                                       kT[rows, hp, 0:(t + 1) * P], start=True, stop=True)
                    mm.then_inc(scores_ready, 1)

                def turn(n):
                    t = n % TT
                    pe.wait_ge(probs_ready, 2 * n + 2)
                    if n >= 1:
                        pe.wait_ge(probT_ready, 2 * n)
                    for e in range(2):
                        for j in range(t + 1):
                            mm = pe.transpose(bank[4 + e][:, j * P:(j + 1) * P], prob[:, n % 2, e, j * P:(j + 1) * P],
                                              table("identity"))
                    mm.then_inc(probs_turned, 1)

                def values(n):
                    hp, t = divmod(n, TT)
                    pe.wait_ge(probT_ready, 2 * n + 2)
                    if t == 0 and hp >= 2:
                        pe.wait_ge(att_y, 2 * (hp - 1))
                    for e in range(2):
                        head = 2 * hp + e
                        for j in range(t + 1):
                            mm = pe.matmul(bank[6 + hp % 2][64 * e:64 * e + 64, t * P:(t + 1) * P],
                                           v[:, j, head * HD:(head + 1) * HD], probT[:, n % 2, e, j * P:(j + 1) * P],
                                           start=(j == 0), stop=(j == t))
                    mm.then_inc(pv_done, 1)

                pe.wait_ge(gate_sig, 2 * HT)
                pe.wait_ge(gl_scaled, HT)
                pe.wait_ge(qkT_ready, 2 * HT)
                scores(0)
                scores(1)
                for n in range(ATT_STEPS):
                    if n + 2 < ATT_STEPS:
                        scores(n + 2)
                    turn(n)
                    if n >= 1:
                        values(n - 1)
                values(ATT_STEPS - 1)
                project(stage, E_O, 1, lambda k: (y_lru_hi[:, k, :], y_lru_lo[:, k, :]) if k < HT
                        else (y_att_hi[:, k - HT, :], y_att_lo[:, k - HT, :]),
                        lambda k: pe.wait_ge(*((lru_y, k + 1) if k < HT else (att_y, 2 * (k - HT) + 2))))

            pe.wait_ge(consts_set, 3)
            for stage, part in enumerate(order):
                if part == 0:
                    even_mixer(stage)
                if part == 2:
                    odd_mixer(stage)
                if part in (1, 3):
                    mlp(stage, first_unit[part] - first)

        @block.scalar
        def _(act):
            def gain_tile(stage, k, u):
                xk = x[:, bass.ds(k, 1), :].rearrange("p a t -> p (a t)")
                hk = h_hi[:, bass.ds(k, 1), :].rearrange("p a t -> p (a t)")
                act.activation(hk, xk, ACT.Identity, bias=zero[:, 0:1],
                               scale=cols[:, bass.ds(COL["norm"] + KT * order[stage] + k, 1)]).then_inc(gained_hi, 1)
                act.activation(squares[:, u, :], xk, ACT.Square).then_inc(squared, 1)

            def take_x():
                act.wait_ge(consts_set, 3)
                act.wait_ge(inputs_in, 16)
                for k in range(KT):
                    act.wait_ge(x_in[k], 16)
                    if k >= 2:
                        act.wait_ge(added, k - 1)
                    gain_tile(0, k, k % 2)

            def take_residual(stage):
                def tile(i, u, warm):
                    act.wait_ge(x_ready, i * 2 + (KT * stage + u + 1))
                    if warm:
                        act.wait_ge(added, i * 2 + (KT * (stage + 1) + u - 1))
                    gain_tile(stage + 1, i * 2 + u, u)

                for u in range(2):
                    tile(0, u, False)
                with act.Fori(1, KT // 2) as i:
                    for u in range(2):
                        tile(i, u, True)

            def find_rms(stage, mixer):
                act.wait_ge(summed, rms_after(stage) - mixer)
                act.activation(rstd[:], bank[6][:], ACT.Sqrt, bias=eps[:, 0:1], scale=1.0 / D).then_inc(rms_ready, 1)
                if mixer:
                    act.wait_ge(summed, rms_after(stage))
                    act.activation(rstd_t[:], bank[7][:, 0:TT], ACT.Sqrt, bias=eps[:, 0:1], scale=1.0 / D).then_inc(rms_ready, 1)

            def mlp(stage, layer, n0):
                base = FT * (stage // 2 if len(order) == 4 else 0)

                def tile(i, u, warm):
                    j = i * 2 + u
                    act.wait_ge(scaled, i * 2 + (base + u + 1))
                    if warm:
                        act.wait_ge(gelu_done, i * 2 + (base + u - 1))
                    w = COL["mlp_w"] + layer * 3 * FT + 2 * FT
                    b = COL["mlp_b"] + layer * FT
                    act.activation(conv[:, u, :], a_scaled[:, u, :], ACT.Identity,
                                   bias=cols[:, bass.ds(b + j, 1)], scale=cols[:, bass.ds(w + j, 1)]).then_inc(newest_tap, 1)
                    act.wait_ge(conv_done, i * 2 + (base + u + 1))
                    if warm:
                        act.wait_ge(gate_done, i * 2 + (base + u - 1))
                    act.activation(gelu[:, u, :], conv[:, u, :], ACT.Gelu_apprx_tanh).then_inc(gelu_done, 1)

                for u in range(2):
                    tile(0, u, False)
                with act.Fori(1, FT // 2) as i:
                    for u in range(2):
                        tile(i, u, True)

            def s5_diagonal():
                act.wait_ge(s5_in, 16)
                act.wait_ge(w3_zero, 1)
                for ri in range(2):
                    for e in range(2):
                        rows = slice(64 * e, 64 * e + 64)
                        c0 = 3 * PAIRS + (2 + ri) * PAIRS * GP
                        act.activation(c_diag[rows, ri, :, e * GP:(e + 1) * GP],
                                       s5p[rows, c0:c0 + PAIRS * GP].rearrange("p (q c) -> p q c", c=GP),
                                       ACT.Copy, scale=(1.0, -1.0)[ri]).then_inc(s5_diag, 1)
            def s5_phases():
                act.wait_ge(s5_small, TURN_STEPS)
                act.activation(rot_s[:], turns[:], ACT.Sin, scale=TWO_PI).then_inc(s5_sin, 1)
                act.activation(rot_c[:], turns[:], ACT.Sin, scale=TWO_PI / 2).then_inc(s5_sin, 1)

            def s5_store_rotations():
                act.wait_ge(s5_small, PHASE_STEPS)
                act.dma_start(rot_dram[:, 0], rot_c[:, :, POWERS:ANGLES]).then_inc(s5_rot_stored, 16)
                act.dma_start(rot_dram[:, 1], rot_s[:, :, POWERS:ANGLES]).then_inc(s5_rot_stored, 16)
                act.wait_ge(s5_small, MAG_STEPS)
                act.activation(small[:, 16], mag[:, :, CH], ACT.Copy).then_inc(s5_m8, 1)
                act.wait_ge(s5_m8, 1)
                act.dma_start(m8_dram, small[:, 16]).then_inc(s5_stored, 16)
                zeros = GP * (CH - 1)
                act.wait_ge(w3_zero, 1)
                act.dma_start(k_dram.rearrange("p (a b) k c -> (p a) b (k c)", b=4)[:, :, 0:zeros],
                              stage_zero[:, 0:4 * zeros].rearrange("p (b n) -> p b n", b=4)).then_inc(s5_stored, 16)

            def s5_prepare():
                act.wait_ge(s5_prep_mm, 1)
                act.activation(stage_v, bank[4][:], ACT.Copy).then_inc(s5_v_out, 1)
                for n in range(8):
                    act.wait_ge(s5_prep_mm, n + 2)
                    slot = n % W1_SLOTS
                    if n >= W1_SLOTS:
                        act.wait_ge(s5_w1_stored[slot], 16)
                    act.activation(stage_w1[:, slot, :], bank[5 + n % 3][:], ACT.Copy).then_inc(s5_w1_out, 1)
                    act.wait_ge(s5_w1_out, n + 1)
                    act.dma_start(w1_dram[:, n * 512:(n + 1) * 512], stage_w1[:, slot, :]).then_inc(s5_w1_stored[slot], 16)
                act.wait_ge(s5_v_out, 1)
                for e in range(CH):
                    act.dma_start(k_dram[:, :, CH - 1 + e, :], stage_v[e * GP:(e + 1) * GP, :].rearrange("p (g c) -> p g c", c=GP))\
                       .then_inc(s5_stored, 16)

            def s5_store_output():
                act.wait_ge(s5_bmat, CMAT_STEPS)
                act.dma_start(w2_dram, b_mat[:].rearrange("p r q l c -> p (r q l c)")).then_inc(s5_w2_stored, 16)

            def odd_mixer(stage):
                if 0 not in order:
                    s5_store_rotations()
                    s5_prepare()
                    s5_store_output()
                act.wait_ge(s5_stored, 16 * S5_STORES)
                act.wait_ge(s5_rot_stored, 32)
                act.wait_ge(s5_w2_stored, 16)
                for slot in range(W1_SLOTS):
                    act.wait_ge(s5_w1_stored[slot], 32)
                act.dma_start(gkw[:], gk_w).then_inc(gk_in, 16)
                act.dma_start(wst[:].rearrange("p r q n -> p (r q n)"), w1_dram).then_inc(s5_loaded, 16)
                act.dma_start(rot[:], rot_dram).then_inc(s5_rot_in, 16)
                act.dma_start(m8[:], m8_dram).then_inc(s5_rot_in, 16)
                find_rms(stage, 1)
                for m in range(HT):
                    act.wait_ge(u_ready, m + 1)
                    act.dma_start(u_dram[m], u[:, m]).then_inc(u_stored, 16)
                act.wait_ge(u_stored, 16 * HT)
                ud = u_dram.rearrange("m (g p) l c -> p (m g) l c", p=GP)
                for e in range(CH):
                    act.dma_start(u_in[e * GP:(e + 1) * GP], ud[:, :, CH - 1 - e, :]).then_inc(u_loaded, 16)
                for e in range(CH):
                    act.dma_start(w3[e * GP:(e + 1) * GP], k_dram[:, :, e:e + CH, :].rearrange("p g k c -> p g (k c)"))\
                       .then_inc(w3_in, 16)
                act.wait_ge(gk_logs, 2)
                act.activation(e_pos[:], logs[:], ACT.Abs).then_inc(gk_abs, 1)
                act.wait_ge(gk_abs, 1)
                act.activation(e_pos[:], e_pos[:], ACT.Exp, scale=-1.0).then_inc(gk_abs, 1)
                act.wait_ge(gk_abs, 2)
                act.activation(e_pos[:], e_pos[:], ACT.Ln, bias=ones[:, 0:1]).then_inc(gk_abs, 1)
                act.wait_ge(gk_sum, 3)
                act.activation(e_pos[:], logs[:], ACT.Exp, scale=1.0 / 16).then_inc(gk_exp, 1)
                act.activation(e_neg[:], logs[:], ACT.Exp, scale=-1.0 / 16).then_inc(gk_exp, 1)
                act.wait_ge(s5_local, 1)
                act.dma_start(wst[:].rearrange("p r q n -> p (r q n)"), w2_dram).then_inc(s5_w2_loaded, 16)
                act.wait_ge(used, O_V - first + 4)
                for t in range(TT):
                    act.activation(vg[:, t, :], bank[4 + t][:], ACT.Identity, bias=zero[:, 0:1],
                                   scale=rstd_t[:, t:t + 1]).then_inc(vg_ready, 1)
                for n in range(HT):
                    act.wait_ge(s5_y_ready, n + 1)
                    dst = st[:, 0:2].rearrange("p a q c -> p (a q) c")[:, 8 * n:8 * n + 8, :]
                    act.activation(dst, bank[4 + n][:].rearrange("p (g c) -> p g c", c=CHUNKS), ACT.Copy).then_inc(s5_y_out, 1)
                act.wait_ge(k_turned, 2)
                for i in range(2):
                    act.activation(k_end[:, i, :], bank[i][:], ACT.Copy).then_inc(k_end_ready, 1)
                act.wait_ge(s5_y_out, 4)
                yd = y_dram.rearrange("g p l c -> p g l c")
                for l in range(CH):
                    act.dma_start(yd[:, :, l, :], st[l * GP:(l + 1) * GP, 0:2].rearrange("p a q c -> p (a q) c"))\
                       .then_inc(y_stored, 16)
                act.wait_ge(y_stored, 16 * CH)
                y_in = u_in[:].rearrange("p g c -> p (g c)").rearrange("p (m n) -> p m n", m=HT)
                act.dma_start(y_in, y_dram.rearrange("(m g) p l c -> (g p) m (l c)", m=HT)).then_inc(y_loaded, 16)
                for t in range(TT):
                    act.wait_ge(inter_ready, t // 2 * 2 + 2)
                    for e in range(2):
                        dst = o[:, t, :].rearrange("p (i e d) -> p i e d", i=2, e=2)[:, :, e, :]
                        src = bank[4 + 2 * e + t // 2][:, t % 2 * 256:t % 2 * 256 + 256].rearrange("p (i d) -> p i d", i=2)
                        act.activation(dst, src, ACT.Copy).then_inc(inter_out, 1)
                act.wait_ge(ys_ready, 1)
                act.activation(u_in[:], u_in[:], ACT.Gelu_apprx_tanh).then_inc(ys_gelu, 1)
                act.wait_ge(ys_gelu, 1)
                act.activation(ys_hi[:], y_in, ACT.Copy).then_inc(ys_split, 1)
                for t in range(TT):
                    act.wait_ge(o_ready, t + 1)
                    if t >= 2:
                        act.wait_ge(o_sum, t - 1)
                    act.activation(squares[:, t % 2, :], o[:, t, :], ACT.Square).then_inc(o_squared, 1)
                act.wait_ge(o_sum, TT)
                act.activation(gla_var[:], gla_var[:], ACT.Sqrt, bias=eps[:, 0:1], scale=1.0 / DV).then_inc(o_rms, 1)
                act.wait_ge(used, O_G - first + 4)
                for t in range(TT):
                    act.activation(sg[:, t, :], bank[t][:], ACT.Silu, scale=rstd_t[:, t:t + 1]).then_inc(sg_ready, 1)
                sig = st[:, 0:2].rearrange("p a q c -> p (a q c)").rearrange("p (m n) -> p m n", m=HT)
                for part in range(2):
                    act.wait_ge(used, O_GLU - first + part + 1)
                    for m in (2 * part, 2 * part + 1):
                        act.activation(sig[:, m], bank[4 + m][:], ACT.Sigmoid, bias=column("glu_b", m)).then_inc(glu_sig, 1)
                    for m in (2 * part, 2 * part + 1):
                        act.wait_ge(s5_gated, m + 1)
                        act.activation(y_s5_hi[:, m, :].rearrange("p (c l) -> p c l", l=CH),
                                       y_in[:, m].rearrange("p (l c) -> p c l", c=CHUNKS), ACT.Copy).then_inc(s5_hi, 1)
                for h in range(GH):
                    act.wait_ge(o_turned, h + 1)
                    act.activation(y_gla_hi[:, h, :], bank[h][:], ACT.Copy).then_inc(gla_hi, 1)

            def even_mixer(stage):
                if 2 in order:
                    s5_diagonal()
                find_rms(stage, 1)
                if 2 in order:
                    s5_phases()
                act.wait_ge(lam_step, LAM_ABS)
                act.activation(lam_tmp[:, 0, :], lam_tmp[:, 5, :], ACT.Exp).then_inc(lam_exp, 1)
                act.wait_ge(rstd_ready, 2)
                for which in range(2):
                    act.wait_ge(used, 4 * which + 4)
                    for t in range(TT):
                        n = TT * which + t
                        if n >= 2:
                            act.wait_ge(qk_sum, n - 1)
                        act.activation(squares[:, n % 2, :], bank[4 * which + t][:], ACT.Square,
                                       scale=rstd_t[:, t:t + 1]).then_inc(qk_squared, 1)
                    act.wait_ge(qk_sum, TT * (which + 1))
                    act.activation(qk_var[:, which, :], qk_var[:, which, :], ACT.Sqrt, bias=eps[:, 0:1],
                                   scale=1.0 / HD).then_inc(qk_rms, 1)
                act.wait_ge(used, 12)
                for t in range(TT):
                    act.activation(v[:, t, :], bank[t][:], ACT.Identity, bias=zero[:, 0:1],
                                   scale=rstd_t[:, t:t + 1]).then_inc(v_ready, 1)
                if 2 in order:
                    s5_store_rotations()
                    act.wait_ge(s5_rot_stored, 32)
                for m in range(HT):
                    act.wait_ge(xl_scaled, m + 1)
                    act.activation(xc[:, m, :], xl(m), ACT.Identity, bias=column("lru_b", m),
                                   scale=column("lru_w", 3 * HT + m)).then_inc(x_newest, 1)
                if 2 in order:
                    s5_prepare()
                    act.wait_ge(s5_stored, 16 * S5_STORES)
                    for slot in range(W1_SLOTS):
                        act.wait_ge(s5_w1_stored[slot], 32)
                for n in range(2 * HT):
                    act.wait_ge(qk_turned, n + 1)
                    dst = (qT, kT)[n // HT]
                    act.activation(dst[:, n % HT, :], bank[4 + n % 4][:], ACT.Copy).then_inc(qkT_ready, 1)
                if 2 in order:
                    s5_store_output()
                    act.wait_ge(s5_w2_stored, 16)
                for m in range(HT):
                    b = 4 + 2 * (m % 2)
                    act.wait_ge(gates_made, 2 * m + 1)
                    act.activation(rg[:, m, :], bank[b][:], ACT.Sigmoid, bias=column("gate_a_b", m)).then_inc(gate_sig, 1)
                    act.wait_ge(gates_made, 2 * m + 2)
                    act.activation(ig[:, m, :], bank[b + 1][:], ACT.Sigmoid, bias=column("gate_x_b", m)).then_inc(gate_sig, 1)
                act.wait_ge(gate_sig, 2 * HT)
                act.wait_ge(lam_step, LAM_STEPS)
                for m in range(HT):
                    act.activation(coef[:, m, :], rg[:, m, :], ACT.Tanh, scale=neg_c[:, m:m + 1]).then_inc(lru_exp, 1)
                for m in range(HT):
                    act.activation(decay[:, m, :], rg[:, m, :], ACT.Exp, scale=pos_c[:, m:m + 1]).then_inc(lru_exp, 1)
                for m in range(HT):
                    act.wait_ge(gl_scaled, m + 1)
                    act.activation(xl(m), xl(m), ACT.Gelu_apprx_tanh).then_inc(gg_ready, 1)

                def exps(n):
                    act.wait_ge(negmax_ready, n + 1)
                    w = (n % TT + 1) * P
                    for e in range(2):
                        act.activation(prob[:, n % 2, e, 0:w], prob[:, n % 2, e, 0:w], ACT.Exp,
                                       bias=neg_max[:, n % 2, e:e + 1], scale=HD ** -0.5,
                                       accum_out=row_sum[:, n % 2, e:e + 1]).then_inc(exped, 1)

                def copy_turned(n):
                    w = (n % TT + 1) * P
                    act.wait_ge(probs_turned, n + 1)
                    if n >= 2:
                        act.wait_ge(pv_done, n - 1)
                    for e in range(2):
                        act.activation(probT[:, n % 2, e, 0:w], bank[4 + e][:, 0:w], ACT.Copy).then_inc(probT_ready, 1)

                exps(0)
                for n in range(ATT_STEPS):
                    if n + 1 < ATT_STEPS:
                        exps(n + 1)
                    copy_turned(n)
                    if n == LRU_STEP:
                        act.wait_ge(lru_step, 3)
                        act.activation(coef[:], coef[:], ACT.Sqrt, scale=2.0).then_inc(lru_sqrt, 1)

            take_x()
            if 2 in order and 0 not in order:
                s5_diagonal()
                s5_phases()
            for stage, part in enumerate(order):
                if part == 0:
                    even_mixer(stage)
                if part == 2:
                    odd_mixer(stage)
                if part in (1, 3):
                    find_rms(stage, 0)
                    mlp(stage, part // 2, first_unit[part] - first)
                if stage < len(order) - 1:
                    take_residual(stage)

        @block.vector
        def _(dve):
            def low_half(stage, k, gained, u):
                xk = x[:, bass.ds(k, 1), :].rearrange("p a t -> p (a t)")
                hi = h_hi[:, bass.ds(k, 1), :].rearrange("p a t -> p (a t)").bitcast(F32)
                lo = h_lo[:, bass.ds(k, 1), :].rearrange("p a t -> p (a t)")
                dve.wait_ge(gained_hi, gained)
                dve.scalar_tensor_tensor(out=lo, in0=xk, scalar=cols[:, bass.ds(COL["norm"] + KT * order[stage] + k, 1)],
                                         in1=hi, op0=ALU.mult, op1=ALU.subtract).then_inc(h_ready, 1)
                dve.wait_ge(squared, gained)
                dve.tensor_tensor(total[:], total[:], squares[:, u, :], ALU.add).then_inc(added, 1)

            def clear_total(stage):
                dve.memset(total[:], 0.0).then_inc(total_clear, 1)
                dve.wait_ge(total_clear, stage + 1)

            def take_x():
                clear_total(0)
                dve.wait_ge(inputs_in, 16)
                for k in range(KT):
                    if k >= 1:
                        dve.wait_ge(added, k)
                    low_half(0, k, k + 1, k % 2)

            def find_rstd(stage, mixer):
                dve.wait_ge(rms_ready, rms_after(stage) - mixer)
                dve.reciprocal(rstd[:], rstd[:]).then_inc(rstd_ready, 1)
                if mixer:
                    dve.wait_ge(rms_ready, rms_after(stage))
                    dve.reciprocal(rstd_t[:], rstd_t[:]).then_inc(rstd_ready, 1)
                dve.wait_ge(rstd_ready, rms_after(stage))

            def add_residual(stage, n1, per_tile):
                last = stage == len(order) - 1

                def tile(i, u):
                    m = i * 2 + u
                    dve.wait_ge(used, i * (2 * per_tile) + (n1 + per_tile * (u + 1)))
                    xm = x[:, bass.ds(m, 1), :].rearrange("p a t -> p (a t)")
                    dve.tensor_tensor(xm, bank[4 + u][:], xm, ALU.add).then_inc(x_ready, 1)
                    if not last:
                        dve.wait_ge(added, i * 2 + (KT * (stage + 1) + u))
                        low_half(stage + 1, m, i * 2 + (KT * (stage + 1) + u + 1), u)

                if not last:
                    dve.wait_ge(used, n1 + 1)
                    clear_total(stage + 1)
                with dve.Fori(0, KT // 2) as i:
                    for u in range(2):
                        tile(i, u)

            def mlp(stage, layer, n0):
                base = FT * (stage // 2 if len(order) == 4 else 0)

                def tile(i, u):
                    j = i * 2 + u
                    w = COL["mlp_w"] + layer * 3 * FT
                    dve.wait_ge(used, i * 4 + (n0 + 2 * u + 1))
                    dve.tensor_tensor(a_scaled[:, u, :], bank[u][:], rstd[:], ALU.mult).then_inc(scaled, 1)
                    dve.wait_ge(newest_tap, i * 2 + (base + u + 1))
                    dve.scalar_tensor_tensor(out=conv[:, u, 1:S], in0=a_scaled[:, u, 0:S - 1],
                                             scalar=cols[:, bass.ds(w + FT + j, 1)], in1=conv[:, u, 1:S],
                                             op0=ALU.mult, op1=ALU.add).then_inc(middle_tap, 1)
                    dve.wait_ge(middle_tap, i * 2 + (base + u + 1))
                    dve.scalar_tensor_tensor(out=conv[:, u, 2:S], in0=a_scaled[:, u, 0:S - 2],
                                             scalar=cols[:, bass.ds(w + j, 1)], in1=conv[:, u, 2:S],
                                             op0=ALU.mult, op1=ALU.add).then_inc(conv_done, 1)
                    dve.wait_ge(gelu_done, i * 2 + (base + u + 1))
                    dve.wait_ge(used, i * 4 + (n0 + 2 * u + 2))
                    dve.tensor_tensor(gate[:, u, :], bank[2 + u][:], gelu[:, u, :], ALU.mult).then_inc(gate_raw, 1)
                    dve.wait_ge(gate_raw, i * 2 + (base + u + 1))
                    dve.tensor_tensor(gate[:, u, :], gate[:, u, :], rstd[:], ALU.mult).then_inc(gate_done, 1)
                    dve.wait_ge(gate_done, i * 2 + (base + u + 1))
                    gj_hi = g_hi[:, bass.ds(j, 1), :].rearrange("p a t -> p (a t)")
                    gj_lo = g_lo[:, bass.ds(j, 1), :].rearrange("p a t -> p (a t)")
                    dve.tensor_copy(gj_hi, gate[:, u, :]).then_inc(gate_hi_done, 1)
                    dve.wait_ge(gate_hi_done, i * 2 + (base + u + 1))
                    dve.tensor_tensor(gj_lo, gate[:, u, :], gj_hi.bitcast(F32), ALU.subtract).then_inc(gate_ready, 1)

                with dve.Fori(0, FT // 2) as i:
                    for u in range(2):
                        tile(i, u)

            def lru_constants():
                lam = cols[:, COL["lambda"]:COL["lambda"] + HT]
                z, w, w2, acc, neg, tmp = (lam_tmp[:, i, :] for i in range(6))
                step = [0]

                def then(ins):
                    ins.then_inc(lam_step, 1)
                    step[0] += 1
                    dve.wait_ge(lam_step, step[0])

                dve.wait_ge(inputs_in, 32)
                then(dve.tensor_scalar(neg, lam, -1.0, 0.0, ALU.mult, ALU.max))
                then(dve.scalar_tensor_tensor(out=tmp, in0=neg, scalar=-2.0, in1=lam, op0=ALU.mult, op1=ALU.subtract))
                assert step[0] == LAM_ABS
                dve.wait_ge(lam_exp, 1)
                then(dve.tensor_scalar(tmp, z, 2.0, None, ALU.add))
                then(dve.reciprocal(tmp, tmp))
                then(dve.tensor_tensor(w, z, tmp, ALU.mult))
                then(dve.tensor_tensor(w2, w, w, ALU.mult))
                then(dve.tensor_scalar(acc, w2, ATANH[-1], ATANH[-2], ALU.mult, ALU.add))
                for c in ATANH[-3::-1]:
                    then(dve.tensor_tensor(acc, acc, w2, ALU.mult))
                    then(dve.tensor_scalar(acc, acc, c, None, ALU.add))
                then(dve.tensor_tensor(acc, acc, w, ALU.mult))
                then(dve.scalar_tensor_tensor(out=acc, in0=acc, scalar=2.0, in1=neg, op0=ALU.mult, op1=ALU.add))
                then(dve.tensor_scalar(neg_c[:], acc, 8.0, None, ALU.mult))
                then(dve.tensor_scalar(pos_c[:], acc, -8.0, None, ALU.mult))
                assert step[0] == LAM_STEPS

            lr, li = s5p[:, 0:PAIRS], s5p[:, PAIRS:2 * PAIRS]
            step, zr, th, q, f, fh, fl = (small[:, i] for i in range(7))
            done = [0]

            def then(ins):
                ins.then_inc(s5_small, 1)
                done[0] += 1
                dve.wait_ge(s5_small, done[0])

            def spread(a, n):
                return a.unsqueeze(2).broadcast_to([P, PAIRS, n])

            ks = table("angles").unsqueeze(1).broadcast_to([P, PAIRS, ANGLES])

            def exp(out, z):
                n, r, acc, bits = (small[:, i] for i in range(7, 11))
                then(dve.tensor_scalar(r, z, 89.0, -110.0, ALU.min, ALU.max))
                then(dve.tensor_scalar(n, r, float(np.log2(np.e)), ROUND, ALU.mult, ALU.add))
                then(dve.tensor_scalar(n, n, ROUND, None, ALU.subtract))
                for part in LN2_PARTS:
                    then(dve.scalar_tensor_tensor(out=r, in0=n, scalar=-part, in1=r, op0=ALU.mult, op1=ALU.add))
                then(dve.tensor_scalar(acc, r, 1 / 5040, None, ALU.mult))
                for c in (1 / 720, 1 / 120, 1 / 24, 1 / 6, 1 / 2, 1.0):
                    then(dve.scalar_tensor_tensor(out=acc, in0=acc, scalar=c, in1=r, op0=ALU.add, op1=ALU.mult))
                then(dve.tensor_scalar(n, n, 126.0, 0.0, ALU.add, ALU.max))
                then(dve.tensor_scalar(bits.bitcast(I32), n, float(2 ** 23), None, ALU.mult))
                then(dve.scalar_tensor_tensor(out=acc, in0=acc, scalar=1.0, in1=bits, op0=ALU.add, op1=ALU.mult))
                then(dve.tensor_scalar(out, acc, 2.0, None, ALU.mult))

            def s5_turns():
                dve.wait_ge(inputs_in, 32)
                dve.wait_ge(s5_in, 16)
                exp(step, s5p[:, 2 * PAIRS:3 * PAIRS])
                then(dve.tensor_tensor(th, li, step, ALU.mult))
                then(dve.tensor_scalar(q, th, 1 / (2 * np.pi), ROUND, ALU.mult, ALU.add))
                then(dve.tensor_scalar(q, q, ROUND, None, ALU.subtract))
                for part in PI_PARTS:
                    then(dve.scalar_tensor_tensor(out=th, in0=q, scalar=-part, in1=th, op0=ALU.mult, op1=ALU.add))
                then(dve.tensor_scalar(f, th, 1 / (2 * np.pi), None, ALU.mult))
                then(dve.tensor_scalar(fh, f, ROUND12, ROUND12, ALU.add, ALU.subtract))
                then(dve.tensor_tensor(fl, f, fh, ALU.subtract))
                then(dve.tensor_tensor(turns[:], ks, spread(fh, ANGLES), ALU.mult))
                then(dve.tensor_scalar(rot_s[:], turns[:], ROUND, ROUND, ALU.add, ALU.subtract))
                then(dve.tensor_tensor(turns[:], turns[:], rot_s[:], ALU.subtract))
                then(dve.tensor_tensor(rot_c[:], ks, spread(fl, ANGLES), ALU.mult))
                then(dve.tensor_tensor(turns[:], turns[:], rot_c[:], ALU.add))
                then(dve.tensor_scalar(rot_s[:], turns[:], ROUND, ROUND, ALU.add, ALU.subtract))
                then(dve.tensor_tensor(turns[:], turns[:], rot_s[:], ALU.subtract))
                assert done[0] == TURN_STEPS, done

            def s5_rotations():
                dve.wait_ge(s5_sin, 2)
                then(dve.tensor_tensor(turns[:], rot_c[:], rot_c[:], ALU.mult))
                then(dve.tensor_scalar(rot_c[:], turns[:], -2.0, 1.0, ALU.mult, ALU.add))
                assert done[0] == PHASE_STEPS
                then(dve.tensor_tensor(zr, lr, step, ALU.mult))
                exp(mag[:, :, 1], zr)
                then(dve.tensor_tensor(mag[:, :, 2], mag[:, :, 1], mag[:, :, 1], ALU.mult))
                for n in (2, 4):
                    then(dve.tensor_tensor(mag[:, :, n + 1:2 * n + 1], mag[:, :, 1:n + 1], spread(mag[:, :, n], n), ALU.mult))
                then(dve.memset(mag[:, :, 0:1], 1.0))
                assert done[0] == MAG_STEPS, done

            def s5_matrices():
                lr, li = s5p[:, 0:PAIRS], s5p[:, PAIRS:2 * PAIRS]

                def param(i):
                    c = 3 * PAIRS + i * PAIRS * GP
                    return s5p[:, c:c + PAIRS * GP].rearrange("p (q c) -> p q c", c=GP)

                br, bi, cr_, ci_ = (param(i) for i in range(4))
                den, am1, cr, ci, t1, t2, t3, t4 = (small[:, i] for i in range(7, 15))
                ar, ai = pow_r[:, :, 1], pow_i[:, :, 1]
                done = [0]

                def then(*steps):
                    for ins in steps:
                        ins.then_inc(s5_bmat, 1)
                        done[0] += 1
                    dve.wait_ge(s5_bmat, done[0])

                def spread(a):
                    return a.unsqueeze(2).broadcast_to([P, PAIRS, GP])

                then(dve.tensor_tensor(pow_r[:], mag[:], rot_c[:, :, 0:POWERS], ALU.mult),
                     dve.tensor_tensor(pow_i[:], mag[:], rot_s[:, :, 0:POWERS], ALU.mult),
                     dve.tensor_tensor(t1, lr, lr, ALU.mult), dve.tensor_tensor(t2, li, li, ALU.mult))
                then(dve.tensor_tensor(den, t1, t2, ALU.add), dve.tensor_scalar(am1, ar, -1.0, None, ALU.add))
                then(dve.reciprocal(den, den), dve.tensor_tensor(t1, am1, lr, ALU.mult),
                     dve.tensor_tensor(t2, ai, li, ALU.mult), dve.tensor_tensor(t3, ai, lr, ALU.mult),
                     dve.tensor_tensor(t4, am1, li, ALU.mult))
                then(dve.tensor_tensor(cr, t1, t2, ALU.add), dve.tensor_tensor(ci, t3, t4, ALU.subtract))
                then(dve.tensor_tensor(cr, cr, den, ALU.mult), dve.tensor_tensor(ci, ci, den, ALU.mult))
                then(dve.tensor_tensor(bb[:, 0], br, spread(cr), ALU.mult), dve.tensor_tensor(bb[:, 1], bi, spread(ci), ALU.mult),
                     dve.tensor_tensor(bb[:, 2], bi, spread(cr), ALU.mult), dve.tensor_tensor(bb[:, 3], br, spread(ci), ALU.mult))
                then(dve.tensor_tensor(bb[:, 0], bb[:, 0], bb[:, 1], ALU.subtract),
                     dve.tensor_tensor(bb[:, 2], bb[:, 2], bb[:, 3], ALU.add))
                then(dve.tensor_scalar(bb[:, 3], ci_, -1.0, None, ALU.mult))

                def product(power, re, im, conj):
                    a = [t[:, :, power:power + CH].unsqueeze(3).broadcast_to([P, PAIRS, CH, GP]) for t in (pow_r, pow_i)]
                    b = [t.unsqueeze(2).broadcast_to([P, PAIRS, CH, GP]) for t in (re, im)]
                    yield dve.tensor_tensor(b_mat[:, 0], b[0], a[0], ALU.mult), dve.tensor_tensor(t_mat[:, 0], b[1], a[1], ALU.mult)
                    yield (dve.tensor_tensor(b_mat[:, 0], b_mat[:, 0], t_mat[:, 0], ALU.add if conj else ALU.subtract),
                           dve.tensor_tensor(b_mat[:, 1], b[1], a[0], ALU.mult), dve.tensor_tensor(t_mat[:, 1], b[0], a[1], ALU.mult))
                    yield (dve.tensor_tensor(b_mat[:, 1], b_mat[:, 1], t_mat[:, 1], ALU.subtract if conj else ALU.add),)

                for steps in product(0, bb[:, 0], bb[:, 2], False):
                    then(*steps)
                assert done[0] == BMAT_STEPS
                return then, product, cr_, done

            def s5_output_matrices(then, product, c_re, done):
                dve.wait_ge(s5_prep_mm, 9)
                for steps in product(1, c_re, bb[:, 3], True):
                    then(*steps)
                assert done[0] == CMAT_STEPS

            def odd_mixer(stage):
                dve.memset(start_re[:], 0.0).then_inc(starts_clear, 1)
                dve.memset(start_im[:], 0.0).then_inc(starts_clear, 1)
                for m in range(HT):
                    dve.wait_ge(used, O_U - first + m + 1)
                    dve.tensor_tensor(u[:, m], bank[m][:].rearrange("p (c l) -> p l c", l=CH),
                                      rstd[:].rearrange("p (c l) -> p l c", l=CH), ALU.mult).then_inc(u_ready, 1)
                dve.wait_ge(used, O_GK - first + 1)
                dve.tensor_tensor(squares[0:16, 0, :], bank[4][0:16, :], rstd[0:16, :], ALU.mult).then_inc(gk_ready, 1)
                for i in range(2):
                    dve.wait_ge(gate_pre, i + 1)
                    dve.tensor_scalar(logs[:, i, :], bank[5 + i][:], column("gk_b", i), None, ALU.add).then_inc(gk_logs, 1)
                dve.wait_ge(gk_logs, 2)
                dve.wait_ge(gk_abs, 3)
                flat_logs = logs[:].rearrange("p i t -> p (i t)")
                dve.scalar_tensor_tensor(out=flat_logs, in0=flat_logs, scalar=0.0, in1=e_pos[:].rearrange("p i t -> p (i t)"),
                                         op0=ALU.min, op1=ALU.subtract).then_inc(gk_sum, 1)
                dve.wait_ge(gk_sum, 1)
                for i in range(2):
                    dve.tensor_tensor_scan(logs[:, i, :], table("chunk_keep"), logs[:, i, :], 0.0, ALU.mult, ALU.add).then_inc(gk_sum, 1)
                dve.wait_ge(gk_exp, 2)
                dve.tensor_copy(chunk_decay[:], e_pos[:].rearrange("p i (n c) -> p i n c", c=GC)[:, :, :, GC - 1]).then_inc(gk_step, 1)
                dve.wait_ge(gk_step, 1)
                for e in (e_pos, e_neg):
                    dve.tensor_tensor(e[:], e[:], rstd[:].unsqueeze(1).broadcast_to([P, 2, S]), ALU.mult).then_inc(gk_scaled, 1)
                dve.wait_ge(gk_scaled, 2)
                for i in range(2):
                    dve.wait_ge(used, O_Q - first + i + 1)
                    dve.scalar_tensor_tensor(out=e_pos[:, i, :], in0=bank[(7, 4)[i]][:], scalar=64 ** -0.5, in1=e_pos[:, i, :],
                                             op0=ALU.mult, op1=ALU.mult).then_inc(gk_dec, 1)
                for i in range(2):
                    dve.wait_ge(used, O_K - first + i + 1)
                    dve.tensor_tensor(e_neg[:, i, :], bank[5 + i][:], e_neg[:, i, :], ALU.mult).then_inc(gk_dec, 1)
                dve.wait_ge(gk_dec, 4)
                for i in range(2):
                    dve.tensor_tensor(logs[:, i, :].rearrange("p (n c) -> p n c", c=GC),
                                      e_neg[:, i, :].rearrange("p (n c) -> p n c", c=GC),
                                      chunk_decay[:, i, :].unsqueeze(2).broadcast_to([P, GN, GC]), ALU.mult).then_inc(gk_dec, 1)

                a, b_, c, d_, e_ = spare_pairs, square_pairs, st[:, 0], st[:, 1], st[:, 2]
                cos_, sin_ = rot[:, 0], rot[:, 1]
                done = [0]

                def then(*steps):
                    for ins in steps:
                        ins.then_inc(s5_step, 1)
                        done[0] += 1
                    dve.wait_ge(s5_step, done[0])

                def local(ri):
                    return [bank[2 * ri + i][:].rearrange("p (q c) -> p q c", c=CHUNKS) for i in range(2)]

                def times(out, ri, by):
                    return [dve.tensor_tensor(out[:, 8 * i:8 * i + 8], local(ri)[i], by[:, 8 * i:8 * i + 8], ALU.mult) for i in range(2)]

                dve.wait_ge(starts_clear, 2)
                dve.wait_ge(s5_local, 1)
                dve.wait_ge(s5_rot_in, 32)
                dve.tensor_copy(d_, m8[:].unsqueeze(2).broadcast_to([P, PAIRS, CHUNKS])).then_inc(s5_coef, 1)
                times_all = times(a, 0, cos_) + times(c, 1, cos_) + times(b_, 1, sin_) + times(e_, 0, sin_)
                last_reads = times_all
                for n, ins in enumerate(last_reads):
                    if n % 2:
                        ins.then_inc(s5_step, 1)
                    else:
                        ins.then_inc(s5_half, 1)
                done[0] = 4
                dve.wait_ge(s5_step, 4)
                dve.wait_ge(s5_half, 4)
                dve.wait_ge(s5_coef, 1)
                then(dve.tensor_tensor(a, a, b_, ALU.add), dve.tensor_tensor(c, c, e_, ALU.subtract),
                     dve.memset(d_[:, :, 0:1], 0.0))
                flat = [t.rearrange("p q c -> p (q c)") for t in (a, c, d_)]
                then(dve.tensor_tensor_scan(flat[0], flat[2], flat[0], 0.0, ALU.mult, ALU.add),
                     dve.tensor_tensor_scan(flat[1], flat[2], flat[1], 0.0, ALU.mult, ALU.add))
                def to_starts(start, op):
                    rows = [slice(ST * g, ST * (g + 1)) for g in range(2)]
                    return [dve.tensor_tensor(start[r, :, g, 1:CHUNKS], d_[r, :, 0:CHUNKS - 1], b_[r, :, 0:CHUNKS - 1], op)
                            for g, r in enumerate(rows)]

                then(dve.tensor_tensor(d_, a, cos_, ALU.mult), dve.tensor_tensor(b_, c, sin_, ALU.mult))
                then(*to_starts(start_re, ALU.subtract))
                then(dve.tensor_tensor(d_, a, sin_, ALU.mult), dve.tensor_tensor(b_, c, cos_, ALU.mult))
                then(*to_starts(start_im, ALU.add))
                assert done[0] == S5_STEPS

                dve.wait_ge(s5_y_ready, 4)
                dve.memset(state[:, 0], 0.0).then_inc(state_step, 1)
                for h in range(GH):
                    dve.wait_ge(att_ready, h + 1)
                    causal = table("chunk_causal").unsqueeze(1).broadcast_to([P, TT, P])
                    dve.tensor_tensor(attT[:, h, :].rearrange("p (t c) -> p t c", c=P),
                                      bank[(2, 3, 0, 1)[h]][:].rearrange("p (t c) -> p t c", c=P), causal, ALU.mult).then_inc(attT_ready, 1)
                for n in range(GN - 1):
                    dve.wait_ge(kv_ready, min(n // 4 * 4 + 4, GN - 1))
                    dve.wait_ge(state_step, 1 + 2 * n)
                    for i in range(2):
                        col = (n // 2 % 2) * 256 + i * DV
                        dve.scalar_tensor_tensor(out=state[:, n + 1, i], in0=state[:, n, i], scalar=chunk_decay[:, i, n:n + 1],
                                                 in1=bank[4 + 2 * (n % 2) + n // 4][:, col:col + DV],
                                                 op0=ALU.mult, op1=ALU.add).then_inc(state_step, 1)
                dve.wait_ge(y_loaded, 16)
                uf = u[:].rearrange("p m l c -> p m (l c)")
                y_in = u_in[:].rearrange("p g c -> p (g c)").rearrange("p (m n) -> p m n", m=HT)
                for m in range(HT):
                    ins = dve.scalar_tensor_tensor(out=y_in[:, m], in0=uf[:, m], scalar=column("s5_d", m), in1=y_in[:, m],
                                                   op0=ALU.mult, op1=ALU.add)
                ins.then_inc(ys_ready, 1)
                for t in range(TT):
                    dve.wait_ge(intra_ready, t + 1)
                    dve.wait_ge(inter_out, 2 * t + 2)
                    dve.tensor_tensor(o[:, t, :], bank[t][:], o[:, t, :], ALU.add).then_inc(o_ready, 1)
                dve.wait_ge(ys_split, 1)
                dve.tensor_tensor(ys_lo[:], y_in, ys_hi[:].bitcast(F32), ALU.subtract).then_inc(ys_split, 1)
                for t in range(TT):
                    dve.wait_ge(o_squared, t + 1)
                    dve.tensor_reduce(gla_var[:, t * GH:(t + 1) * GH], squares[:, t % 2, :].rearrange("p (h d) -> p h d", d=DV),
                                      AX_X, ALU.add).then_inc(o_sum, 1)
                dve.wait_ge(o_rms, 1)
                dve.reciprocal(gla_var[:], gla_var[:]).then_inc(o_inv, 1)
                dve.wait_ge(o_inv, 1)
                o16 = o[:].rearrange("p t (h d) -> p (t h) d", d=DV)
                dve.tensor_tensor(o16, o16, gla_var[:].unsqueeze(2).broadcast_to([P, TT * GH, DV]), ALU.mult).then_inc(o_step, 1)
                for t in range(TT):
                    dve.wait_ge(sg_ready, t + 1)
                    g4 = sg[:, t, :].rearrange("p (h d) -> p h d", d=DV)
                    gain = cols[:, COL["gla_norm"]:COL["gla_norm"] + DV].unsqueeze(1).broadcast_to([P, GH, DV])
                    dve.tensor_tensor(g4, g4, gain, ALU.mult).then_inc(sg_gain, 1)
                dve.wait_ge(o_step, 1)
                dve.wait_ge(sg_gain, TT)
                dve.tensor_tensor(o[:], o[:], sg[:], ALU.mult).then_inc(o_step, 1)
                sig = st[:, 0:2].rearrange("p a q c -> p (a q c)").rearrange("p (m n) -> p m n", m=HT)
                for part in range(2):
                    for m in (2 * part, 2 * part + 1):
                        dve.wait_ge(glu_sig, m + 1)
                        dve.tensor_tensor(y_in[:, m], y_in[:, m], sig[:, m], ALU.mult).then_inc(s5_gated, 1)
                    for m in (2 * part, 2 * part + 1):
                        dve.wait_ge(s5_hi, m + 1)
                        in_time = y_in[:, m].rearrange("p (l c) -> p c l", c=CHUNKS)
                        dve.tensor_tensor(y_s5_lo[:, m, :].rearrange("p (c l) -> p c l", l=CH), in_time,
                                          y_s5_hi[:, m, :].rearrange("p (c l) -> p c l", l=CH).bitcast(F32), ALU.subtract).then_inc(s5_out, 1)
                for h in range(GH):
                    dve.wait_ge(gla_hi, h + 1)
                    dve.tensor_tensor(y_gla_lo[:, h, :], bank[h][:], y_gla_hi[:, h, :].bitcast(F32), ALU.subtract).then_inc(gla_y, 1)

            def even_mixer(stage):
                def head_norms(which):
                    var = qk_var[:, which, :]
                    for t in range(TT):
                        n = TT * which + t
                        dve.wait_ge(qk_squared, n + 1)
                        dve.tensor_reduce(var[:, t * HEADS:(t + 1) * HEADS],
                                          squares[:, n % 2, :].rearrange("p (h d) -> p h d", d=HD),
                                          AX_X, ALU.add).then_inc(qk_sum, 1)
                    dve.wait_ge(qk_rms, which + 1)
                    dve.reciprocal(var, var).then_inc(qk_inv, 1)
                    dve.wait_ge(qk_inv, which + 1)
                    heads = var.rearrange("p (t h) -> p t h", h=HEADS)
                    dve.tensor_tensor(heads, heads, rstd_t[:].unsqueeze(2).broadcast_to([P, TT, HEADS]), ALU.mult).then_inc(q_inv_scaled, 1)
                    dve.wait_ge(q_inv_scaled, which + 1)
                    for t in range(TT):
                        inv = var[:, t * HEADS:(t + 1) * HEADS].unsqueeze(2).broadcast_to([P, HEADS, HD])
                        dve.tensor_tensor(qk[:, which, t, :].rearrange("p (h d) -> p h d", d=HD),
                                          bank[4 * which + t][:].rearrange("p (h d) -> p h d", d=HD), inv,
                                          ALU.mult).then_inc(qk_step, 1)

                lru_constants()
                head_norms(0)
                if 2 in order:
                    s5_rotations()
                    matrices = s5_matrices()
                head_norms(1)
                for which in range(2):
                    a = qk[:, which].rearrange("p t (h d) -> p (t h) d", d=HD)
                    gain = cols[:, COL[("q_norm", "k_norm")[which]]:][:, 0:HD].unsqueeze(1).broadcast_to([P, TT * HEADS, HD])
                    dve.wait_ge(qk_step, 4 * which + 4)
                    base = 2 * TT + 3 * which
                    dve.tensor_tensor(a, a, gain, ALU.mult).then_inc(qk_step, 1)
                    dve.wait_ge(qk_step, base + 1)
                    r = qk[:, which].rearrange("p t (h d) -> p t h d", d=HD)
                    x1, x2 = r[:, :, :, 0:ROPE], r[:, :, :, ROPE:2 * ROPE]
                    c, sn = (table(n).rearrange("p (t d) -> p t d", d=ROPE).unsqueeze(2).broadcast_to([P, TT, HEADS, ROPE])
                             for n in ("cos", "sin"))
                    for i, (xx, tt_) in enumerate(((x1, c), (x2, sn), (x2, c), (x1, sn))):
                        op = dve.tensor_tensor(rope_tmp[:, i], xx, tt_, ALU.mult)
                        op.then_inc(qk_rope, 1)
                    dve.wait_ge(qk_rope, 4 * (which + 1))
                    dve.tensor_tensor(x1, rope_tmp[:, 0], rope_tmp[:, 1], ALU.subtract).then_inc(qk_step, 1)
                    dve.tensor_tensor(x2, rope_tmp[:, 2], rope_tmp[:, 3], ALU.add).then_inc(qk_step, 1)
                    if which == 0:
                        dve.wait_ge(qk_step, 2 * TT + 3)

                for m in range(HT):
                    dve.wait_ge(used, E_X + m + 1)
                    dve.tensor_tensor(xl(m), bank[4 + m][:], rstd[:], ALU.mult).then_inc(xl_scaled, 1)
                for m in range(HT):
                    dve.wait_ge(x_newest, m + 1)
                    for i in range(3):
                        back = i + 1
                        dve.scalar_tensor_tensor(out=xc[:, m, back:S], in0=xl(m)[:, 0:S - back],
                                                 scalar=column("lru_w", (3 - back) * HT + m), in1=xc[:, m, back:S],
                                                 op0=ALU.mult, op1=ALU.add).then_inc(x_conv, 1)
                        dve.wait_ge(x_conv, 3 * m + i + 1)
                if 2 in order:
                    s5_output_matrices(*matrices)
                for m in range(HT):
                    dve.wait_ge(used, E_G + m + 1)
                    dve.tensor_tensor(xl(m), bank[m][:], rstd[:], ALU.mult).then_inc(gl_scaled, 1)
                def lru_piece(n):
                    if n == 0:
                        dve.wait_ge(lru_exp, 2 * HT)
                        dve.tensor_scalar(rg[:], coef[:], 1.0, None, ALU.add).then_inc(lru_step, 1)
                    if n == 1:
                        dve.wait_ge(lru_step, 1)
                        dve.reciprocal(rg[:], rg[:]).then_inc(lru_step, 1)
                    if n == 2:
                        dve.wait_ge(lru_step, 2)
                        dve.tensor_tensor(coef[:], coef[:], rg[:], ALU.mult).then_inc(lru_step, 1)
                    if n == LRU_STEP:
                        dve.wait_ge(gate_sig, 2 * HT)
                        dve.tensor_tensor(ig[:], ig[:], xc[:], ALU.mult).then_inc(lru_in, 1)
                    if n <= LRU_STEP:
                        return
                    m, piece = divmod(n - LRU_STEP - 1, 3)
                    step = 3 + 4 * m
                    if piece == 0:
                        dve.wait_ge(lru_in, 1)
                        dve.wait_ge(lru_sqrt, 1)
                        dve.tensor_tensor(ig[:, m, :], ig[:, m, :], coef[:, m, :], ALU.mult).then_inc(lru_step, 1)
                    if piece == 1:
                        dve.wait_ge(lru_step, step + 1)
                        dve.tensor_tensor_scan(coef[:, m, :], decay[:, m, :], ig[:, m, :], 0.0, ALU.mult, ALU.add).then_inc(lru_step, 1)
                    if piece == 2:
                        dve.wait_ge(lru_step, step + 2)
                        dve.wait_ge(gg_ready, HT)
                        dve.tensor_tensor(coef[:, m, :], coef[:, m, :], xl(m), ALU.mult).then_inc(lru_step, 1)
                        dve.wait_ge(lru_step, step + 3)
                        dve.tensor_copy(y_lru_hi[:, m, :], coef[:, m, :]).then_inc(lru_step, 1)
                        dve.wait_ge(lru_step, step + 4)
                        dve.tensor_tensor(y_lru_lo[:, m, :], coef[:, m, :], y_lru_hi[:, m, :].bitcast(F32), ALU.subtract).then_inc(lru_y, 1)

                def mask_scores(n):
                    t = n % TT
                    w = (t + 1) * P
                    dve.wait_ge(scores_ready, n + 1)
                    if n >= 2:
                        dve.wait_ge(probs_turned, n - 1)
                    for e in range(2):
                        dve.tensor_tensor_reduce(prob[:, n % 2, e, 0:w], bank[2 * e + n % 2][:, 0:w],
                                                 table("mask")[:, S - w:S], 1.0, NEVER, ALU.add, ALU.max,
                                                 row_max[:, n % 2, e:e + 1]).then_inc(masked, 1)
                    dve.wait_ge(masked, 2 * n + 2)
                    dve.tensor_scalar(neg_max[:, n % 2, :], row_max[:, n % 2, :], -HD ** -0.5, None,
                                      ALU.mult).then_inc(negmax_ready, 1)

                def normalise(n):
                    w = (n % TT + 1) * P
                    dve.wait_ge(exped, 2 * n + 2)
                    dve.reciprocal(row_inv[:, n % 2, :], row_sum[:, n % 2, :]).then_inc(rinv_ready, 1)
                    dve.wait_ge(rinv_ready, n + 1)
                    for e in range(2):
                        dve.tensor_scalar(prob[:, n % 2, e, 0:w], prob[:, n % 2, e, 0:w], row_inv[:, n % 2, e:e + 1],
                                          None, ALU.mult).then_inc(probs_ready, 1)

                def take_heads(hp):
                    dve.wait_ge(pv_done, TT * (hp + 1))
                    y_hi, y_lo = y_att_hi[:, hp, :], y_att_lo[:, hp, :]
                    dve.tensor_copy(y_hi, bank[6 + hp % 2][:]).then_inc(att_y, 1)
                    dve.wait_ge(att_y, 2 * hp + 1)
                    dve.tensor_tensor(y_lo, bank[6 + hp % 2][:], y_hi.bitcast(F32), ALU.subtract).then_inc(att_y, 1)

                mask_scores(0)
                mask_scores(1)
                for n in range(ATT_STEPS):
                    normalise(n)
                    lru_piece(n)
                    if n + 2 < ATT_STEPS:
                        mask_scores(n + 2)
                    if n % TT == 1 and n > TT:
                        take_heads(n // TT - 1)
                take_heads(HT - 1)

            if 2 in order:
                dve.memset(qT[:, 1:HT, :], 0.0).then_inc(w3_zero, 1)
            take_x()
            if 2 in order:
                s5_turns()
                if 0 not in order:
                    s5_rotations()
                    s5_output_matrices(*s5_matrices())
            for stage, part in enumerate(order):
                find_rstd(stage, 1 - part % 2)
                if part == 0:
                    even_mixer(stage)
                    add_residual(stage, E_O, 1)
                if part == 2:
                    odd_mixer(stage)
                    add_residual(stage, O_O - first, 1)
                if part in (1, 3):
                    mlp(stage, part // 2, first_unit[part] - first)
                    add_residual(stage, first_unit[part] - first + 2 * FT, 3)


PARTS = (0, 1, 2, 3)


def by_tiles(w):
    k, n = w.shape
    t = w.reshape(k // (8 * P), 8, P, n // P, P)
    return np.ascontiguousarray(t.transpose(3, 0, 2, 1, 4)).reshape(-1, P, UNIT)


def by_rows(w):
    return np.ascontiguousarray(w.reshape(4, 2, P, 512).transpose(0, 2, 1, 3)).reshape(-1, P, UNIT)


def on_partitions(v):
    return np.ascontiguousarray(v.reshape(-1, P).T)


def make_tables():
    back = np.arange(P)[:, None] + (S - P) - np.arange(S)[None, :]
    count = sum(((back >= 0) & (back % dil == 0) & (back <= BACK * dil)).astype(np.float32) for _, dil in PATTERNS)
    mask = np.where(count > 0, np.log(np.maximum(count, 1)) * HD ** 0.5, NEVER)
    inv = np.float32(500000.0) ** (-np.arange(0, 2 * ROPE, 2, dtype=np.float32) / np.float32(2 * ROPE))
    angle = np.arange(S, dtype=np.float32)[:, None] * inv[None, :]
    step, chunk = np.arange(P), np.arange(P) // GC
    parts = {
        "identity": np.eye(P), "mask": mask,
        "angles": np.broadcast_to(np.concatenate([np.arange(POWERS), CH * np.arange(CHUNKS)]), (P, ANGLES)),
        "chunk_keep": np.broadcast_to(np.arange(S) % GC != 0, (P, S)),
        "chunk_causal": (step[:, None] <= step[None, :]) & (chunk[:, None] == chunk[None, :]),
    }
    for name, f in (("cos", np.cos), ("sin", np.sin)):
        parts[name] = f(angle).reshape(TT, P, ROPE).transpose(1, 0, 2).reshape(P, -1)
    return np.ascontiguousarray(np.concatenate([parts[n] for n, _ in _TABLES], axis=1).astype(np.float32))


def block_diagonal(w):
    out = np.zeros((P, HT, P), w.dtype)
    for b in range(8):
        at = slice(64 * (b % 2), 64 * (b % 2) + 64)
        out[at, b // 2, at] = w[b]
    return out


def lay_out(x, e_norm, e_w_in, e_w_out, e_conv_w, e_conv_b, e_gate_a_w, e_gate_a_b, e_gate_x_w, e_gate_x_b,
            e_lambda, e_q_norm, e_k_norm, o_lambda_re, o_lambda_im, o_b_re, o_b_im, o_c_re, o_c_im, o_d, o_log_step,
            o_glu_b, o_gk_w, o_gk_b, o_gla_norm, o_norm, o_w_in, o_glu_w, o_w_out, f_norm, f_w_in, f_conv_w, f_conv_b, f_w_out):
    def cut(w, sizes):
        return np.split(w, np.cumsum(sizes)[:-1], axis=1)

    ex, eg, eq, ek, ev = cut(e_w_in[0], [512] * 5)
    ou, oq, ok, ov, og, ogk = cut(o_w_in[0], [512, 256, 256, 512, 512, 16])
    ogk = np.pad(ogk, ((0, 0), (0, P - 16)))

    def mlp(layer):
        up = by_tiles(f_w_in[layer]).reshape(2, FT, P, UNIT).transpose(1, 0, 2, 3).reshape(-1, P, UNIT)
        return [up, by_tiles(f_w_out[layer])]

    glu = o_glu_w[0].reshape(HT, P, HT, P).transpose(2, 0, 1, 3).reshape(2, 8, P, P).transpose(0, 2, 1, 3).reshape(2, P, UNIT)
    units = np.concatenate(
        [by_rows(eq), by_rows(ek), by_rows(ev), by_tiles(ex), by_tiles(eg), by_tiles(e_w_out[0])] + mlp(0)
        + [by_tiles(ou), by_tiles(ogk), by_tiles(oq), by_tiles(ok), by_rows(ov), by_rows(og), glu, by_tiles(o_w_out[0])]
        + mlp(1))
    assert units.shape == (N_UNITS, P, UNIT)
    columns = {
        "norm": np.concatenate([on_partitions(v) for v in (e_norm[0], f_norm[0], o_norm[0], f_norm[1])], axis=1),
        "mlp_w": on_partitions(f_conv_w), "mlp_b": on_partitions(f_conv_b),
        "lru_w": on_partitions(e_conv_w), "lru_b": on_partitions(e_conv_b), "gate_a_b": on_partitions(e_gate_a_b),
        "gate_x_b": on_partitions(e_gate_x_b), "lambda": on_partitions(e_lambda),
        "s5_d": on_partitions(o_d), "glu_b": on_partitions(o_glu_b), "gk_b": on_partitions(o_gk_b),
        "gla_norm": np.broadcast_to(o_gla_norm, (P, DV)),
        "q_norm": np.broadcast_to(e_q_norm, (P, HD)), "k_norm": np.broadcast_to(e_k_norm, (P, HD)),
    }
    columns = np.concatenate([columns[n] for n, _ in _COLUMNS], axis=1)
    assert columns.shape == (P, N_COLS)

    def states(a):
        return a.reshape(PAIRS, 2, ST, -1).transpose(1, 2, 0, 3).reshape(P, -1)

    s5 = np.concatenate([states(o_lambda_re[0]), states(o_lambda_im[0]),
                         states(np.broadcast_to(o_log_step[0][:, None], (2 * PAIRS, ST))),
                         states(o_b_re[0]), states(o_b_im[0]),
                         states(o_c_re[0].transpose(0, 2, 1)), states(o_c_im[0].transpose(0, 2, 1))], axis=1)
    return {"s5": np.ascontiguousarray(s5), "gk_w": np.ascontiguousarray(o_gk_w[0]),
            "xT": np.ascontiguousarray(x[0].T), "units": units, "columns": np.ascontiguousarray(columns),
            "tables": make_tables(), "gates_a": block_diagonal(e_gate_a_w[0]), "gates_x": block_diagonal(e_gate_x_w[0])}


def kernel(**inputs):
    import concourse.bacc as bacc
    from concourse.bass_utils import run_bass_kernel_spmd

    arrays = lay_out(**{n: np.asarray(a) for n, a in inputs.items()})
    nc = bacc.Bacc("TRN2", target_bir_lowering=False, num_devices=1)
    args = {n: nc.dram_tensor(n, a.shape, F32, kind="ExternalInput").ap() for n, a in arrays.items()}
    outT = nc.dram_tensor("outT", (D, S), F32, kind="ExternalOutput").ap()
    build(nc, PARTS, outT=outT, **args)
    r = run_bass_kernel_spmd(nc, [arrays], core_ids=[0])
    return np.ascontiguousarray(r.results[0]["outT"].T)[None]
```
